# Optimizing a Trainium2 kernel written in Bass

```python
import math
import jax, jax.numpy as jnp
from jax import lax
import numpy as np

D_MODEL = 1024
BATCH = 1
SEQ = 128
DEPTH = 2
DEC_BATCH = 1
DEC_SEQ = 256
PAST_LEN = 128

GRID_W = 64
HEAD_DIM = 64
NA_HEADS = 4
NA_WIDTH = NA_HEADS * HEAD_DIM
NA_WIN_ROWS = 8
NA_WIN_COLS = 16
NA_QBLK_COLS = 16
NA_KBLK_COLS = NA_QBLK_COLS + NA_WIN_COLS
SC_WIDTH = 256
DA_HEADS = 4
DA_DIM = 64
DA_QK_WIDTH = 2 * DA_HEADS * DA_DIM
DA_V_WIDTH = DA_HEADS * 2 * DA_DIM
MIX_WIDTH = NA_WIDTH + SC_WIDTH + DA_V_WIDTH
IN_WIDTH = 3 * NA_WIDTH + 3 * SC_WIDTH + 2 * DA_QK_WIDTH + DA_V_WIDTH
IN_SPLITS = (NA_WIDTH, 2 * NA_WIDTH, 3 * NA_WIDTH,
             3 * NA_WIDTH + SC_WIDTH, 3 * NA_WIDTH + 2 * SC_WIDTH, 3 * NA_WIDTH + 3 * SC_WIDTH,
             3 * NA_WIDTH + 3 * SC_WIDTH + DA_QK_WIDTH, 3 * NA_WIDTH + 3 * SC_WIDTH + 2 * DA_QK_WIDTH)
QBLK = 128
ROPE_BASE = 10000.0
N_EXPERTS = 16
N_EXPERT_GROUPS = 4
EXPERTS_PER_GROUP = N_EXPERTS // N_EXPERT_GROUPS
TOP_K = 2
D_EXPERT = 256
DEEPNORM_ALPHA = (2 * DEPTH) ** 0.25
DEEPNORM_BETA = (8 * DEPTH) ** -0.25
LN_EPS = 1e-5

kernel_name = "hybrid_na_conv_diffattn_moe_diffusion_step"

def _layer_norm(x):
    xf = x.astype(jnp.float32)
    mu = jnp.mean(xf, -1, keepdims=True)
    var = jnp.mean(jnp.square(xf - mu), -1, keepdims=True)
    return ((xf - mu) * lax.rsqrt(var + LN_EPS)).astype(x.dtype)

def _rms_norm(x, g):
    xf = x.astype(jnp.float32)
    return (xf * lax.rsqrt(jnp.mean(xf * xf, -1, keepdims=True) + LN_EPS)).astype(x.dtype) * g

def _post_norm(x, y, g, b):
    return _layer_norm(DEEPNORM_ALPHA * x + y) * g + b

def _modulation(cond, w_mod, b_mod):
    m = jnp.einsum('nd,de->ne', jax.nn.silu(cond), w_mod) + b_mod
    return tuple(t[:, None, :] for t in jnp.split(m, 6, axis=-1))

def _in_proj(h, w):
    B, L, _ = h.shape
    u = jnp.einsum('bld,de->ble', h, w)
    na_q, na_k, na_v, sc_b, sc_c, sc_x, da_q, da_k, da_v = jnp.split(u, IN_SPLITS, axis=-1)
    na = lambda t: t.reshape(B, L, NA_HEADS, HEAD_DIM)
    return (na(na_q), na(na_k), na(na_v), sc_b, sc_c, sc_x,
            da_q.reshape(B, L, 2 * DA_HEADS, DA_DIM), da_k.reshape(B, L, 2 * DA_HEADS, DA_DIM),
            da_v.reshape(B, L, DA_HEADS, 2 * DA_DIM))

def _rope_1d(x, pos):
    half = x.shape[-1] // 2
    inv_freq = ROPE_BASE ** (-np.arange(half, dtype=np.float32) / half)
    ang = pos.astype(np.float32)[:, None] * inv_freq[None, :]
    cos = jnp.asarray(np.cos(ang))[:, None, :].astype(x.dtype)
    sin = jnp.asarray(np.sin(ang))[:, None, :].astype(x.dtype)
    x1, x2 = x[..., :half], x[..., half:]
    return jnp.concatenate([x1 * cos - x2 * sin, x2 * cos + x1 * sin], axis=-1)

def _axial_rope(x):
    S = x.shape[1]
    t = np.arange(S)
    half = x.shape[-1] // 2
    return jnp.concatenate([_rope_1d(x[..., :half], t // GRID_W),
                            _rope_1d(x[..., half:], t % GRID_W)], axis=-1)

def _query_blocks(q):
    B, L = q.shape[:2]
    return jnp.moveaxis(q.reshape(B, L // QBLK, QBLK, *q.shape[2:]), 1, 0)

def _merge_blocks(o):
    nb, B, qb = o.shape[:3]
    return jnp.moveaxis(o, 0, 1).reshape(B, nb * qb, *o.shape[3:])

def _softmax_attn(q, k, v):
    scale = q.shape[-1] ** -0.5
    def one(qb):
        s = jnp.einsum('bqhd,bkhd->bhqk', qb, k).astype(jnp.float32) * scale
        p = jax.nn.softmax(s, axis=-1).astype(v.dtype)
        return jnp.einsum('bhqk,bkhd->bqhd', p, v)
    o = _merge_blocks(lax.map(one, _query_blocks(q)))
    return o.reshape(o.shape[0], o.shape[1], -1)

def _neighbourhood_attn(q, k, v, ctx_k, ctx_v, rel_bias):
    B, S, H, dh = q.shape
    rows = S // GRID_W
    wr = min(NA_WIN_ROWS, rows)
    ncb = GRID_W // NA_QBLK_COLS
    qr = np.arange(rows)
    key_rows = np.clip(qr - wr // 2, 0, rows - wr)[:, None] + np.arange(wr)
    band = np.clip(np.arange(ncb) * NA_QBLK_COLS - NA_WIN_COLS // 2, 0, GRID_W - NA_KBLK_COLS)
    key_cols = band[:, None] + np.arange(NA_KBLK_COLS)
    qc = np.arange(GRID_W).reshape(ncb, NA_QBLK_COLS)
    win0 = np.clip(qc - NA_WIN_COLS // 2, 0, GRID_W - NA_WIN_COLS)
    in_win = (key_cols[:, None, :] >= win0[:, :, None]) & (key_cols[:, None, :] < win0[:, :, None] + NA_WIN_COLS)
    d_row = key_rows - qr[:, None] + NA_WIN_ROWS - 1
    d_col = np.clip(key_cols[:, None, :] - qc[:, :, None], 1 - NA_WIN_COLS, NA_WIN_COLS - 1) + NA_WIN_COLS - 1
    n_loc = wr * NA_KBLK_COLS
    bias = rel_bias.astype(jnp.float32)[:, d_row[:, None, None, :, None], d_col[None, :, :, None, :]]
    bias = jnp.where(in_win[None, None, :, :, None, :], bias, -jnp.inf)
    bias = bias.reshape(H, rows, ncb, NA_QBLK_COLS, n_loc)
    qg = q.reshape(B, rows, ncb, NA_QBLK_COLS, H, dh)
    ridx = key_rows[:, None, :, None]
    cidx = key_cols[None, :, None, :]
    kg = k.reshape(B, rows, GRID_W, H, dh)[:, ridx, cidx].reshape(B, rows, ncb, n_loc, H, dh)
    vg = v.reshape(B, rows, GRID_W, H, dh)[:, ridx, cidx].reshape(B, rows, ncb, n_loc, H, dh)
    scale = dh ** -0.5
    s_loc = jnp.einsum('brcqhd,brckhd->bhrcqk', qg, kg).astype(jnp.float32) * scale + bias
    s_ctx = jnp.einsum('brcqhd,bkhd->bhrcqk', qg, ctx_k).astype(jnp.float32) * scale
    p = jax.nn.softmax(jnp.concatenate([s_loc, s_ctx], axis=-1), axis=-1).astype(v.dtype)
    o = (jnp.einsum('bhrcqk,brckhd->brcqhd', p[..., :n_loc], vg)
         + jnp.einsum('bhrcqk,bkhd->brcqhd', p[..., n_loc:], ctx_v))
    return o.reshape(B, S, H * dh)

def _diff_attn(q, k, v, lam, lam_init, gain):
    B = q.shape[0]
    scale = DA_DIM ** -0.5
    def one(qb):
        s = jnp.einsum('bqhd,bkhd->bhqk', qb, k).astype(jnp.float32) * scale
        p = jax.nn.softmax(s, axis=-1).reshape(B, DA_HEADS, 2, QBLK, -1)
        a = (p[:, :, 0] - lam * p[:, :, 1]).astype(v.dtype)
        return jnp.einsum('bhqk,bkhd->bqhd', a, v)
    o = _merge_blocks(lax.map(one, _query_blocks(q)))
    o = _rms_norm(o, gain) * (1.0 - lam_init)
    return o.reshape(o.shape[0], o.shape[1], DA_V_WIDTH)

def _short_conv(u, w, b):
    up = jnp.pad(u, ((0, 0), (1, 1), (0, 0)))
    return up[:, :-2] * w[0] + up[:, 1:-1] * w[1] + up[:, 2:] * w[2] + b

def _moe(h, w_router, b_router, w1, w3, w2):
    B, L, _ = h.shape
    scores = jax.nn.sigmoid(jnp.einsum('bld,de->ble', h, w_router).astype(jnp.float32))
    grouped = (scores + b_router.astype(jnp.float32)).reshape(B, L, N_EXPERT_GROUPS, EXPERTS_PER_GROUP)
    group_score = jnp.sum(lax.top_k(grouped, TOP_K)[0], axis=-1)
    sel_group = jnp.argmax(group_score, axis=-1)
    in_group = (jnp.arange(N_EXPERT_GROUPS) == sel_group[..., None])[..., None]
    masked = jnp.where(in_group, grouped, -jnp.inf).reshape(B, L, N_EXPERTS)
    _, top_e = lax.top_k(masked, TOP_K)
    top_w = jnp.take_along_axis(scores, top_e, axis=-1)
    top_w = top_w / jnp.sum(top_w, -1, keepdims=True)
    gates = jnp.sum(jax.nn.one_hot(top_e, N_EXPERTS, dtype=jnp.float32) * top_w[..., None], axis=-2).astype(h.dtype)
    a = jnp.einsum('bld,edf->blef', h, w1)
    g = jnp.einsum('bld,edf->blef', h, w3)
    hid = jax.nn.silu(a) * g * gates[..., None]
    return jnp.einsum('blef,efd->bld', hid, w2)

def _layer(x, cond, attn_fn, w_mod, b_mod, w_in, sc_conv_w, sc_conv_b, w_out, ln1_g, ln1_b,
           w_router, b_router, w1, w3, w2, ln2_g, ln2_b):
    shift1, scale1, gate1, shift2, scale2, gate2 = _modulation(cond, w_mod, b_mod)
    h = _layer_norm(x) * (1 + scale1) + shift1
    na_q, na_k, na_v, sc_b, sc_c, sc_x, da_q, da_k, da_v = _in_proj(h, w_in)
    o_na, o_da, ctx_state = attn_fn(na_q, na_k, na_v, da_q, da_k, da_v)
    o_sc = sc_b * _short_conv(sc_c * sc_x, sc_conv_w, sc_conv_b)
    y = jnp.einsum('blm,md->bld', jnp.concatenate([o_na, o_sc, o_da], axis=-1), w_out)
    x = _post_norm(x, gate1 * y, ln1_g, ln1_b)
    h = _layer_norm(x) * (1 + scale2) + shift2
    x = _post_norm(x, gate2 * _moe(h, w_router, b_router, w1, w3, w2), ln2_g, ln2_b)
    return x, ctx_state

def setup_inputs(seed: int = 0) -> dict:
    key = jax.random.key(seed)
    def nrm(i, shape, std):
        return jax.random.normal(jax.random.fold_in(key, i), shape, jnp.float32) * std
    D = D_MODEL
    return {
        "x_prompt": nrm(0, (BATCH, SEQ, D), 1.0),
        "x_sample": nrm(1, (DEC_BATCH, DEC_SEQ, D), 1.0),
        "cache_na_k": nrm(2, (DEC_BATCH, DEPTH, PAST_LEN, NA_HEADS, HEAD_DIM), 1.0),
        "cache_na_v": nrm(3, (DEC_BATCH, DEPTH, PAST_LEN, NA_HEADS, HEAD_DIM), 1.0),
        "cache_da_k": nrm(4, (DEC_BATCH, DEPTH, PAST_LEN, 2 * DA_HEADS, DA_DIM), 1.0),
        "cache_da_v": nrm(5, (DEC_BATCH, DEPTH, PAST_LEN, DA_HEADS, 2 * DA_DIM), 1.0),
        "c": nrm(6, (DEC_BATCH, D), 1.0),
        "c_ctx": nrm(7, (D,), 1.0),
        "w_mod": nrm(8, (DEPTH, D, 6 * D), 0.5 * D ** -0.5),
        "b_mod": nrm(9, (DEPTH, 6 * D), 0.02),
        "w_in": nrm(10, (DEPTH, D, IN_WIDTH), D ** -0.5),
        "na_rel_bias": nrm(11, (DEPTH, NA_HEADS, 2 * NA_WIN_ROWS - 1, 2 * NA_WIN_COLS - 1), 0.1),
        "sc_conv_w": nrm(12, (DEPTH, 3, SC_WIDTH), 3 ** -0.5),
        "sc_conv_b": nrm(13, (DEPTH, SC_WIDTH), 0.02),
        "da_lambda": nrm(14, (DEPTH, 4, DA_DIM), 0.1),
        "da_norm_g": 1.0 + nrm(15, (DEPTH, 2 * DA_DIM), 0.02),
        "w_out": nrm(16, (DEPTH, MIX_WIDTH, D), DEEPNORM_BETA * MIX_WIDTH ** -0.5),
        "ln1_g": 1.0 + nrm(17, (DEPTH, D), 0.02),
        "ln1_b": nrm(18, (DEPTH, D), 0.02),
        "w_router": nrm(19, (D, N_EXPERTS), D ** -0.5),
        "b_router": nrm(20, (N_EXPERTS,), 0.01),
        "moe_w1": nrm(21, (DEPTH, N_EXPERTS, D, D_EXPERT), D ** -0.5),
        "moe_w3": nrm(22, (DEPTH, N_EXPERTS, D, D_EXPERT), D ** -0.5),
        "moe_w2": nrm(23, (DEPTH, N_EXPERTS, D_EXPERT, D), DEEPNORM_BETA * D_EXPERT ** -0.5),
        "ln2_g": 1.0 + nrm(24, (DEPTH, D), 0.02),
        "ln2_b": nrm(25, (DEPTH, D), 0.02),
    }

def reference(x_prompt, x_sample, cache_na_k, cache_na_v, cache_da_k, cache_da_v, c, c_ctx,
              w_mod, b_mod, w_in, na_rel_bias, sc_conv_w, sc_conv_b, da_lambda, da_norm_g, w_out,
              ln1_g, ln1_b, w_router, b_router, moe_w1, moe_w3, moe_w2, ln2_g, ln2_b):
    xp, xs = x_prompt, x_sample
    na_k_list, na_v_list, da_k_list, da_v_list = [], [], [], []
    for l in range(DEPTH):
        lam_init = 0.8 - 0.6 * math.exp(-0.3 * l)
        lp = da_lambda[l].astype(jnp.float32)
        lam = jnp.exp(jnp.sum(lp[0] * lp[1])) - jnp.exp(jnp.sum(lp[2] * lp[3])) + lam_init
        params = (w_mod[l], b_mod[l], w_in[l], sc_conv_w[l], sc_conv_b[l], w_out[l], ln1_g[l], ln1_b[l],
                  w_router, b_router, moe_w1[l], moe_w3[l], moe_w2[l], ln2_g[l], ln2_b[l])

        def ctx_attn(na_q, na_k, na_v, da_q, da_k, da_v):
            o_na = _softmax_attn(na_q, na_k, na_v)
            o_da = _diff_attn(da_q, da_k, da_v, lam, lam_init, da_norm_g[l])
            return o_na, o_da, (na_k, na_v, da_k, da_v)

        def lat_attn(na_q, na_k, na_v, da_q, da_k, da_v):
            o_na = _neighbourhood_attn(na_q, na_k, na_v, cache_na_k[:, l], cache_na_v[:, l], na_rel_bias[l])
            k_all = jnp.concatenate([_axial_rope(da_k), cache_da_k[:, l]], axis=1)
            v_all = jnp.concatenate([da_v, cache_da_v[:, l]], axis=1)
            o_da = _diff_attn(_axial_rope(da_q), k_all, v_all, lam, lam_init, da_norm_g[l])
            return o_na, o_da, None

        xp, (nk, nv, dk, dv) = _layer(xp, c_ctx[None, :], ctx_attn, *params)
        xs, _ = _layer(xs, c, lat_attn, *params)
        na_k_list.append(nk)
        na_v_list.append(nv)
        da_k_list.append(dk)
        da_v_list.append(dv)
    new_na_k = jnp.stack(na_k_list, axis=1)
    new_na_v = jnp.stack(na_v_list, axis=1)
    new_da_k = jnp.stack(da_k_list, axis=1)
    new_da_v = jnp.stack(da_v_list, axis=1)
    return (xp, xs, new_na_k, new_na_v, new_da_k, new_da_v)


_drawn_inputs = setup_inputs


def setup_inputs(seed=0):
    import zlib

    import numpy as np

    out = dict(_drawn_inputs(seed))
    spreads = {}
    factors = {'cache_na_k': 7.546,
     'cache_na_v': 6.631,
     'na_rel_bias': 64.0,
     'sc_conv_b': 30.94,
     'da_lambda': 4.216,
     'da_norm_g': 28.77,
     'b_router': 2.704}
    for name, (base, spread) in spreads.items():
        noise = np.random.default_rng([zlib.crc32(name.encode()), seed]).standard_normal(out[name].shape)
        drawn = base * np.exp(spread * noise) if base else spread * noise
        out[name] = __import__('jax').numpy.asarray(drawn.astype(out[name].dtype))
    for name, factor in factors.items():
        out[name] = (out[name] * factor).astype(out[name].dtype)
    return out
```

```python
from contextlib import ExitStack

import numpy as np

import concourse.bass as bass
from concourse import mybir

ALU = mybir.AluOpType
ACT = mybir.ActivationFunctionType
AX = mybir.AxisListType
F32 = mybir.dt.float32
BF16 = mybir.dt.bfloat16
U32 = mybir.dt.uint32

P = 128
D = 1024
KC = D // P
DEPTH = 2
TILES = 3
T = TILES * P
LAT = 2 * P
GRID_W = 64
DA_HEADS = 4
NA_HEADS = 4
DH = 64
E = 16
GROUPS = 4
DE = 256
HALF = 64
PAIRS = E // 2
BLOCKS = (2 * T // HALF + E - 1 + T // HALF) // 2
EXPERT = 6144
BUFS = 4
SCALE = DH ** -0.5
ALPHA = (2 * DEPTH) ** 0.25
EPS = 1e-5
MASKED = -1.0e30

RING = 8
ITEM = 2048
N_MOD = 6
MODS = [4 * v for v in range(2)] + [20 + 4 * v for v in range(4)]
W_IN0 = 8
W_OUT0 = 36
ITEMS = 40

T_FIRST, T_LAST, T_ACTIVE, T_COUNT, T_START, T_BLOCKS, T_WHO = 0, 1, 2, 3, 4, 12, 20

KCH = {"dak": 0, "nak": 4}
QCH = {"daq": 0, "naq": 4, "scc": 6, "scx": 8, "scb": 10}
PIECES = [("dak", 0), ("dak", 1), ("daq", 0), ("daq", 1), ("nak", 0), ("naq", 0),
          ("dav", 0), ("dav", 1), ("nav", 0), ("scc", 0), ("scx", 0), ("scb", 0)]
PIECE_COL = {"naq": 0, "nak": 256, "nav": 512, "scb": 768, "scc": 1024, "scx": 1280,
             "daq": 1536, "dak": 2048, "dav": 2560}
V_COL = {"dav": 0, "nav": 512}

(C_ID, C_SWAP, C_COS, C_SIN, C_MASK, C_UTRI, C_IOTA, C_LT4, C_NUM, C_TOK, C_LT16, C_PREV, C_ROWS, C_HALF) = (
    0, 128, 256, 512, 768, 1476, 1604, 832, 848, 880, 888, 1144, 1400, 1416)
N_KEPT = 1476
N_CONST = 1732
SLOT_BANK = {"A": 0, "B": 2, "C": 4, "D": 6, "E": 7}

STEPS = [("da", h, t) for h in range(DA_HEADS) for t in range(TILES)] + \
        [("na", h, t) for h in range(NA_HEADS) for t in range(TILES)]
N_STEPS = len(STEPS)
MIX_DELAY = 4


def psum_plan():
    jobs = [("cacheT", "A"), (("mod", 0), "D"), (("mod", 1), "E")]
    jobs += [(("hT", t), "BCA"[t]) for t in range(TILES)]
    proj = 0
    for piece, half in PIECES:
        for j in range(TILES if piece in V_COL else 2):
            jobs.append((("proj", proj), "BCA"[proj % 3]))
            proj += 1
            if piece in ("dak", "daq"):
                if proj >= 2:
                    jobs.append((("rope", proj - 2), "DE"[proj % 2]))
            elif proj == 9:
                jobs.append((("rope", 7), "DE"[1]))
    jobs.append(("kout", "B"))
    jobs += [(("score", 0), "A"), (("score", 1), "B")]
    mixes = 0
    for i, (kind, h, t) in enumerate(STEPS):
        if i + 2 < N_STEPS:
            jobs.append((("score", i + 2), "ABC"[(i + 2) % 3]))
        if kind == "da" and t == 2:
            jobs.append((("mod", 2 + h), "D"))
        jobs.append((("probT", i), "D"))
        if t == 0:
            jobs.append((("out", kind, h), "E"))
        if mixes < DA_HEADS and i == 3 * mixes + 2 + MIX_DELAY:
            jobs.append((("mixT", mixes), "D"))
            mixes += 1
    jobs += [(("y", 0), "A"), (("y", 1), "B"), (("h2T", 0), "C"), (("logit", 0), "D"),
             (("y", 2), "A"), (("h2T", 1), "B"), (("logit", 1), "E"),
             (("h2T", 2), "C"), (("logit", 2), "D"), ("place", "E")]
    jobs.append(("index", "D"))
    turn, plan = {s: 0 for s in SLOT_BANK}, {}
    for name, slot in jobs:
        assert name not in plan, name
        plan[name] = (slot, turn[slot])
        turn[slot] += 1
    return plan, turn


def hybrid_step_kernel(nc, walls, experts_in, x_in, cond_in, cache_in, bias_in, conv_in, lam_in, lamc_in, gain_in,
                       ln_in, router_in, brouter_in, bmod_in, const_in,
                       y_prompt, y_sample, new_na_k, new_na_v, new_da_k, new_da_v):
    plan, turns = psum_plan()
    mod_d = nc.dram_tensor("mod_rows", [2, N_MOD, D], F32, kind="Internal").ap()
    h2_d = nc.dram_tensor("h2_rows", [T, D], F32, kind="Internal").ap()
    moe_d = nc.dram_tensor("moe_rows", [BLOCKS * P, D], F32, kind="Internal").ap()

    with ExitStack() as ctx:
        def sb(name, shape, dt=F32):
            return ctx.enter_context(nc.sbuf_tensor(name, shape, dt))

        def sem(name):
            return ctx.enter_context(nc.semaphore(name))

        big = sb("big", [P, RING * ITEM + 2 * TILES * D + 4608])
        ring = big[:, 0:RING * ITEM].rearrange("p (s n) -> p s n", s=RING)
        expert_w = big[:, 0:BUFS * EXPERT]
        tail = big[:, RING * ITEM:]
        x = sb("x", [P, TILES, D])
        act_a = tail[:, 0:TILES * D].rearrange("p (t d) -> p t d", t=TILES)
        act_b = tail[:, TILES * D:2 * TILES * D]
        attn = tail[:, 2 * TILES * D:]
        shared = sb("shared", [P, 7680])
        v_sb = sb("v_sb", [P, TILES, 768])
        cache = sb("cache", [P, 1536])
        bias = attn[:, 0:1536].rearrange("p (h s c) -> p h s c", h=NA_HEADS, s=6)
        probs = attn[:, 1536:3840].rearrange("p (b m k) -> p b m k", b=3, m=2)
        probT = attn[:, 3840:4608].rearrange("p (b k t) -> p b k t", b=2, k=3)
        mod2_b = attn[:, 0:4096].rearrange("p (c v d) -> p c v d", c=2, v=2)
        gate_b = sb("gate_b", [P, 2, D])
        ln_b = sb("ln_b", [P, 2, D])
        wide = sb("wide", [P, 1280])
        mrow = sb("mrow", [P, N_MOD, 256])
        modT = sb("modT", [P, 2, 2, KC])
        const = sb("const", [P, N_KEPT])
        constb = sb("constb", [P, 4 * P + 8], BF16)
        convp = sb("convp", [P, 2, 4])
        lamv = sb("lamv", [P, 4, 64])
        lamc = sb("lamc", [P, 2])
        lams = sb("lams", [P, 8])
        gain = sb("gain", [P, P])
        routw = sb("routw", [P, KC, E])
        broute = sb("broute", [P, E])
        condv = sb("condv", [P, 2, KC])
        conds = sb("conds", [P, 2, 2, KC])
        condT = sb("condT", [P, KC, 32])
        kout = cache[:, 0:768]
        osb = sb("osb", [P, TILES, P])
        sq = wide[:, 768:1152].rearrange("p (t d) -> p t d", t=TILES)
        on = sb("on", [P, TILES, P])
        st = sb("st", [P, 24])
        mxs = sb("mxs", [P, 3, 2])
        rsum = sb("rsum", [P, 3, 2])
        rinv = sb("rinv", [P, 3, 4])
        msr = sb("msr", [P, 4, TILES])
        stats = sb("stats", [P, 3, 2, 6])
        mv = sb("mv", [P, 3, 2])
        lnv = sb("lnv", [P, 3, 4])
        half = sb("half", [P, 4])
        rt = sb("rt", [P, 16, TILES * E])
        pair = wide[:, 0:1024].rearrange("p (b n) -> p b n", b=2)
        sel = v_sb[:, :, :].rearrange("p a b -> p (a b)").bitcast(BF16)[:, 0:2 * TILES * P]\
            .rearrange("p (c s) -> p c s", c=2 * TILES)
        where = sb("where", [P, 2 * TILES, 2, BLOCKS], BF16)
        maskb = sb("maskb", [P, TILES * E], BF16)
        gidx = sb("gidx", [P, BLOCKS], U32)
        gcol = sb("gcol", [P, 1], U32)
        ridx = sb("ridx", [P, 2, TILES], U32)
        tab = sb("tab", [P, 36])
        tabu = sb("tabu", [P, 36], U32)
        gates = sb("gates", [P, 2, TILES])
        psum = ctx.enter_context(nc.psum_tensor("psum", [P, 8, 512], F32))

        ident = const[:, C_ID:C_ID + P]
        swap = const[:, C_SWAP:C_SWAP + P]
        cos_t = const[:, C_COS:C_COS + LAT]
        sin_t = const[:, C_SIN:C_SIN + LAT]
        utri, ones, iota, tok = (constb[:, 0:P], constb[:, P:2 * P], constb[:, 2 * P:3 * P],
                                 constb[:, 3 * P:3 * P + 6])
        xn = act_a
        h2 = shared[:, 0:3072].rearrange("p (t d) -> p t d", t=TILES)
        mix = tail[:, 0:TILES * D].rearrange("p (c t) -> p c t", c=8)
        hT = act_b.rearrange("p (k t) -> p k t", k=KC)
        kT = shared[:, 0:3072].rearrange("p (c t) -> p c t", c=6)
        qT = shared[:, 3072:7680].rearrange("p (c t) -> p c t", c=12)
        xg = shared[:, 0:1024]
        xT = shared[:, 1024:2048]
        yo = shared[:, 2048:3072]
        hid = shared[:, 3072:3328]
        hidT = shared[:, 3328:3584]
        silu = shared[:, 3584:3840]
        fetched = [shared[:, 1024 * i:1024 * i + 1024] for i in range(6)]

        arrived = [sem(f"arrived{s}") for s in range(RING)]
        ring_free = sem("ring_free")
        full = {s: sem(f"full_{s}") for s in SLOT_BANK}
        free = {s: sem(f"free_{s}") for s in SLOT_BANK}
        dve_done, act_done, pool_done = sem("dve_done"), sem("act_done"), sem("pool_done")
        const_in_s, x_in_s, layer_in_s = sem("const_in"), sem("x_in"), sem("layer_in")
        bmod_in_s = sem("bmod_in")
        ln_in_s = sem("ln_in")
        cond_exp, cond_ready = sem("cond_exp"), sem("cond_ready")
        constb_ready = sem("constb_ready")
        lam_dot, lam_exp = sem("lam_dot"), sem("lam_exp")
        stats_ready, rstd_ready, xn_ready = sem("stats_ready"), sem("rstd_ready"), sem("xn_ready")
        gained = sem("gained")
        mrow_ready, mod_stored = sem("mrow_ready"), sem("mod_stored")
        mod_loaded = sem("mod_loaded")
        gate1_in, mod2_in, gate2_in = sem("gate1_in"), sem("mod2_in"), sem("gate2_in")
        roped = sem("roped")
        kout_ready, state_out = sem("kout_ready"), sem("state_out")
        bias_ready = sem("bias_ready")
        max_ready, prob_ready, av_done = sem("max_ready"), sem("prob_ready"), sem("av_done")
        ms_ready, rms_ready, on_ready, mix_sc = sem("ms_ready"), sem("rms_ready"), sem("on_ready"), sem("mix_sc")
        h2_ready, h2_stored = sem("h2_ready"), sem("h2_stored")
        mask_ready, sel_ready, sidx_ready = sem("mask_ready"), sem("sel_ready"), sem("sidx_ready")
        table_ready = sem("table_ready")
        pair_done = sem("pair_done")
        expert_in = [sem(f"expert_in{q}") for q in range(BUFS)]
        xg_in, gcol_ready = sem("xg_in"), sem("gcol_ready")
        xT_full, xT_ready, up_full, up_exp, hid_ready, hidT_full, hidT_ready, down_full, yo_ready, yo_stored = (
            sem(n) for n in ("xT_full", "xT_ready", "up_full", "up_exp", "hid_ready", "hidT_full", "hidT_ready",
                             "down_full", "yo_ready", "yo_stored"))
        filled = sem("filled")
        silu_step = sem("silu_step")
        pick_in = [sem(f"pick_in{i}") for i in range(6)]
        x_out = sem("x_out")

        def bank(name, n=1):
            b = SLOT_BANK[plan[name][0]]
            return psum[:, b:b + n, :] if n > 1 else psum[:, b, :]

        def claim(eng, L, name):
            slot, turn = plan[name]
            eng.wait_ge(free[slot], L * turns[slot] + turn + 1)

        def produced(ins, name):
            ins.then_inc(full[plan[name][0]], 1)

        def await_product(eng, L, name):
            slot, turn = plan[name]
            eng.wait_ge(full[slot], L * turns[slot] + turn + 1)

        def read_out(ins, name):
            ins.then_inc(free[plan[name][0]], 1)

        def await_read(eng, L, name):
            slot, turn = plan[name]
            eng.wait_ge(free[slot], L * turns[slot] + turn + 2)

        def chain(eng, done):
            at = [0]

            def restart():
                at[0] = 0
                eng.sem_clear(done)

            def link(ins):
                at[0] += 1
                ins.then_inc(done, 1)
                eng.wait_ge(done, at[0])
            return restart, link

        psA, psB, psC, psD = (psum[:, 0:2, :].rearrange("p a b -> p (a b)"), psum[:, 2, :],
                              psum[:, 4:6, :].rearrange("p a b -> p (a b)"), psum[:, 6, :])

        passed = {e: sem(f"passed_{e}") for e in ("sp", "pe", "act", "pool")}

        def stop_here(eng, name):
            eng.sem_inc(passed[name], 1)

        block = ctx.enter_context(nc.Block())

        @block.sync
        def _(sp):
            with sp.Fori(0, DEPTH) as L:
                sp.wait_ge(pair_done, L * PAIRS + 1)
                for s in range(RING):
                    sp.dma_start(ring[:, s, :], walls[L * ITEMS + s]).then_inc(arrived[s], 16)
                with sp.Fori(1, ITEMS // RING) as turn:
                    for s in range(RING):
                        sp.wait_ge(ring_free, L * ITEMS + turn * RING + (s - RING + 1))
                        sp.dma_start(ring[:, s, :], walls[L * ITEMS + turn * RING + s]).then_inc(arrived[s], 16)
                sp.wait_ge(table_ready, L + 1)
                stop_here(sp, "sp")
                active = sp.value_load(tabu[0:1, T_ACTIVE:T_ACTIVE + 1], min_val=1, max_val=E)
                for r in range(E):
                    q = r % BUFS
                    if r >= BUFS:
                        sp.wait_ge(pair_done, L * PAIRS + ((r - BUFS) // 2 + 2))
                        stop_here(sp, "sp")
                    with sp.If(active > r - r % 2):
                        who = sp.value_load(tabu[0:1, T_WHO + r:T_WHO + r + 1], min_val=0, max_val=E - 1)
                        sp.dma_start(expert_w[:, q * EXPERT:(q + 1) * EXPERT], experts_in[L * E + who])\
                            .then_inc(expert_in[q], 16)
                    with sp.Else():
                        sp.sem_inc(expert_in[q], 16)

        @block.tensor
        def _(pe):
            def item(L, j):
                pe.wait_ge(arrived[j % RING], (L * (ITEMS // RING) + (j // RING + 1)) * 16)
                return ring[:, j % RING, :]

            def transposes(name, n, src):
                out = bank(name, 2).rearrange("p a b -> p (a b)") if n > 4 else bank(name)
                for k in range(n):
                    ins = pe.transpose(out[:, k * P:(k + 1) * P], src(k), ident)
                produced(ins, name)

            def mod_vector(L, v):
                w = [item(L, MODS[v] + g).rearrange("p (k n) -> p k n", k=KC) for g in range(4)]
                claim(pe, L, ("mod", v))
                for k in range(KC):
                    for g in range(4):
                        ins = pe.matmul(bank(("mod", v))[32 * g:32 * g + 32, 0:256], condT[:, k, :],
                                        w[g][:, k, :], start=(k == 0), stop=(k == KC - 1),
                                        skip_group_check=True)
                        if k == KC - 1:
                            ins.then_inc(ring_free, 1)
                pe.drain().then_inc(full[plan[("mod", v)][0]], 1)

            def rope(L, c):
                await_read(pe, L, ("proj", c))
                claim(pe, L, ("rope", c))
                src = kT[:, c, :] if c < 4 else qT[:, c - 4, :]
                ins = pe.matmul(bank(("rope", c))[:, 0:LAT], swap, src[:, P:P + LAT], start=True, stop=True)
                produced(ins, ("rope", c))

            def score(L, i):
                kind, h, t = STEPS[i]
                claim(pe, L, ("score", i))
                if i == 0:
                    pe.wait_ge(roped, L * 8 + 8)
                    await_read(pe, L, "cacheT")
                keys = slice(0, P) if t == 0 else slice(P, P + 384)
                nk = P if t == 0 else 384
                if kind == "da":
                    for m in range(2):
                        r = slice(DH * m, DH * m + DH)
                        ins = pe.matmul(bank(("score", i), 2)[:, m, 0:nk], qT[r, QCH["daq"] + h, t * P:(t + 1) * P],
                                        kT[r, KCH["dak"] + h, keys], start=True, stop=True)
                else:
                    r = slice(DH * (h % 2), DH * (h % 2) + DH)
                    ins = pe.matmul(bank(("score", i))[:, 0:nk], qT[r, QCH["naq"] + h // 2, t * P:(t + 1) * P],
                                    kT[r, KCH["nak"] + h // 2, keys], start=True, stop=True)
                produced(ins, ("score", i))

            def values(kind, h, t, kc):
                w, col = (P, P * h) if kind == "da" else (DH, 512 + DH * h)
                if t == 0:
                    return v_sb[:, 0, col:col + w]
                if kc < 2:
                    return v_sb[:, 1 + kc, col:col + w]
                return cache[:, 768 + col:768 + col + w]

            def prob_transposes(L, i):
                kind, h, t = STEPS[i]
                pe.wait_ge(prob_ready, L * N_STEPS + i + 1)
                claim(pe, L, ("probT", i))
                transposes(("probT", i), 1 if t == 0 else 3, lambda k: probs[:, i % 3, 0, k * P:(k + 1) * P])

            def attend(L, i):
                kind, h, t = STEPS[i]
                name = ("out", kind, h)
                if i == 0:
                    for n in (24, 25, 26):
                        await_read(pe, L, ("proj", n))
                if t == 0:
                    claim(pe, L, name)
                await_read(pe, L, ("probT", i))
                n = 1 if t == 0 else 3
                for kc in range(n):
                    v = values(kind, h, t, kc)
                    p = probT[:, i % 2, kc, :]
                    if kind == "da":
                        ins = pe.matmul(bank(name)[:, t * P:(t + 1) * P], p, v, start=(kc == 0), stop=(kc == n - 1),
                                        skip_group_check=True)
                    else:
                        r = slice(DH * (h % 2), DH * (h % 2) + DH)
                        ins = pe.matmul(bank(name)[r, t * P:(t + 1) * P], v, p, start=(kc == 0), stop=(kc == n - 1),
                                        skip_group_check=True)
                ins.then_inc(av_done, 1)
                if t == 2:
                    pe.drain().then_inc(full[plan[name][0]], 1)

            def out_proj(L, t):
                name = ("y", t)
                if t == 0:
                    for h in range(DA_HEADS):
                        await_read(pe, L, ("mixT", h))
                        await_read(pe, L, ("out", "na", h))
                    pe.wait_ge(mix_sc, 2 * L + 2)
                claim(pe, L, name)
                y = bank(name, 2).rearrange("p a b -> p (a b)")
                for n in range(4):
                    w = item(L, W_OUT0 + n).rearrange("p (k n) -> p k n", k=KC)
                    for k in range(KC):
                        ins = pe.matmul(y[:, 256 * n:256 * n + 256], mix[:, k, t * P:(t + 1) * P], w[:, k, :],
                                        start=(k == 0), stop=(k == KC - 1), skip_group_check=True)
                    if t == 2:
                        ins.then_inc(ring_free, 1)
                if t == 2:
                    pe.drain().then_inc(full[plan[name][0]], 1)
                else:
                    produced(ins, name)

            def router(L, t):
                pe.wait_ge(h2_ready, 3 * L + t + 1)
                claim(pe, L, ("h2T", t))
                transposes(("h2T", t), KC, lambda k: h2[:, t, :].rearrange("p (a k) -> p a k", k=KC)[:, :, k])
                await_read(pe, L, ("h2T", t))
                claim(pe, L, ("logit", t))
                for k in range(KC):
                    ins = pe.matmul(bank(("logit", t))[:, 0:E], hT[:, k, t * P:(t + 1) * P], routw[:, k, :],
                                    start=(k == 0), stop=(k == KC - 1))
                produced(ins, ("logit", t))

            def expert_block(i, w):
                pe.wait_ge(xg_in, i * 16)
                pe.wait_ge(xT_ready, i)
                for k in range(KC):
                    ins = pe.transpose(psA[:, k * P:(k + 1) * P],
                                       xg.rearrange("p (a k) -> p a k", k=KC)[:, :, k], ident)
                ins.then_inc(xT_full, 1)
                pe.wait_ge(xT_ready, i + 1)
                pe.wait_ge(hid_ready, i)
                for k in range(KC):
                    for h in range(2):
                        ins = pe.matmul(psD[HALF * h:HALF * h + HALF, :],
                                        xT[:, k * P + HALF * h:k * P + HALF * h + HALF],
                                        w[h][:, 2 * DE * k:2 * DE * k + 2 * DE],
                                        start=(k == 0), stop=(k == KC - 1), skip_group_check=True)
                ins.then_inc(up_full, 1)
                pe.wait_ge(hid_ready, i + 1)
                for k in range(2):
                    ins = pe.transpose(psB[:, k * P:(k + 1) * P], hid[:, k * P:(k + 1) * P], ident)
                ins.then_inc(hidT_full, 1)
                pe.wait_ge(hidT_ready, i + 1)
                pe.wait_ge(yo_ready, i)
                for n in range(2):
                    for k in range(2):
                        for h in range(2):
                            ins = pe.matmul(psC[HALF * h:HALF * h + HALF, 512 * n:512 * n + 512],
                                            hidT[:, k * P + HALF * h:k * P + HALF * h + HALF],
                                            w[h][:, 2 * DE * KC + D * k + 512 * n:2 * DE * KC + D * k + 512 * n + 512],
                                            start=(k == 0), stop=(k == 1), skip_group_check=True)
                ins.then_inc(down_full, 1)

            for s in SLOT_BANK:
                pe.sem_inc(free[s], 1)
            for s in (pair_done, xT_full, up_full, hidT_full, down_full):
                pe.sem_inc(s, 1)
            pe.wait_ge(const_in_s, 80)
            pe.wait_ge(cond_ready, 2)
            pe.wait_ge(constb_ready, 4)
            with pe.Fori(0, DEPTH) as L:
                pe.wait_ge(layer_in_s, (L + 1) * 16 * 6)
                claim(pe, L, "cacheT")
                transposes("cacheT", 6, lambda c: cache[:, c * P:(c + 1) * P])
                for v in range(2):
                    mod_vector(L, v)
                for t in range(TILES):
                    pe.wait_ge(xn_ready, 12 * L + t + 1)
                    claim(pe, L, ("hT", t))
                    transposes(("hT", t), KC, lambda k: xn[:, t, :].rearrange("p (a k) -> p a k", k=KC)[:, :, k])
                for t in range(TILES):
                    await_read(pe, L, ("hT", t))
                proj = 0
                for n, (piece, half_n) in enumerate(PIECES):
                    w = item(L, W_IN0 + n).rearrange("p (k n) -> p k n", k=KC)
                    jobs = TILES if piece in V_COL else 2
                    for j in range(jobs):
                        name = ("proj", proj)
                        claim(pe, L, name)
                        for k in range(KC):
                            if piece in V_COL:
                                ins = pe.matmul(bank(name)[:, 0:256], hT[:, k, j * P:(j + 1) * P], w[:, k, :],
                                                start=(k == 0), stop=(k == KC - 1))
                            else:
                                ins = pe.matmul(bank(name)[:, 0:T], w[:, k, j * P:(j + 1) * P], hT[:, k, :],
                                                start=(k == 0), stop=(k == KC - 1))
                        if j == jobs - 1:
                            ins.then_inc(ring_free, 1)
                            pe.drain().then_inc(full[plan[name][0]], 1)
                        else:
                            produced(ins, name)
                        proj += 1
                        if piece in ("dak", "daq"):
                            if proj >= 2:
                                rope(L, proj - 2)
                        elif proj == 9:
                            rope(L, 7)
                for n in (9, 10, 11):
                    await_read(pe, L, ("proj", n))
                claim(pe, L, "kout")
                transposes("kout", 6, lambda c: kT[:, c, 0:P])
                score(L, 0)
                score(L, 1)
                mixes = 0
                for i, (kind, h, t) in enumerate(STEPS):
                    if i + 2 < N_STEPS:
                        score(L, i + 2)
                    if kind == "da" and t == 2:
                        mod_vector(L, 2 + h)
                    prob_transposes(L, i)
                    attend(L, i)
                    if mixes < DA_HEADS and i == 3 * mixes + 2 + MIX_DELAY:
                        pe.wait_ge(on_ready, 4 * L + mixes + 1)
                        claim(pe, L, ("mixT", mixes))
                        transposes(("mixT", mixes), 3, lambda k: on[:, k, :])
                        mixes += 1
                out_proj(L, 0)
                out_proj(L, 1)
                router(L, 0)
                out_proj(L, 2)
                router(L, 1)
                router(L, 2)
                pe.wait_ge(mask_ready, L + 1)
                claim(pe, L, "place")
                place = bank("place")
                for t in range(TILES):
                    for s in range(t + 1):
                        pe.matmul(place[:, t * E:(t + 1) * E], ones if s < t else utri, maskb[:, s * E:(s + 1) * E],
                                  start=(s == 0), stop=(s == t), skip_group_check=True)
                for t in range(TILES):
                    ins = pe.matmul(place[:, TILES * E:TILES * E + E], ones, maskb[:, t * E:(t + 1) * E],
                                    start=(t == 0), stop=(t == TILES - 1), skip_group_check=True)
                produced(ins, "place")
                pe.wait_ge(sel_ready, L + 1)
                claim(pe, L, "index")
                for n in range(2 * TILES):
                    ins = pe.matmul(bank("index")[:, 0:2 * BLOCKS], sel[:, n, :],
                                    where[:, n, :, :].rearrange("p a b -> p (a b)"),
                                    start=(n == 0), stop=(n == 2 * TILES - 1))
                produced(ins, "index")
                pe.wait_ge(table_ready, L + 1)
                stop_here(pe, "pe")
                active = pe.value_load(tabu[0:1, T_ACTIVE:T_ACTIVE + 1], min_val=1, max_val=E)
                with pe.Fori(0, PAIRS // 2) as two:
                    for odd in range(2):
                        w = [expert_w[:, (2 * odd + h) * EXPERT:(2 * odd + h + 1) * EXPERT] for h in range(2)]
                        for h in range(2):
                            pe.wait_ge(expert_in[2 * odd + h], (L * (E // BUFS) + two + 1) * 16)
                        with pe.If(active > two * 4 + 2 * odd):
                            start = pe.value_load(tabu[0:1, bass.ds(two * 2 + (T_START + odd), 1)], min_val=1, max_val=BLOCKS * DEPTH + 1)
                            blocks = pe.value_load(tabu[0:1, bass.ds(two * 2 + (T_BLOCKS + odd), 1)], min_val=1, max_val=T // HALF)
                            with pe.Fori(0, blocks) as j:
                                expert_block(start + j, w)
                        pe.drain().then_inc(pair_done, 1)

        @block.scalar
        def _(act):
            restart, link = chain(act, act_done)
            copy = ACT.Copy

            def normalise(L, n, src, dst):
                act.wait_ge(rstd_ready, 12 * L + n + 1)
                act.activation(dst, src, ACT.Identity, scale=lnv[:, n % 3, 1:2],
                               bias=lnv[:, n % 3, 2:3]).then_inc(xn_ready, 1)

            for t in range(TILES):
                act.dma_start(x[:, t, :], x_in[t]).then_inc(x_in_s, 16)
            act.dma_start(condv[:, :, :], cond_in).then_inc(const_in_s, 16)
            act.dma_start(const[:, :], const_in[:, 0:N_KEPT]).then_inc(const_in_s, 16)
            act.dma_start(wide[:, 0:2 * P], const_in[:, N_KEPT:N_CONST]).then_inc(const_in_s, 16)
            act.dma_start(routw[:, :, :], router_in).then_inc(const_in_s, 16)
            act.dma_start(broute[:, :], brouter_in.partition_broadcast(P)).then_inc(const_in_s, 16)
            act.wait_ge(const_in_s, 80)
            act.activation(conds[:, 0, :, :], condv[:, :, :], ACT.Exp, scale=-1.0).then_inc(cond_exp, 1)
            for s in (xT_ready, up_exp, hidT_ready, yo_ready):
                act.sem_inc(s, 1)
            act.sem_inc(yo_stored, 16)
            act.sem_inc(state_out, 16)
            with act.Fori(0, DEPTH) as L:
                restart()
                for t in range(TILES):
                    normalise(L, t, x[:, t, :], xn[:, t, :])
                    if t == 0:
                        await_product(act, L, "cacheT")
                        read_out(act.activation(kT[:, :, 384:512],
                                                bank("cacheT", 2).rearrange("p a b -> p (a b)")[:, 0:768]
                                                .rearrange("p (c t) -> p c t", c=6), copy), "cacheT")
                        act.wait_ge(mrow_ready, N_MOD * L + 2)
                        for c in range(2):
                            act.dma_start(mod_d[c, 0:2, :].rearrange("v (g n) -> g v n", g=4),
                                          mrow[c:c + 97:32, 0:2, :]).then_inc(mod_stored, 16)
                act.wait_ge(lam_dot, 2 * L + 2)
                act.activation(lams[:, 2:4], lams[:, 0:2], ACT.Exp).then_inc(lam_exp, 1)
                proj = 0
                for piece, half_n in PIECES:
                    for j in range(TILES if piece in V_COL else 2):
                        name = ("proj", proj)
                        await_product(act, L, name)
                        if piece in V_COL:
                            col = V_COL[piece] + 256 * half_n
                            ins = act.activation(v_sb[:, j, col:col + 256], bank(name)[:, 0:256], copy)
                        elif piece in KCH:
                            ins = act.activation(kT[:, KCH[piece] + 2 * half_n + j, 0:T], bank(name)[:, 0:T], copy)
                        else:
                            ins = act.activation(qT[:, QCH[piece] + 2 * half_n + j, :], bank(name)[:, 0:T], copy,
                                                 scale=SCALE if piece in ("daq", "naq") else 1.0)
                        read_out(ins, name)
                        proj += 1
                await_product(act, L, "kout")
                read_out(act.activation(kout[:, :], bank("kout", 2).rearrange("p a b -> p (a b)")[:, 0:768], copy), "kout")
                await_read(act, L, "kout")
                act.dma_start(new_da_k[L], kout[:, 0:512]).then_inc(state_out, 16)
                act.dma_start(new_na_k[L], kout[:, 512:768]).then_inc(state_out, 16)
                act.dma_start(new_da_v[L], v_sb[:, 0, 0:512]).then_inc(state_out, 16)
                act.dma_start(new_na_v[L], v_sb[:, 0, 512:768]).then_inc(state_out, 16)

                def exps(i):
                    kind, h, t = STEPS[i]
                    nk = P if t == 0 else 384
                    act.wait_ge(max_ready, N_STEPS * L + i + 1)
                    if i >= 3:
                        await_product(act, L, ("probT", i - 3))
                    n = 2 if kind == "da" else 1
                    for m in range(n):
                        src = bank(("score", i), 2)[:, m, 0:nk]
                        ins = act.activation(probs[:, i % 3, m, 0:nk], src, ACT.Exp, bias=mxs[:, i % 3, m:m + 1],
                                             accum_out=rsum[:, i % 3, m:m + 1])
                    read_out(ins, ("score", i))

                def probT_out(i):
                    kind, h, t = STEPS[i]
                    n = 1 if t == 0 else 3
                    name = ("probT", i)
                    await_product(act, L, name)
                    if i >= 2:
                        act.wait_ge(av_done, N_STEPS * L + i - 1)
                    read_out(act.activation(probT[:, i % 2, 0:n, :],
                                            bank(name)[:, 0:n * P].rearrange("p (k t) -> p k t", k=n), copy), name)

                exps(0)
                mixes = 0
                for i, (kind, h, t) in enumerate(STEPS):
                    if i + 1 < N_STEPS:
                        exps(i + 1)
                    if kind == "da" and t == 2:
                        v = 2 + h
                        act.wait_ge(mrow_ready, N_MOD * L + v + 1)
                        for c in range(2):
                            act.dma_start(mod_d[c, v, :].rearrange("(g n) -> g n", g=4),
                                          mrow[c:c + 97:32, v, :]).then_inc(mod_stored, 16)
                    probT_out(i)
                    if t == 2:
                        name = ("out", kind, h)
                        await_product(act, L, name)
                        if kind == "da":
                            if h:
                                act.wait_ge(on_ready, 4 * L + h)
                            ins = act.activation(osb[:, :, :], bank(name)[:, 0:T].rearrange("p (t d) -> p t d", t=TILES), copy)
                        else:
                            r = slice(DH * (h % 2), DH * (h % 2) + DH)
                            ins = act.activation(mix[r, h // 2, :], bank(name)[r, 0:T], copy)
                        read_out(ins, name)
                    if mixes < DA_HEADS and i == 3 * mixes + 2 + MIX_DELAY:
                        name = ("mixT", mixes)
                        await_product(act, L, name)
                        read_out(act.activation(mix[:, 4 + mixes, :], bank(name)[:, 0:T], copy), name)
                        mixes += 1

                def h2T_out(t):
                    name = ("h2T", t)
                    await_product(act, L, name)
                    read_out(act.activation(hT[:, :, t * P:(t + 1) * P],
                                            bank(name, 2).rearrange("p a (b q) -> p (a b) q", q=P), copy), name)
                    act.wait_ge(h2_ready, 3 * L + t + 1)
                    act.dma_start(h2_d[t * P:(t + 1) * P, :], h2[:, t, :]).then_inc(h2_stored, 16)

                def logit_exps(t):
                    name = ("logit", t)
                    await_product(act, L, name)
                    read_out(act.activation(rt[:, 0, t * E:(t + 1) * E], bank(name)[:, 0:E], ACT.Exp, scale=-1.0), name)

                for t in range(TILES):
                    normalise(L, 3 + 2 * t, x[:, t, :], x[:, t, :])
                    normalise(L, 4 + 2 * t, x[:, t, :], h2[:, t, :])
                    h2T_out(t)
                    logit_exps(t)

                act.wait_ge(table_ready, L + 1)
                stop_here(act, "act")
                first = act.value_load(tabu[0:1, T_FIRST:T_FIRST + 1], min_val=1, max_val=BLOCKS * DEPTH + 1)
                count = act.value_load(tabu[0:1, T_COUNT:T_COUNT + 1], min_val=1, max_val=BLOCKS)
                with act.Fori(0, count) as j:
                    i = j + first
                    act.wait_ge(xT_full, i + 1)
                    act.wait_ge(up_full, i)
                    act.activation(xT, psA, copy).then_inc(xT_ready, 1)
                    act.wait_ge(up_full, i + 1)
                    act.wait_ge(hid_ready, i)
                    act.activation(silu, psD[:, 0:DE], ACT.Exp, scale=-1.0).then_inc(up_exp, 1)
                    act.wait_ge(hidT_full, i + 1)
                    act.wait_ge(down_full, i)
                    act.activation(hidT, psB[:, 0:DE], copy).then_inc(hidT_ready, 1)
                    act.wait_ge(down_full, i + 1)
                    act.wait_ge(yo_stored, i * 16)
                    act.activation(yo, psC, copy).then_inc(yo_ready, 1)
                    act.wait_ge(yo_ready, i + 1)
                    act.dma_start(moe_d[bass.ds(j * P, P), :], yo).then_inc(yo_stored, 16)
                for t in range(TILES):
                    normalise(L, 9 + t, x[:, t, :], x[:, t, :])
            for t in range(TILES):
                act.wait_ge(gained, 6 * (DEPTH - 1) + 3 + t + 2)
                act.dma_start(y_prompt if t == 0 else y_sample[(t - 1) * P:t * P, :], x[:, t, :]).then_inc(x_out, 16)
            act.wait_ge(x_out, 48)
            act.wait_ge(state_out, 64 * DEPTH + 16)

        @block.vector
        def _(dve):
            restart, link = chain(dve, dve_done)
            tt, ts, stt = dve.tensor_tensor, dve.tensor_scalar, dve.scalar_tensor_tensor

            def norm_stats(L, n, src):
                for half_n in range(2):
                    ins = dve.bn_stats(stats[:, n % 3, half_n, :], src[:, 512 * half_n:512 * half_n + 512])
                    link(ins)
                dve.bn_aggr(mv[:, n % 3, :], stats[:, n % 3, :, :].rearrange("p a b -> p (a b)")).then_inc(stats_ready, 1)

            def mod_out(L, v):
                name = ("mod", v)
                if v == 0:
                    dve.wait_ge(bmod_in_s, 64 * (L + 1))
                await_product(dve, L, name)
                link(tt(mrow[:, v, :], bank(name)[:, 0:256], mrow[:, v, :], ALU.add))
                dve.sem_inc(free[plan[name][0]], 1)
                dve.sem_inc(mrow_ready, 1)

            link(dve.memset(tab[:, :], 1.0))
            dve.sem_inc(hid_ready, 1)
            dve.sem_inc(silu_step, 3)
            link(dve.memset(condT[:, :, :], 0.0))
            link(dve.memset(half[:, 0:3], -0.5))
            dve.memset(half[:, 3:4], EPS).then_inc(cond_ready, 1)
            dve.wait_ge(const_in_s, 80)
            dve.tensor_copy(constb[:, 0:P], wide[:, 0:P]).then_inc(constb_ready, 1)
            dve.memset(constb[:, P:2 * P], 1.0).then_inc(constb_ready, 1)
            dve.tensor_copy(constb[:, 2 * P:3 * P], wide[:, P:2 * P]).then_inc(constb_ready, 1)
            dve.tensor_copy(constb[:, 3 * P:3 * P + 6], const[:, C_TOK:C_TOK + 6]).then_inc(constb_ready, 1)
            dve.wait_ge(cond_exp, 1)
            link(ts(conds[:, 1, :, :], conds[:, 0, :, :], 1.0, None, ALU.add))
            link(dve.reciprocal(conds[:, 0, :, :], conds[:, 1, :, :]))
            tt(condT[:, :, 0:2], condv[:, :, :].rearrange("p c k -> p k c"),
               conds[:, 0, :, :].rearrange("p c k -> p k c"), ALU.mult).then_inc(cond_ready, 1)
            dve.wait_ge(constb_ready, 4)
            dve.wait_ge(x_in_s, 48)

            with dve.Fori(0, DEPTH) as L:
                restart()
                for t in range(TILES):
                    dve.wait_ge(gained, 6 * L + 1) if t == 0 else None
                    norm_stats(L, t, x[:, t, :])
                dve.wait_ge(layer_in_s, (L + 1) * 16 * 6)
                link(tt(wide[:, 0:128].rearrange("p (a b) -> p a b", a=2), lamv[:, 0:3:2, :], lamv[:, 1:4:2, :], ALU.mult))
                for a in range(2):
                    dve.tensor_reduce(lams[:, a:a + 1], wide[:, 64 * a:64 * a + 64], AX.X, ALU.add).then_inc(lam_dot, 1)
                mod_out(L, 0)
                mod_out(L, 1)
                dve.wait_ge(mod_loaded, (L + 1) * 16 * 4)
                link(ts(modT[:, :, 1, :], modT[:, :, 1, :], 1.0, None, ALU.add))
                for t in range(TILES):
                    name = ("hT", t)
                    await_product(dve, L, name)
                    c = min(t, 1)
                    for k in range(KC):
                        ins = ts(hT[:, k, t * P:(t + 1) * P], bank(name, 2).rearrange("p a b -> p (a b)")[:, k * P:(k + 1) * P],
                                 modT[:, c, 1, k:k + 1], modT[:, c, 0, k:k + 1], ALU.mult, ALU.add)
                    read_out(ins, name)
                for c in range(8):
                    name = ("rope", c)
                    await_product(dve, L, name)
                    src = (kT[:, c, :] if c < 4 else qT[:, c - 4, :])[:, P:P + LAT]
                    ins = tt(wide[:, 0:LAT], bank(name)[:, 0:LAT], sin_t, ALU.mult)
                    read_out(ins, name)
                    link(tt(src, src, cos_t, ALU.mult))
                    tt(src, src, wide[:, 0:LAT], ALU.add).then_inc(roped, 1)
                    dve.wait_ge(roped, 8 * L + c + 1)
                dve.wait_ge(lam_exp, L + 1)
                link(tt(lams[:, 4:5], lams[:, 2:3], lams[:, 3:4], ALU.subtract))
                link(tt(lams[:, 5:6], lams[:, 4:5], lamc[:, 0:1], ALU.add))
                link(ts(gain[:, :], gain[:, :], lamc[:, 1:2], None, ALU.mult))

                def row_max(i):
                    kind, h, t = STEPS[i]
                    nk = P if t == 0 else 384
                    name = ("score", i)
                    await_product(dve, L, name)
                    if kind == "da":
                        ins = dve.tensor_reduce(mxs[:, i % 3, :], bank(name, 2)[:, :, 0:nk], AX.X, ALU.max, negate=True)
                    else:
                        if t > 0:
                            if h == 0 and t == 1:
                                dve.wait_ge(bias_ready, L + 1)
                            s0 = 2 - 2 * (t - 1)
                            link(tt(bank(name)[:, 0:LAT], bank(name)[:, 0:LAT],
                                    bias[:, h, s0:s0 + 4, :].rearrange("p a b -> p (a b)"), ALU.add))
                        ins = dve.tensor_reduce(mxs[:, i % 3, 0:1], bank(name)[:, 0:nk], AX.X, ALU.max, negate=True)
                    ins.then_inc(max_ready, 1)

                def probabilities(i):
                    kind, h, t = STEPS[i]
                    nk = P if t == 0 else 384
                    await_read(dve, L, ("score", i))
                    p = probs[:, i % 3, :, 0:nk]
                    r = rinv[:, i % 3, :]
                    if kind == "da":
                        link(dve.reciprocal(r[:, 0:2], rsum[:, i % 3, :]))
                        link(tt(r[:, 2:3], r[:, 1:2], lams[:, 5:6], ALU.mult))
                        link(ts(p[:, 1, :], p[:, 1, :], r[:, 2:3], None, ALU.mult))
                        stt(p[:, 0, :], p[:, 0, :], r[:, 0:1], p[:, 1, :], ALU.mult, ALU.subtract).then_inc(prob_ready, 1)
                    else:
                        link(dve.reciprocal(r[:, 0:1], rsum[:, i % 3, 0:1]))
                        ts(p[:, 0, :], p[:, 0, :], r[:, 0:1], None, ALU.mult).then_inc(prob_ready, 1)

                def head_norm(h):
                    await_read(dve, L, ("out", "da", h))
                    link(tt(sq[:, :, :], osb[:, :, :], osb[:, :, :], ALU.mult))
                    link(dve.tensor_reduce(msr[:, 0, :], sq[:, :, :], AX.X, ALU.add))
                    ts(msr[:, 1, :], msr[:, 0, :], 1.0 / P, EPS, ALU.mult, ALU.add).then_inc(ms_ready, 1)

                def head_scale(h):
                    dve.wait_ge(rms_ready, 4 * L + h + 1)
                    if h:
                        await_product(dve, L, ("mixT", h - 1))
                    for t in range(TILES):
                        ins = stt(on[:, t, :], osb[:, t, :], msr[:, 2, t:t + 1], gain[:, :], ALU.mult, ALU.mult)
                    link(ins)
                    dve.sem_inc(on_ready, 1)

                def conv(c):
                    z, o = wide[:, 0:T], wide[:, T:2 * T]
                    link(tt(z, qT[:, QCH["scc"] + c, :], qT[:, QCH["scx"] + c, :], ALU.mult))
                    link(ts(o, z, convp[:, c, 1:2], convp[:, c, 3:4], ALU.mult, ALU.add))
                    for a, b in ((0, P), (P, T)):
                        link(stt(o[:, a + 1:b], z[:, a:b - 1], convp[:, c, 0:1], o[:, a + 1:b], ALU.mult, ALU.add))
                        link(stt(o[:, a:b - 1], z[:, a + 1:b], convp[:, c, 2:3], o[:, a:b - 1], ALU.mult, ALU.add))
                    link(tt(mix[:, 2 + c, :], o, qT[:, QCH["scb"] + c, :], ALU.mult))
                    dve.sem_inc(mix_sc, 1)

                row_max(0)
                row_max(1)
                for i, (kind, h, t) in enumerate(STEPS):
                    probabilities(i)
                    if i + 2 < N_STEPS:
                        row_max(i + 2)
                    if kind == "da" and t == 2:
                        mod_out(L, 2 + h)
                    if i in (1, 2):
                        conv(i - 1)
                    if i >= 3 and (i - 3) % 3 == 0 and (i - 3) // 3 < DA_HEADS:
                        head_norm((i - 3) // 3)
                    if i >= 4 and (i - 4) % 3 == 0 and (i - 4) // 3 < DA_HEADS:
                        head_scale((i - 4) // 3)

                def residual(t, tmp):
                    ins = stt(x[:, t, :], x[:, t, :], ALPHA, tmp, ALU.mult, ALU.add)
                    link(ins)

                dve.wait_ge(gate1_in, 16 * (L + 1))
                dve.wait_ge(mod2_in, 16 * (L + 1))

                for t in range(TILES):
                    name = ("y", t)
                    c = min(t, 1)
                    await_product(dve, L, name)
                    ins = tt(wide[:, 0:D], bank(name, 2).rearrange("p a b -> p (a b)"), gate_b[:, c, :], ALU.mult)
                    read_out(ins, name)
                    await_read(dve, L, name)
                    residual(t, wide[:, 0:D])
                    norm_stats(L, 3 + 2 * t, x[:, t, :])
                    dve.wait_ge(gained, 6 * L + t + 2)
                    norm_stats(L, 4 + 2 * t, x[:, t, :])
                    dve.wait_ge(xn_ready, 12 * L + 5 + 2 * t)
                    link(stt(h2[:, t, :], mod2_b[:, c, 1, :], 1.0, h2[:, t, :], ALU.add, ALU.mult))
                    tt(h2[:, t, :], h2[:, t, :], mod2_b[:, c, 0, :], ALU.add).then_inc(h2_ready, 1)

                def v16(n):
                    return rt[:, n, :]

                def v44(n):
                    return rt[:, n, :].rearrange("p (g j) -> p g j", j=4)

                def ranks(val, n_out, a, b):
                    n = val.shape[1]
                    vi = val.rearrange("p (g u i) -> p g u i", u=1, i=4).broadcast_to([P, n // 4, 4, 4])
                    vj = val.rearrange("p (g j u) -> p g j u", j=4, u=1).broadcast_to([P, n // 4, 4, 4])
                    pa = pair[:, 0, 0:4 * n].rearrange("p (g j i) -> p g j i", j=4, i=4)
                    pb = pair[:, 1, 0:4 * n].rearrange("p (g j i) -> p g j i", j=4, i=4)
                    lt = const[:, C_LT4:C_LT4 + 16].rearrange("p (g j i) -> p g j i", g=1, i=4).broadcast_to([P, n // 4, 4, 4])
                    link(tt(pa, vi, vj, ALU.is_gt))
                    link(tt(pb, vi, vj, ALU.is_equal))
                    link(tt(pb, pb, lt, ALU.mult))
                    link(tt(pa, pa, pb, ALU.add))
                    link(dve.tensor_reduce(n_out, pa, AX.X, ALU.add))

                for t in range(TILES):
                    await_read(dve, L, ("logit", t))
                link(ts(v16(1), v16(0), 1.0, None, ALU.add))
                link(dve.reciprocal(v16(2), v16(1)))
                link(tt(v16(3).rearrange("p (t e) -> p t e", t=TILES), v16(2).rearrange("p (t e) -> p t e", t=TILES),
                        broute[:, :].rearrange("p (u e) -> p u e", u=1).broadcast_to([P, TILES, E]), ALU.add))
                ranks(v16(3), v44(4), 0, 1)
                link(ts(v16(4), v16(4), 2.0, None, ALU.is_lt))
                link(tt(v16(5), v16(4), v16(3), ALU.mult))
                link(dve.tensor_reduce(rt[:, 6, 0:TILES * GROUPS], v44(5), AX.X, ALU.add))
                ranks(rt[:, 6, 0:TILES * GROUPS], rt[:, 7, 0:TILES * GROUPS].rearrange("p (t g) -> p t g", g=4), 0, 1)
                link(ts(rt[:, 7, 0:TILES * GROUPS], rt[:, 7, 0:TILES * GROUPS], 1.0, None, ALU.is_lt))
                link(tt(v44(8), v44(4), rt[:, 7, 0:TILES * GROUPS].rearrange("p (g u) -> p g u", u=1)
                        .broadcast_to([P, TILES * GROUPS, 4]), ALU.mult))
                dve.tensor_copy(maskb[:, :], v16(8)).then_inc(mask_ready, 1)
                link(tt(v16(9), v16(8), v16(2), ALU.mult))
                link(dve.tensor_reduce(st[:, 0:3], v16(9).rearrange("p (t e) -> p t e", t=TILES), AX.X, ALU.add))
                link(dve.reciprocal(st[:, 3:6], st[:, 0:3]))
                link(tt(v16(9).rearrange("p (t e) -> p t e", t=TILES), v16(9).rearrange("p (t e) -> p t e", t=TILES),
                        st[:, 3:6].rearrange("p (t u) -> p t u", u=1).broadcast_to([P, TILES, E]), ALU.mult))
                await_product(dve, L, "place")
                link(dve.tensor_copy(v16(10), bank("place")[:, 0:TILES * E]))
                tokens = rt[:, 15, 0:E]
                read_out(dve.tensor_copy(tokens, bank("place")[:, TILES * E:TILES * E + E]), "place")
                await_read(dve, L, "place")

                def rows(ap, n):
                    return ap.rearrange("p (u e) -> p u e", u=1).broadcast_to([P, n, E])

                def cols(ap, n):
                    return ap.rearrange("p (e u) -> p e u", u=1).broadcast_to([P, ap.shape[1], n])

                def grid(b, n, m):
                    return pair[:, b, 0:n * m].rearrange("p (a b) -> p a b", a=n)

                lt16 = const[:, C_LT16:C_LT16 + E * E].rearrange("p (a b) -> p a b", a=E)
                prev = const[:, C_PREV:C_PREV + E * E].rearrange("p (a b) -> p a b", a=E)
                num = const[:, C_NUM:C_NUM + 32]
                halves, rank, by_rank, base, bases = (rt[:, 11, 0:16], rt[:, 11, 16:32], rt[:, 11, 32:48],
                                                      rt[:, 12, 0:16], rt[:, 12, 16:32])
                link(tt(grid(0, E, 6), cols(tokens, 6),
                        const[:, C_HALF:C_HALF + 6].rearrange("p (u j) -> p u j", u=1).broadcast_to([P, E, 6]), ALU.is_gt))
                link(dve.tensor_reduce(halves, grid(0, E, 6), AX.X, ALU.add))
                link(tt(grid(0, E, E), rows(halves, E), cols(halves, E), ALU.is_gt))
                link(tt(grid(1, E, E), rows(halves, E), cols(halves, E), ALU.is_equal))
                link(tt(grid(1, E, E), grid(1, E, E), lt16, ALU.mult))
                link(tt(grid(0, E, E), grid(0, E, E), grid(1, E, E), ALU.add))
                link(dve.tensor_reduce(rank, grid(0, E, E), AX.X, ALU.add))
                link(tt(grid(1, E, E), rows(rank, E), cols(num[:, 0:E], E), ALU.is_equal))
                link(tt(grid(0, E, E), grid(1, E, E), rows(halves, E), ALU.mult))
                link(dve.tensor_reduce(by_rank, grid(0, E, E), AX.X, ALU.add))
                link(tt(grid(0, E, E), prev, rows(by_rank, E), ALU.mult))
                link(dve.tensor_reduce(base, grid(0, E, E), AX.X, ALU.add))
                link(stt(bases, base, float(P), const[:, C_HALF + 8:C_HALF + 24], ALU.mult, ALU.add))
                link(tt(grid(0, E, E), cols(rank, E), rows(num[:, 0:E], E), ALU.is_equal))
                link(tt(grid(0, E, E), grid(0, E, E), rows(bases, E), ALU.mult))
                link(dve.tensor_reduce(rt[:, 12, 32:48], grid(0, E, E), AX.X, ALU.add))
                link(tt(v16(0).rearrange("p (t e) -> p t e", t=TILES), rows(rt[:, 12, 32:48], TILES),
                        v16(10).rearrange("p (t e) -> p t e", t=TILES), ALU.add))
                t16 = lambda n: rt[:, n, :].rearrange("p (t e) -> p t e", t=TILES)
                link(tt(t16(13), t16(8), rows(const[:, C_NUM + 1:C_NUM + 1 + E], TILES), ALU.mult))
                link(dve.tensor_reduce(st[:, 0:3], t16(13), AX.X, ALU.max))
                link(tt(t16(13), t16(13), st[:, 0:3].rearrange("p (t u) -> p t u", u=1).broadcast_to([P, TILES, E]),
                        ALU.is_equal))
                link(tt(v16(14), v16(8), v16(13), ALU.subtract))
                for a, who in ((0, 14), (1, 13)):
                    link(tt(v16(3), v16(0), v16(who), ALU.mult))
                    link(dve.tensor_reduce(st[:, 8 + 3 * a:11 + 3 * a], t16(3), AX.X, ALU.add))
                    link(tt(v16(3), v16(10), v16(who), ALU.mult))
                    link(dve.tensor_reduce(st[:, 14 + 3 * a:17 + 3 * a], t16(3), AX.X, ALU.add))
                    link(tt(v16(3), v16(9), v16(who), ALU.mult))
                    link(dve.tensor_reduce(gates[:, a, :], t16(3), AX.X, ALU.add))
                over = pair[:, 0, 0:30].rearrange("p (c j) -> p c j", c=6)
                link(tt(over, cols(st[:, 14:20], 5),
                        const[:, C_HALF + 1:C_HALF + 6].rearrange("p (u j) -> p u j", u=1).broadcast_to([P, 6, 5]), ALU.is_ge))
                link(dve.tensor_reduce(st[:, 14:20], over, AX.X, ALU.add))
                link(stt(st[:, 8:14], st[:, 14:20], float(HALF), st[:, 8:14], ALU.mult, ALU.add))
                link(dve.tensor_copy(ridx[:, :, :].rearrange("p a t -> p (a t)"), st[:, 8:14]))
                link(tt(pair[:, 0, 0:6 * (BLOCKS - 1)].rearrange("p (c b) -> p c b", c=6), cols(st[:, 8:14], BLOCKS - 1),
                        const[:, C_ROWS:C_ROWS + BLOCKS - 1].rearrange("p (u b) -> p u b", u=1)
                        .broadcast_to([P, 6, BLOCKS - 1]), ALU.is_ge))
                link(dve.tensor_reduce(st[:, 14:20], pair[:, 0, 0:6 * (BLOCKS - 1)].rearrange("p (c b) -> p c b", c=6),
                                       AX.X, ALU.add))
                link(stt(st[:, 8:14], st[:, 14:20], -float(P), st[:, 8:14], ALU.mult, ALU.add))
                dve.wait_ge(state_out, 64 * (L + 1) + 16)
                link(tt(sel, cols(st[:, 8:14], P), iota.rearrange("p (u s) -> p u s", u=1).broadcast_to([P, 6, P]),
                        ALU.is_equal))
                blk = pair[:, 0, 0:6 * BLOCKS].rearrange("p (c b) -> p c b", c=6)
                link(tt(blk, cols(st[:, 14:20], BLOCKS),
                        num[:, 0:BLOCKS].rearrange("p (u b) -> p u b", u=1).broadcast_to([P, 6, BLOCKS]), ALU.is_equal))
                for part in range(2):
                    for t in range(TILES):
                        ins = ts(where[:, t::TILES, part, :], blk[:, t::TILES, :],
                                 const[:, C_TOK + 2 * t + part:C_TOK + 2 * t + part + 1], None, ALU.mult)
                link(ins)
                dve.sem_inc(sel_ready, 1)
                link(ts(pair[:, 0, 0:E], halves, 0.0, None, ALU.is_gt))
                link(dve.tensor_reduce(tab[:, T_ACTIVE:T_ACTIVE + 1], pair[:, 0, 0:E], AX.X, ALU.add))
                link(tt(grid(0, E, E), grid(1, E, E), rows(num[:, 0:E], E), ALU.mult))
                link(dve.tensor_reduce(tab[:, T_WHO:T_WHO + E], grid(0, E, E), AX.X, ALU.add))
                link(dve.tensor_copy(tab[:, T_BLOCKS:T_BLOCKS + PAIRS], by_rank[:, 0::2]))
                link(dve.tensor_reduce(tab[:, T_COUNT:T_COUNT + 1], by_rank[:, 0::2], AX.X, ALU.add))
                link(dve.tensor_copy(tab[:, T_FIRST:T_FIRST + 1], tab[:, T_LAST:T_LAST + 1]))
                link(ts(tab[:, T_START:T_START + PAIRS], base[:, 0::2], tab[:, T_FIRST:T_FIRST + 1], None, ALU.add))
                link(tt(tab[:, T_LAST:T_LAST + 1], tab[:, T_FIRST:T_FIRST + 1], tab[:, T_COUNT:T_COUNT + 1], ALU.add))
                link(dve.tensor_copy(tabu[:, :], tab[:, :]))
                dve.sem_inc(table_ready, 1)
                await_product(dve, L, "index")
                src = bank("index")[:, 0:2 * BLOCKS]
                link(dve.tensor_copy(pair[:, 0, 0:BLOCKS], src[:, BLOCKS:2 * BLOCKS]))
                read_out(tt(gidx[:, :], src[:, 0:BLOCKS], pair[:, 0, 0:BLOCKS], ALU.add), "index")

                first = dve.value_load(tabu[0:1, T_FIRST:T_FIRST + 1], min_val=1, max_val=BLOCKS * DEPTH + 1)
                count = dve.value_load(tabu[0:1, T_COUNT:T_COUNT + 1], min_val=1, max_val=BLOCKS)
                with dve.Fori(0, count) as j:
                    i = j + first
                    dve.wait_ge(up_exp, i + 1)
                    ts(silu, silu, 1.0, None, ALU.add).then_inc(silu_step, 1)
                    dve.wait_ge(silu_step, i * 3 + 1)
                    dve.reciprocal(silu, silu).then_inc(silu_step, 1)
                    dve.wait_ge(silu_step, i * 3 + 2)
                    tt(silu, silu, psD[:, 0:DE], ALU.mult).then_inc(silu_step, 1)
                    dve.wait_ge(silu_step, i * 3 + 3)
                    dve.wait_ge(hidT_full, i)
                    tt(hid, silu, psD[:, DE:2 * DE], ALU.mult).then_inc(hid_ready, 1)

                dve.wait_ge(gate2_in, 16 * (L + 1))
                for t in range(TILES):
                    c = min(t, 1)
                    a, b = fetched[2 * t], fetched[2 * t + 1]
                    dve.wait_ge(pick_in[2 * t], 16 * (L + 1))
                    dve.wait_ge(pick_in[2 * t + 1], 16 * (L + 1))
                    link(ts(a, a, gates[:, 0, t:t + 1], None, ALU.mult))
                    link(stt(a, b, gates[:, 1, t:t + 1], a, ALU.mult, ALU.add))
                    link(tt(a, a, gate_b[:, c, :], ALU.mult))
                    residual(t, a)
                    norm_stats(L, 9 + t, x[:, t, :])

        @block.gpsimd
        def _(pool):
            restart, link = chain(pool, pool_done)

            def rstd(L, n):
                pool.wait_ge(stats_ready, 12 * L + n + 1)
                b = n % 3
                link(pool.tensor_tensor(lnv[:, b, 0:1], mv[:, b, 1:2], half[:, 3:4], ALU.add))
                link(pool.tensor_tensor(lnv[:, b, 1:2], lnv[:, b, 0:1], half[:, 0:1], ALU.pow))
                pool.tensor_scalar(lnv[:, b, 2:3], mv[:, b, 0:1], lnv[:, b, 1:2], -1.0, ALU.mult, ALU.mult)\
                    .then_inc(rstd_ready, 1)

            def apply_gain(L, n, t):
                pool.wait_ge(xn_ready, 12 * L + n + 1)
                link(pool.tensor_tensor(x[:, t, :], x[:, t, :], ln_b[:, 0, :], ALU.mult))
                pool.tensor_tensor(x[:, t, :], x[:, t, :], ln_b[:, 1, :], ALU.add).then_inc(gained, 1)

            pool.wait_ge(cond_ready, 1)
            pool.wait_ge(const_in_s, 80)
            pool.sem_inc(gained, 1)
            pool.sem_inc(gcol_ready, 1)
            with pool.Fori(0, DEPTH) as L:
                restart()
                pool.wait_ge(gained, 6 * L + 1)
                pool.wait_ge(state_out, 64 * L + 16)
                pool.dma_start(cache[:, :], cache_in[L]).then_inc(layer_in_s, 16)
                pool.dma_start(convp[:, :, :], conv_in[L]).then_inc(layer_in_s, 16)
                pool.dma_start(lamv[:, :, :], lam_in[L].partition_broadcast(P)).then_inc(layer_in_s, 16)
                pool.dma_start(lamc[:, :], lamc_in[L].partition_broadcast(P)).then_inc(layer_in_s, 16)
                pool.dma_start(gain[:, :], gain_in[L].partition_broadcast(P)).then_inc(layer_in_s, 16)
                pool.dma_start(bias[:, :, :, :], bias_in[L]).then_inc(layer_in_s, 16)
                pool.dma_start(ln_b[:, :, :], ln_in[L, 0:2].partition_broadcast(P)).then_inc(ln_in_s, 16)
                for g in range(4):
                    pool.dma_start(mrow[32 * g:32 * g + 32, :, :], bmod_in[L, g].partition_broadcast(32)).then_inc(bmod_in_s, 16)
                for t in range(TILES):
                    rstd(L, t)
                pool.wait_ge(mod_stored, (L * 10 + 2) * 16)
                stop_here(pool, "pool")
                for c in range(2):
                    for v in range(2):
                        pool.dma_start(modT[:, c, v, :], mod_d[c, v, :].rearrange("(p k) -> p k", k=KC)).then_inc(mod_loaded, 16)
                pool.wait_ge(layer_in_s, (L + 1) * 16 * 6)
                flat = bias[:, :, :, :].rearrange("p h s c -> p (h s) c")
                pool.tensor_tensor(flat, flat, const[:, C_MASK:C_MASK + GRID_W].rearrange("p (u c) -> p u c", u=1)
                                   .broadcast_to([P, 6 * NA_HEADS, GRID_W]), ALU.add).then_inc(bias_ready, 1)
                with pool.If(L < 1):
                    pool.wait_ge(ln_in_s, 16)
                    pool.dma_start(moe_d.rearrange("(b p) d -> p b d", p=P),
                                   ln_b[:, 0:1, :].broadcast_to([P, BLOCKS, D])).then_inc(filled, 16)
                    pool.wait_ge(filled, 16)
                for h in range(DA_HEADS):
                    pool.wait_ge(ms_ready, 4 * L + h + 1)
                    pool.tensor_tensor(msr[:, 2, :], msr[:, 1, :], half[:, 0:3], ALU.pow).then_inc(rms_ready, 1)
                pool.wait_ge(mod_stored, (L * 10 + 10) * 16)
                stop_here(pool, "pool")
                pool.dma_start(gate_b[:, :, :], mod_d[:, 2, :].partition_broadcast(P)).then_inc(gate1_in, 16)
                pool.wait_ge(av_done, N_STEPS * (L + 1))
                stop_here(pool, "pool")
                pool.dma_start(mod2_b[:, :, :, :], mod_d[:, 3:5, :].partition_broadcast(P)).then_inc(mod2_in, 16)
                pool.wait_ge(ln_in_s, (2 * L + 1) * 16)
                for t in range(TILES):
                    rstd(L, 3 + 2 * t)
                    apply_gain(L, 3 + 2 * t, t)
                    rstd(L, 4 + 2 * t)
                pool.wait_ge(h2_ready, 3 * L + 3)
                pool.dma_start(ln_b[:, :, :], ln_in[L, 2:4].partition_broadcast(P)).then_inc(ln_in_s, 16)
                pool.dma_start(gate_b[:, :, :], mod_d[:, 5, :].partition_broadcast(P)).then_inc(gate2_in, 16)
                pool.wait_ge(h2_stored, 16 * 3 * (L + 1))
                await_read(pool, L, "index")
                pool.wait_ge(table_ready, L + 1)
                stop_here(pool, "pool")
                first = pool.value_load(tabu[0:1, T_FIRST:T_FIRST + 1], min_val=1, max_val=BLOCKS * DEPTH + 1)
                count = pool.value_load(tabu[0:1, T_COUNT:T_COUNT + 1], min_val=1, max_val=BLOCKS)
                with pool.Fori(0, count) as j:
                    i = j + first
                    pool.wait_ge(xT_full, i)
                    pool.tensor_copy(gcol[:, :], gidx[:, bass.ds(j, 1)]).then_inc(gcol_ready, 1)
                    pool.wait_ge(gcol_ready, i + 1)
                    stop_here(pool, "pool")
                    pool.indirect_dma_start(xg, None, h2_d[:, :],
                                            bass.IndirectOffsetOnAxis(gcol[:, 0:1], 0)).then_inc(xg_in, 16)
                pool.wait_ge(yo_stored, (first + count) * 16)
                stop_here(pool, "pool")
                for t in range(TILES):
                    for a in range(2):
                        pool.indirect_dma_start(fetched[2 * t + a], None, moe_d[:, :],
                                                bass.IndirectOffsetOnAxis(ridx[:, a, t:t + 1], 0))\
                            .then_inc(pick_in[2 * t + a], 16)
                pool.wait_ge(ln_in_s, (2 * L + 2) * 16)
                for t in range(TILES):
                    rstd(L, 9 + t)
                    apply_gain(L, 9 + t, t)


def _constants():
    c = np.zeros((P, N_CONST), np.float32)
    p = np.arange(P)
    c[:, C_ID:C_ID + P] = np.eye(P)
    c[p, C_SWAP + (p ^ 16)] = 1.0
    j = p % 64
    inv = (np.float32(10000.0) ** (-np.arange(16, dtype=np.float32) / 16)).astype(np.float32)
    t = np.arange(LAT)
    pos = np.where((j // 32 == 0)[:, None], t[None, :] // GRID_W, t[None, :] % GRID_W).astype(np.float32)
    ang = pos * inv[j % 16][:, None]
    c[:, C_COS:C_COS + LAT] = np.cos(ang)
    c[:, C_SIN:C_SIN + LAT] = np.where((j % 32 < 16)[:, None], -np.sin(ang), np.sin(ang))
    qc, kc = p % GRID_W, np.arange(GRID_W)
    w0 = np.clip(qc - 8, 0, GRID_W - 16)[:, None]
    c[:, C_MASK:C_MASK + GRID_W] = np.where((kc >= w0) & (kc < w0 + 16), 0.0, MASKED)
    c[:, C_UTRI:C_UTRI + P] = p[:, None] < p[None, :]
    c[:, C_IOTA:C_IOTA + P] = p[None, :]
    jj, ii = np.meshgrid(np.arange(4), np.arange(4), indexing="ij")
    c[:, C_LT4:C_LT4 + 16] = (ii < jj).reshape(1, 16)
    c[:, C_NUM:C_NUM + 32] = np.arange(32)
    r = np.arange(E)
    c[:, C_LT16:C_LT16 + E * E] = (r[None, :] < r[:, None]).reshape(1, E * E)
    c[:, C_PREV:C_PREV + E * E] = ((r[None, :] % 2 == 0) & (r[None, :] < r[:, None] // 2 * 2)).reshape(1, E * E)
    c[:, C_ROWS:C_ROWS + BLOCKS - 1] = P * np.arange(1, BLOCKS)
    c[:, C_HALF:C_HALF + 6] = HALF * np.arange(6)
    c[:, C_HALF + 8:C_HALF + 24] = HALF * (r % 2)
    for t in range(TILES):
        c[:, C_TOK + 2 * t] = p
        c[:, C_TOK + 2 * t + 1] = P * t
    return c


def _experts(w1, w3, w2):
    up = np.concatenate([w1.reshape(DEPTH, E, P, KC, DE), w3.reshape(DEPTH, E, P, KC, DE)], axis=4)
    down = w2.reshape(DEPTH, E, 2, P, D).transpose(0, 1, 3, 2, 4)
    return np.concatenate([up.reshape(DEPTH, E, P, -1), down.reshape(DEPTH, E, P, -1)], axis=3).reshape(DEPTH * E, P, EXPERT)


def _weights(w_mod, w_in, w_out):
    walls = np.empty((DEPTH, ITEMS, P, ITEM), np.float32)
    for l in range(DEPTH):
        m = w_mod[l].reshape(P, KC, N_MOD, 4, 256)
        for v in range(N_MOD):
            for g in range(4):
                walls[l, MODS[v] + g] = m[:, :, v, g, :].reshape(P, ITEM)
        wi = w_in[l].reshape(P, KC, -1)
        for n, (piece, half) in enumerate(PIECES):
            col = PIECE_COL[piece] + 256 * half
            walls[l, W_IN0 + n] = wi[:, :, col:col + 256].reshape(P, ITEM)
        wo = w_out[l].reshape(KC, P, D)
        for n in range(4):
            walls[l, W_OUT0 + n] = wo[:, :, 256 * n:256 * n + 256].transpose(1, 0, 2).reshape(P, ITEM)
    return walls.reshape(DEPTH * ITEMS, P, ITEM)


def _local_bias(rel):
    p = np.arange(P)[:, None, None]
    row = np.arange(6)[None, :, None] + np.where(p < 64, 5, 4)
    col = np.clip(np.arange(GRID_W)[None, None, :] - p % GRID_W + 15, 0, 30)
    return np.ascontiguousarray(rel[:, :, row, col].transpose(0, 2, 1, 3, 4))


def kernel(x_prompt, x_sample, cache_na_k, cache_na_v, cache_da_k, cache_da_v, c, c_ctx,
           w_mod, b_mod, w_in, na_rel_bias, sc_conv_w, sc_conv_b, da_lambda, da_norm_g, w_out,
           ln1_g, ln1_b, w_router, b_router, moe_w1, moe_w3, moe_w2, ln2_g, ln2_b):
    import math

    import concourse.bacc as bacc
    from concourse.bass_utils import run_bass_kernel_spmd

    a = np.asarray
    cache = np.concatenate([a(cache_da_k)[0].reshape(DEPTH, P, 512), a(cache_na_k)[0].reshape(DEPTH, P, 256),
                            a(cache_da_v)[0].reshape(DEPTH, P, 512), a(cache_na_v)[0].reshape(DEPTH, P, 256)], axis=2)
    conv = np.concatenate([a(sc_conv_w), a(sc_conv_b)[:, None]], axis=1).reshape(DEPTH, 4, 2, P).transpose(0, 3, 2, 1)
    lam_init = [0.8 - 0.6 * math.exp(-0.3 * l) for l in range(DEPTH)]
    ins = {
        "weights": _weights(a(w_mod), a(w_in), a(w_out)),
        "experts": _experts(a(moe_w1), a(moe_w3), a(moe_w2)),
        "x": np.concatenate([a(x_prompt)[0], a(x_sample)[0]]).reshape(TILES, P, D),
        "cond": np.stack([a(c_ctx), a(c)[0]]).reshape(2, P, KC).transpose(1, 0, 2),
        "cache": cache,
        "local_bias": _local_bias(a(na_rel_bias)),
        "conv": conv,
        "da_lambda": a(da_lambda),
        "lambda_init": np.array([[v, 1.0 - v] for v in lam_init], np.float32),
        "da_gain": a(da_norm_g),
        "ln": np.stack([a(ln1_g), a(ln1_b), a(ln2_g), a(ln2_b)], axis=1),
        "w_router": a(w_router).reshape(P, KC, E),
        "b_router": a(b_router),
        "b_mod": a(b_mod).reshape(DEPTH, N_MOD, 4, 256).transpose(0, 2, 1, 3),
        "constants": _constants(),
    }
    ins = {k: np.ascontiguousarray(v) for k, v in ins.items()}
    outs = {"y_prompt": (P, D), "y_sample": (LAT, D), "new_na_k": (DEPTH, P, 256), "new_na_v": (DEPTH, P, 256),
            "new_da_k": (DEPTH, P, 512), "new_da_v": (DEPTH, P, 512)}
    nc = bacc.Bacc("TRN2", target_bir_lowering=False, num_devices=1)
    args = [nc.dram_tensor(f"in_{k}", v.shape, F32, kind="ExternalInput").ap() for k, v in ins.items()]
    args += [nc.dram_tensor(f"out_{k}", s, F32, kind="ExternalOutput").ap() for k, s in outs.items()]
    hybrid_step_kernel(nc, *args)
    r = run_bass_kernel_spmd(nc, [{f"in_{k}": v for k, v in ins.items()}], core_ids=[0]).results[0]
    return (r["out_y_prompt"].reshape(1, P, D), r["out_y_sample"].reshape(1, LAT, D),
            r["out_new_na_k"].reshape(1, DEPTH, P, 4, 64), r["out_new_na_v"].reshape(1, DEPTH, P, 4, 64),
            r["out_new_da_k"].reshape(1, DEPTH, P, 8, 64), r["out_new_da_v"].reshape(1, DEPTH, P, 4, 128))
```

```python
from contextlib import ExitStack

import numpy as np

import concourse.bass as bass
from concourse import mybir

ALU = mybir.AluOpType
ACT = mybir.ActivationFunctionType
AX = mybir.AxisListType
F32 = mybir.dt.float32
BF16 = mybir.dt.bfloat16
U32 = mybir.dt.uint32

P = 128
D = 1024
KC = D // P
DEPTH = 2
TILES = 3
T = TILES * P
LAT = 2 * P
GRID_W = 64
DA_HEADS = 4
NA_HEADS = 4
DH = 64
E = 16
GROUPS = 4
DE = 256
HALF = 64
PAIRS = E // 2
BLOCKS = (2 * T // HALF + E - 1 + T // HALF) // 2
EXPERT = 6144
UP = 4096
BUFS = 4
SCALE = DH ** -0.5
ALPHA = (2 * DEPTH) ** 0.25
EPS = 1e-5
MASKED = -1.0e30

RING = 8
ITEM = 2048
N_MOD = 6
W_IN0, MODS0, W_OUT0, NEXT0, ITEMS = 0, 12, 28, 32, 40

T_FIRST, T_ACTIVE, T_COUNT, T_START, T_LAST, T_NONE, T_BLOCKS, T_WHO = 0, 1, 2, 3, 11, 12, 13, 21
STAGES = PAIRS + 1
COLS = BLOCKS + 1

KCH = {"dak": 0, "nak": 4}
QCH = {"daq": 0, "naq": 4, "scc": 6, "scx": 8, "scb": 10}
PIECES = [("dak", 0), ("dak", 1), ("daq", 0), ("daq", 1), ("nak", 0), ("naq", 0),
          ("dav", 0), ("dav", 1), ("nav", 0), ("scc", 0), ("scx", 0), ("scb", 0)]
PIECE_COL = {"naq": 0, "nak": 256, "nav": 512, "scb": 768, "scc": 1024, "scx": 1280,
             "daq": 1536, "dak": 2048, "dav": 2560}
V_COL = {"dav": 0, "nav": 512}

(C_ID, C_SWAP, C_COS, C_SIN, C_MASK, C_UTRI, C_IOTA, C_LT4, C_NUM, C_TOK, C_LT16, C_PREV, C_ROWS, C_HALF) = (
    0, 128, 256, 512, 768, 1476, 1604, 832, 848, 880, 888, 1144, 1400, 1416)
N_KEPT = 1476
N_CONST = 1732
SLOT_BANK = {"A": 0, "B": 2, "C": 4, "D": 6, "E": 7}

STEPS = [("da", h, t) for h in range(DA_HEADS) for t in range(TILES)] + \
        [("na", h, t) for h in range(NA_HEADS) for t in range(TILES)]
N_STEPS = len(STEPS)
MIX_DELAY = 4


def psum_plan():
    jobs = [(("hT", t), "BCA"[t]) for t in range(TILES)]
    proj = 0
    for piece, half in PIECES:
        for j in range(TILES if piece in V_COL else 2):
            jobs.append((("proj", proj), "BCA"[proj % 3]))
            proj += 1
            if piece in ("dak", "daq"):
                if proj >= 2:
                    jobs.append((("rope", proj - 2), "DE"[proj % 2]))
            elif proj == 9:
                jobs.append((("rope", 7), "DE"[1]))
    jobs += [("cacheT", "C"), ("kout", "B")]
    jobs += [(("score", 0), "A"), (("score", 1), "B")]
    mixes = 0
    for i, (kind, h, t) in enumerate(STEPS):
        if i + 2 < N_STEPS:
            jobs.append((("score", i + 2), "ABC"[(i + 2) % 3]))
        jobs.append((("probT", i), "D"))
        if i > 0:
            last, g, u = STEPS[i - 1]
            if u == 0:
                jobs.append((("out", last, g), "E"))
            if last == "da" and u == 2:
                jobs.append((("mod", 2 + g), "D"))
        if mixes < DA_HEADS and i == 3 * mixes + 2 + MIX_DELAY:
            jobs.append((("mixT", mixes), "D"))
            mixes += 1
    jobs += [(("y", t), "ABC"[t]) for t in range(TILES)]
    for t in range(TILES):
        jobs += [(("h2T", t), "ABC"[t]), (("logit", t), "DED"[t])]
    jobs.append(("place", "E"))
    jobs.append(("index", "D"))
    turn, plan = {s: 0 for s in SLOT_BANK}, {}
    for name, slot in jobs:
        assert name not in plan, name
        plan[name] = (slot, turn[slot])
        turn[slot] += 1
    return plan, turn


def hybrid_step_kernel(nc, walls, experts_in, x_in, cond_in, cache_in, bias_in, conv_in, lam_in, lamc_in, gain_in,
                       ln_in, router_in, brouter_in, bmod_in, bmod1_in, const_in,
                       y_prompt, y_sample, new_na_k, new_na_v, new_da_k, new_da_v):
    plan, turns = psum_plan()
    mod_d = nc.dram_tensor("mod_rows", [2, 4, D], F32, kind="Internal").ap()
    h2_d = nc.dram_tensor("h2_rows", [T, D], F32, kind="Internal").ap()
    moe_d = nc.dram_tensor("moe_rows", [BLOCKS * P, D], F32, kind="Internal").ap()

    with ExitStack() as ctx:
        def sb(name, shape, dt=F32):
            return ctx.enter_context(nc.sbuf_tensor(name, shape, dt))

        def sem(name):
            return ctx.enter_context(nc.semaphore(name))

        big = sb("big", [P, RING * ITEM + 2 * TILES * D + 4608])
        ring = big[:, 0:RING * ITEM].rearrange("p (s n) -> p s n", s=RING)
        expert_w = big[:, 0:BUFS * EXPERT]
        tail = big[:, RING * ITEM:]
        x = sb("x", [P, TILES, D])
        act_a = tail[:, 0:TILES * D].rearrange("p (t d) -> p t d", t=TILES)
        act_b = tail[:, TILES * D:2 * TILES * D]
        attn = tail[:, 2 * TILES * D:]
        shared = sb("shared", [P, 7680])
        v_sb = sb("v_sb", [P, TILES, 768])
        cache = sb("cache", [P, 1536])
        bias = attn[:, 0:1536].rearrange("p (h s c) -> p h s c", h=NA_HEADS, s=6)
        probs = attn[:, 1536:3840].rearrange("p (b m k) -> p b m k", b=3, m=2)
        probT = attn[:, 3840:4608].rearrange("p (b k t) -> p b k t", b=2, k=3)
        mod2_b = attn[:, 0:4096].rearrange("p (c v d) -> p c v d", c=2, v=2)
        gate_b = sb("gate_b", [P, 2, D])
        ln_b = sb("ln_b", [P, 2, D])
        wide = sb("wide", [P, 1280])
        mrow = sb("mrow", [P, 4, 256])
        bmod1 = sb("bmod1", [P, DEPTH, 2, KC])
        modT = sb("modT", [P, 2, 2, KC])
        const = sb("const", [P, N_KEPT])
        constb = sb("constb", [P, 4 * P + 8], BF16)
        convp = sb("convp", [P, 2, 4])
        lamv = sb("lamv", [P, 4, 64])
        lamc = sb("lamc", [P, 2])
        lams = sb("lams", [P, 8])
        gain = sb("gain", [P, P])
        routw = sb("routw", [P, KC, E])
        broute = sb("broute", [P, E])
        condv = sb("condv", [P, 2, KC])
        conds = sb("conds", [P, 2, 2, KC])
        condT = sb("condT", [P, KC, 32])
        kout = cache[:, 0:768]
        head = sb("head", [P, 2 * T])
        osb = head[:, 0:T].rearrange("p (t d) -> p t d", t=TILES)
        on = head[:, T:2 * T].rearrange("p (t d) -> p t d", t=TILES)
        mrow1 = head[:, 0:512].rearrange("p (v n) -> p v n", v=2)
        sq = wide[:, 768:1152].rearrange("p (t d) -> p t d", t=TILES)
        st = sb("st", [P, 24])
        mxs = sb("mxs", [P, 3, 2])
        rsum = sb("rsum", [P, 3, 2])
        rinv = sb("rinv", [P, 3, 4])
        msr = sb("msr", [P, 4, TILES])
        stats = sb("stats", [P, 6, 2, 6])
        mv = sb("mv", [P, 6, 2])
        lnv = sb("lnv", [P, 6, 3])
        half = sb("half", [P, 4])
        rt = sb("rt", [P, 16, TILES * E])
        pair = wide[:, 0:1024].rearrange("p (b n) -> p b n", b=2)
        sel = v_sb[:, :, :].rearrange("p a b -> p (a b)").bitcast(BF16)[:, 0:2 * TILES * P]\
            .rearrange("p (c s) -> p c s", c=2 * TILES)
        where = sb("where", [P, 2 * TILES, 2, COLS], BF16)
        maskb = sb("maskb", [P, TILES * E], BF16)
        gidx = sb("gidx", [P, COLS], U32)
        gcol = sb("gcol", [P, 1], U32)
        ridx = sb("ridx", [P, 2, TILES], U32)
        tab = sb("tab", [P, 37])
        tabu = sb("tabu", [P, 37], U32)
        gates = sb("gates", [P, 2, TILES])
        psum = ctx.enter_context(nc.psum_tensor("psum", [P, 8, 512], F32))

        ident = const[:, C_ID:C_ID + P]
        swap = const[:, C_SWAP:C_SWAP + P]
        cos_t = const[:, C_COS:C_COS + LAT]
        sin_t = const[:, C_SIN:C_SIN + LAT]
        utri, ones, iota, tok = (constb[:, 0:P], constb[:, P:2 * P], constb[:, 2 * P:3 * P],
                                 constb[:, 3 * P:3 * P + 6])
        xn = act_a
        h2 = shared[:, 0:3072].rearrange("p (t d) -> p t d", t=TILES)
        mix = tail[:, 0:TILES * D].rearrange("p (c t) -> p c t", c=8)
        hT = act_b.rearrange("p (k t) -> p k t", k=KC)
        kT = shared[:, 0:3072].rearrange("p (c t) -> p c t", c=6)
        qT = shared[:, 3072:7680].rearrange("p (c t) -> p c t", c=12)
        xg = shared[:, 0:1024]
        xT = shared[:, 1024:2048]
        yo = shared[:, 2048:3072]
        hid = shared[:, 3072:3328]
        hidT = shared[:, 3328:3584]
        silu = shared[:, 3584:3840]
        fetched = [shared[:, 1024 * i:1024 * i + 1024] for i in range(6)]

        arrived = [sem(f"arrived{s}") for s in range(RING)]
        ring_free = sem("ring_free")
        full = {s: sem(f"full_{s}") for s in SLOT_BANK}
        free = {s: sem(f"free_{s}") for s in SLOT_BANK}
        dve_done, act_done, pool_done = sem("dve_done"), sem("act_done"), sem("pool_done")
        cond_in_s, const_in_s, x_in_s, layer_in_s = sem("cond_in"), sem("const_in"), sem("x_in"), sem("layer_in")
        bmod_in_s, layer_bias_in = sem("bmod_in"), sem("layer_bias_in")
        ln_in_s = sem("ln_in")
        cond_exp, cond_ready = sem("cond_exp"), sem("cond_ready")
        constb_ready = sem("constb_ready")
        lam_dot, lam_exp = sem("lam_dot"), sem("lam_exp")
        stats_ready, rstd_ready, xn_ready = sem("stats_ready"), sem("rstd_ready"), sem("xn_ready")
        pre_mv, pre_rstd, pre_xn = sem("pre_mv"), sem("pre_rstd"), sem("pre_xn")
        gained = sem("gained")
        mrow_ready, mod_stored = sem("mrow_ready"), sem("mod_stored")
        mod1_full, mod1_rows, mod1T_full, mod1_biased, mod1_ready = (
            sem(n) for n in ("mod1_full", "mod1_rows", "mod1T_full", "mod1_biased", "mod1_ready"))
        gate1_in, mod2_in, gate2_in = sem("gate1_in"), sem("mod2_in"), sem("gate2_in")
        hT_second = sem("hT_second")
        roped = sem("roped")
        kout_ready, state_out = sem("kout_ready"), sem("state_out")
        bias_ready = sem("bias_ready")
        max_ready, prob_ready, av_done = sem("max_ready"), sem("prob_ready"), sem("av_done")
        ms_ready, rms_ready, on_ready, mix_sc = sem("ms_ready"), sem("rms_ready"), sem("on_ready"), sem("mix_sc")
        h2_ready, h2_stored = sem("h2_ready"), sem("h2_stored")
        mask_ready, sel_ready, sidx_ready = sem("mask_ready"), sem("sel_ready"), sem("sidx_ready")
        table_ready = sem("table_ready")
        gates_ready, first_gated = sem("gates_ready"), sem("first_gated")
        pair_done = sem("pair_done")
        up_used = sem("up_used")
        up_in = [sem(f"up_in{q}") for q in range(BUFS)]
        down_in = [sem(f"down_in{q}") for q in range(BUFS)]
        xg_in, gcol_ready = sem("xg_in"), sem("gcol_ready")
        xT_full, xT_ready, up_full, up_exp, hid_ready, hidT_full, hidT_ready, down_full, yo_ready, yo_stored = (
            sem(n) for n in ("xT_full", "xT_ready", "up_full", "up_exp", "hid_ready", "hidT_full", "hidT_ready",
                             "down_full", "yo_ready", "yo_stored"))
        filled = sem("filled")
        silu_step = sem("silu_step")
        pick_in = [sem(f"pick_in{i}") for i in range(6)]
        x_out = sem("x_out")

        def bank(name, n=1):
            b = SLOT_BANK[plan[name][0]]
            return psum[:, b:b + n, :] if n > 1 else psum[:, b, :]

        def claim(eng, L, name):
            slot, turn = plan[name]
            eng.wait_ge(free[slot], L * turns[slot] + turn + 1)

        def produced(ins, name):
            ins.then_inc(full[plan[name][0]], 1)

        def await_product(eng, L, name):
            slot, turn = plan[name]
            eng.wait_ge(full[slot], L * turns[slot] + turn + 1)

        def read_out(ins, name):
            ins.then_inc(free[plan[name][0]], 1)

        def await_read(eng, L, name):
            slot, turn = plan[name]
            eng.wait_ge(free[slot], L * turns[slot] + turn + 2)

        def before_last(L):
            return L.with_bounds(min_val=0, max_val=DEPTH - 2)

        def chain(eng, done):
            at = [0]

            def restart():
                at[0] = 0
                eng.sem_clear(done)

            def link(ins):
                at[0] += 1
                ins.then_inc(done, 1)
                eng.wait_ge(done, at[0])
            return restart, link

        ps_mod1 = psum[:, 6, :].rearrange("p (v n) -> p v n", v=2)
        ps_mod1T = psum[:, 7, :].rearrange("p (v c r) -> p v c r", v=2, c=2)
        psA, psB, psC, psD = (psum[:, 0:2, :].rearrange("p a b -> p (a b)"), psum[:, 2, :],
                              psum[:, 4:6, :].rearrange("p a b -> p (a b)"), psum[:, 6, :])

        passed = {e: sem(f"passed_{e}") for e in ("sp", "pe", "act", "pool")}

        def stop_here(eng, name):
            eng.sem_inc(passed[name], 1)

        block = ctx.enter_context(nc.Block())

        @block.sync
        def _(sp):
            for s in range(RING):
                sp.dma_start(ring[:, s, :], walls[s]).then_inc(arrived[s], 16)
            with sp.Fori(0, DEPTH) as L:
                sp.wait_ge(pair_done, L * STAGES + 1)
                stop_here(sp, "sp")
                with sp.If(L > 0):
                    for s in pick_in:
                        sp.wait_ge(s, L * 16)
                    stop_here(sp, "sp")

                def fill(L, turn):
                    for s in range(RING):
                        sp.wait_ge(ring_free, L * ITEMS + turn * RING + (s + 1))
                        sp.dma_start(ring[:, s, :], walls[(L * ITEMS + RING) + turn * RING + s]).then_inc(arrived[s], 16)

                with sp.Fori(0, NEXT0 // RING) as turn:
                    fill(L, turn)
                with sp.If(L < DEPTH - 1):
                    fill(before_last(L), NEXT0 // RING)
                sp.wait_ge(table_ready, L + 1)
                stop_here(sp, "sp")
                active = sp.value_load(tabu[0:1, T_ACTIVE:T_ACTIVE + 1], min_val=1, max_val=E)
                first = sp.value_load(tabu[0:1, T_FIRST:T_FIRST + 1], min_val=1, max_val=BLOCKS * DEPTH + 1)
                for m in range(PAIRS):
                    buffers = [(2 * m + h) % BUFS for h in range(2)]
                    if m > 1:
                        sp.wait_ge(up_used, L * PAIRS + (m - 1))
                    stop_here(sp, "sp")
                    with sp.If(active > 2 * m):
                        who = [sp.value_load(tabu[0:1, T_WHO + 2 * m + h:T_WHO + 2 * m + h + 1], min_val=0, max_val=E - 1)
                               for h in range(2)]
                        for h, q in enumerate(buffers):
                            sp.dma_start(expert_w[:, q * EXPERT:q * EXPERT + UP], experts_in[L * E + who[h], :, 0:UP])\
                                .then_inc(up_in[q], 16)
                        if m == 0:
                            sp.wait_ge(xg_in, (first + L) * 16)
                        if m > 1:
                            sp.wait_ge(pair_done, L * STAGES + (m + 1))
                        for h, q in enumerate(buffers):
                            sp.dma_start(expert_w[:, q * EXPERT + UP:(q + 1) * EXPERT], experts_in[L * E + who[h], :, UP:EXPERT])\
                                .then_inc(down_in[q], 16)
                    with sp.Else():
                        if m > 1:
                            sp.wait_ge(pair_done, L * STAGES + (m + 1))
                        for q in buffers:
                            sp.sem_inc(up_in[q], 16)
                            sp.sem_inc(down_in[q], 16)

        @block.tensor
        def _(pe):
            def item(L, j):
                pe.wait_ge(arrived[j % RING], (L * (ITEMS // RING) + (j // RING + 2)) * 16)
                return ring[:, j % RING, :]

            def transposes(name, n, src):
                out = bank(name, 2).rearrange("p a b -> p (a b)") if n > 4 else bank(name)
                for k in range(n):
                    ins = pe.transpose(out[:, k * P:(k + 1) * P], src(k), ident)
                produced(ins, name)

            def mod_vector(L, v):
                w = [item(L, MODS0 + 4 * (v - 2) + g).rearrange("p (k n) -> p k n", k=KC) for g in range(4)]
                claim(pe, L, ("mod", v))
                four_groups(bank(("mod", v))[:, 0:256], w)
                pe.drain().then_inc(full[plan[("mod", v)][0]], 1)

            def four_groups(out, w):
                for k in range(KC):
                    for g in range(4):
                        ins = pe.matmul(out[32 * g:32 * g + 32, :], condT[:, k, :], w[g][:, k, :],
                                        start=(k == 0), stop=(k == KC - 1), skip_group_check=True)
                        if k == KC - 1:
                            ins.then_inc(ring_free, 1)

            def first_mods(items):
                for v in range(2):
                    four_groups(ps_mod1[:, v, :], [items(4 * v + g).rearrange("p (k n) -> p k n", k=KC) for g in range(4)])
                pe.drain().then_inc(mod1_full, 1)

            def first_mods_T(layer):
                pe.wait_ge(mod1_rows, layer + 1)
                for v in range(2):
                    for c in range(2):
                        ins = pe.transpose(ps_mod1T[:, v, c, :], mrow1[:, v, c * P:(c + 1) * P], ident)
                ins.then_inc(mod1T_full, 1)

            def first_item(j):
                pe.wait_ge(arrived[j], 16)
                return ring[:, j, :]

            def rope(L, c):
                await_read(pe, L, ("proj", c))
                claim(pe, L, ("rope", c))
                src = kT[:, c, :] if c < 4 else qT[:, c - 4, :]
                ins = pe.matmul(bank(("rope", c))[:, 0:LAT], swap, src[:, P:P + LAT], start=True, stop=True)
                produced(ins, ("rope", c))

            def score(L, i):
                kind, h, t = STEPS[i]
                claim(pe, L, ("score", i))
                if i == 0:
                    pe.wait_ge(roped, L * 8 + 8)
                    await_read(pe, L, "cacheT")
                keys = slice(0, P) if t == 0 else slice(P, P + 384)
                nk = P if t == 0 else 384
                if kind == "da":
                    for m in range(2):
                        r = slice(DH * m, DH * m + DH)
                        ins = pe.matmul(bank(("score", i), 2)[:, m, 0:nk], qT[r, QCH["daq"] + h, t * P:(t + 1) * P],
                                        kT[r, KCH["dak"] + h, keys], start=True, stop=True)
                else:
                    r = slice(DH * (h % 2), DH * (h % 2) + DH)
                    ins = pe.matmul(bank(("score", i))[:, 0:nk], qT[r, QCH["naq"] + h // 2, t * P:(t + 1) * P],
                                    kT[r, KCH["nak"] + h // 2, keys], start=True, stop=True)
                produced(ins, ("score", i))

            def values(kind, h, t, kc):
                w, col = (P, P * h) if kind == "da" else (DH, 512 + DH * h)
                if t == 0:
                    return v_sb[:, 0, col:col + w]
                if kc < 2:
                    return v_sb[:, 1 + kc, col:col + w]
                return cache[:, 768 + col:768 + col + w]

            def prob_transposes(L, i):
                kind, h, t = STEPS[i]
                pe.wait_ge(prob_ready, L * N_STEPS + i + 1)
                claim(pe, L, ("probT", i))
                transposes(("probT", i), 1 if t == 0 else 3, lambda k: probs[:, i % 3, 0, k * P:(k + 1) * P])

            def attend(L, i):
                kind, h, t = STEPS[i]
                name = ("out", kind, h)
                if i == 0:
                    for n in (24, 25, 26):
                        await_read(pe, L, ("proj", n))
                if t == 0:
                    claim(pe, L, name)
                await_read(pe, L, ("probT", i))
                n = 1 if t == 0 else 3
                for kc in range(n):
                    v = values(kind, h, t, kc)
                    p = probT[:, i % 2, kc, :]
                    if kind == "da":
                        ins = pe.matmul(bank(name)[:, t * P:(t + 1) * P], p, v, start=(kc == 0), stop=(kc == n - 1),
                                        skip_group_check=True)
                    else:
                        r = slice(DH * (h % 2), DH * (h % 2) + DH)
                        ins = pe.matmul(bank(name)[r, t * P:(t + 1) * P], v, p, start=(kc == 0), stop=(kc == n - 1),
                                        skip_group_check=True)
                ins.then_inc(av_done, 1)
                if t == 2:
                    pe.drain().then_inc(full[plan[name][0]], 1)

            def out_proj(L, t):
                name = ("y", t)
                if t == 0:
                    for h in range(DA_HEADS):
                        await_read(pe, L, ("mixT", h))
                        await_read(pe, L, ("out", "na", h))
                    pe.wait_ge(mix_sc, 2 * L + 2)
                claim(pe, L, name)
                y = bank(name, 2).rearrange("p a b -> p (a b)")
                for n in range(4):
                    w = item(L, W_OUT0 + n).rearrange("p (k n) -> p k n", k=KC)
                    for k in range(KC):
                        ins = pe.matmul(y[:, 256 * n:256 * n + 256], mix[:, k, t * P:(t + 1) * P], w[:, k, :],
                                        start=(k == 0), stop=(k == KC - 1), skip_group_check=True)
                    if t == 2:
                        ins.then_inc(ring_free, 1)
                if t == 2:
                    pe.drain().then_inc(full[plan[name][0]], 1)
                else:
                    produced(ins, name)

            def router_T(L, t):
                pe.wait_ge(h2_ready, 3 * L + t + 1)
                claim(pe, L, ("h2T", t))
                transposes(("h2T", t), KC, lambda k: h2[:, t, :].rearrange("p (a k) -> p a k", k=KC)[:, :, k])

            def router(L, t):
                await_read(pe, L, ("h2T", t))
                claim(pe, L, ("logit", t))
                for k in range(KC):
                    ins = pe.matmul(bank(("logit", t))[:, 0:E], hT[:, k, t * P:(t + 1) * P], routw[:, k, :],
                                    start=(k == 0), stop=(k == KC - 1))
                produced(ins, ("logit", t))

            def tokens_T(L, i):
                pe.wait_ge(xg_in, (i + L) * 16)
                pe.wait_ge(xT_ready, i + L)
                for k in range(KC):
                    ins = pe.transpose(psA[:, k * P:(k + 1) * P],
                                       xg.rearrange("p (a k) -> p a k", k=KC)[:, :, k], ident)
                ins.then_inc(xT_full, 1)

            def up(L, i, w):
                pe.wait_ge(xT_ready, i + L + 1)
                pe.wait_ge(hid_ready, i)
                for k in range(KC):
                    for h in range(2):
                        ins = pe.matmul(psD[HALF * h:HALF * h + HALF, :],
                                        xT[:, k * P + HALF * h:k * P + HALF * h + HALF],
                                        w[h][:, 2 * DE * k:2 * DE * k + 2 * DE],
                                        start=(k == 0), stop=(k == KC - 1), skip_group_check=True)
                ins.then_inc(up_full, 1)

            def hidden_T(i):
                pe.wait_ge(hid_ready, i + 1)
                for k in range(2):
                    ins = pe.transpose(psB[:, k * P:(k + 1) * P], hid[:, k * P:(k + 1) * P], ident)
                ins.then_inc(hidT_full, 1)

            def down(after, w, n):
                pe.wait_ge(hidT_ready, after)
                pe.wait_ge(yo_ready, after)
                for k in range(2):
                    for h in range(2):
                        ins = pe.matmul(psC[HALF * h:HALF * h + HALF, 512 * n:512 * n + 512],
                                        hidT[:, k * P + HALF * h:k * P + HALF * h + HALF],
                                        w[h][:, UP + D * k + 512 * n:UP + D * k + 512 * n + 512],
                                        start=(k == 0), stop=(k == 1), skip_group_check=True)
                if n == 1:
                    ins.then_inc(down_full, 1)

            def buffers(odd):
                return [expert_w[:, q * EXPERT:(q + 1) * EXPERT] for q in (2 * odd, 2 * odd + 1)]

            def stage(L, two, odd):
                w, last_w = buffers(odd), buffers(1 - odd)
                load = lambda at, low, high: pe.value_load(tabu[0:1, bass.ds(two * 2 + (at + odd), 1)], min_val=low, max_val=high)
                start = load(T_START, 1, BLOCKS * DEPTH + 1)
                blocks = load(T_BLOCKS, 0, T // HALF)
                before = load(T_BLOCKS - 1, 0, T // HALF)
                for h in range(2):
                    pe.wait_ge(up_in[2 * odd + h], (L * (E // BUFS) + two + 1) * 16)
                with pe.If(blocks > 0):
                    up(L, start, w)
                with pe.If(blocks < 2):
                    pe.drain().then_inc(up_used, 1)
                with pe.If(before > 0):
                    for h in range(2):
                        pe.wait_ge(down_in[2 * (1 - odd) + h], (L * (E // BUFS) + two + odd) * 16)
                    for n in range(2):
                        down(start, last_w, n)
                pe.drain().then_inc(pair_done, 1)
                with pe.If(blocks > 0):
                    tokens_T(L, start + 1)
                    hidden_T(start)
                    with pe.If(blocks > 1):
                        for h in range(2):
                            pe.wait_ge(down_in[2 * odd + h], (L * (E // BUFS) + two + 1) * 16)
                        stop_here(pe, "pe")
                        with pe.Fori(1, blocks) as j:
                            up(L, start + j, w)
                            down(start + j, w, 0)
                            tokens_T(L, start + j + 1)
                            down(start + j, w, 1)
                            hidden_T(start + j)
                        pe.drain().then_inc(up_used, 1)

            for s in SLOT_BANK:
                pe.sem_inc(free[s], 1)
            for s in (pair_done, xT_full, up_full, hidT_full, down_full):
                pe.sem_inc(s, 1)
            pe.wait_ge(cond_ready, 2)
            first_mods(first_item)
            pe.wait_ge(const_in_s, 80)
            first_mods_T(0)
            pe.wait_ge(constb_ready, 4)
            with pe.Fori(0, DEPTH) as L:
                for t in range(TILES):
                    pe.wait_ge(pre_xn, 3 * L + t + 1)
                    claim(pe, L, ("hT", t))
                    transposes(("hT", t), KC, lambda k: xn[:, t, :].rearrange("p (a k) -> p a k", k=KC)[:, :, k])
                for t in range(TILES):
                    await_read(pe, L, ("hT", t))
                proj = 0
                for n, (piece, half_n) in enumerate(PIECES):
                    w = item(L, W_IN0 + n).rearrange("p (k n) -> p k n", k=KC)
                    jobs = TILES if piece in V_COL else 2
                    for j in range(jobs):
                        name = ("proj", proj)
                        claim(pe, L, name)
                        for k in range(KC):
                            if piece in V_COL:
                                ins = pe.matmul(bank(name)[:, 0:256], hT[:, k, j * P:(j + 1) * P], w[:, k, :],
                                                start=(k == 0), stop=(k == KC - 1))
                            else:
                                ins = pe.matmul(bank(name)[:, 0:T], w[:, k, j * P:(j + 1) * P], hT[:, k, :],
                                                start=(k == 0), stop=(k == KC - 1))
                        if j == jobs - 1:
                            ins.then_inc(ring_free, 1)
                            pe.drain().then_inc(full[plan[name][0]], 1)
                        else:
                            produced(ins, name)
                        proj += 1
                        if piece in ("dak", "daq"):
                            if proj >= 2:
                                rope(L, proj - 2)
                        elif proj == 9:
                            rope(L, 7)
                pe.wait_ge(layer_in_s, (L + 1) * 16 * 5)
                claim(pe, L, "cacheT")
                transposes("cacheT", 6, lambda c: cache[:, c * P:(c + 1) * P])
                for n in (9, 10, 11):
                    await_read(pe, L, ("proj", n))
                claim(pe, L, "kout")
                transposes("kout", 6, lambda c: kT[:, c, 0:P])
                score(L, 0)
                score(L, 1)
                mixes = 0
                for i, (kind, h, t) in enumerate(STEPS):
                    if i + 2 < N_STEPS:
                        score(L, i + 2)
                    prob_transposes(L, i)
                    if i > 0:
                        attend(L, i - 1)
                        if STEPS[i - 1][0] == "da" and STEPS[i - 1][2] == 2:
                            mod_vector(L, 2 + STEPS[i - 1][1])
                    if mixes < DA_HEADS and i == 3 * mixes + 2 + MIX_DELAY:
                        pe.wait_ge(on_ready, 4 * L + mixes + 1)
                        claim(pe, L, ("mixT", mixes))
                        transposes(("mixT", mixes), 3, lambda k: on[:, k, :])
                        mixes += 1
                attend(L, N_STEPS - 1)
                for t in range(TILES):
                    out_proj(L, t)
                with pe.If(L < DEPTH - 1):
                    claim(pe, L, ("logit", 0))
                    first_mods(lambda j: item(L, NEXT0 + j))
                router_T(L, 0)
                router_T(L, 1)
                with pe.If(L < DEPTH - 1):
                    claim(pe, L, ("logit", 1))
                    first_mods_T(L + 1)
                router(L, 0)
                router_T(L, 2)
                with pe.If(L < DEPTH - 1):
                    pe.wait_ge(mod1_ready, L + 2)
                    stop_here(pe, "pe")
                router(L, 1)
                router(L, 2)
                pe.wait_ge(mask_ready, L + 1)
                claim(pe, L, "place")
                place = bank("place")
                for t in range(TILES):
                    for s in range(t + 1):
                        pe.matmul(place[:, t * E:(t + 1) * E], ones if s < t else utri, maskb[:, s * E:(s + 1) * E],
                                  start=(s == 0), stop=(s == t), skip_group_check=True)
                for t in range(TILES):
                    ins = pe.matmul(place[:, TILES * E:TILES * E + E], ones, maskb[:, t * E:(t + 1) * E],
                                    start=(t == 0), stop=(t == TILES - 1), skip_group_check=True)
                produced(ins, "place")
                pe.wait_ge(sel_ready, L + 1)
                claim(pe, L, "index")
                for n in range(2 * TILES):
                    ins = pe.matmul(bank("index")[:, 0:2 * COLS], sel[:, n, :],
                                    where[:, n, :, :].rearrange("p a b -> p (a b)"),
                                    start=(n == 0), stop=(n == 2 * TILES - 1))
                produced(ins, "index")
                pe.wait_ge(table_ready, L + 1)
                stop_here(pe, "pe")
                first = pe.value_load(tabu[0:1, T_FIRST:T_FIRST + 1], min_val=1, max_val=BLOCKS * DEPTH + 1)
                tokens_T(L, first)
                with pe.Fori(0, PAIRS // 2) as two:
                    for odd in range(2):
                        stage(L, two, odd)
                end = pe.value_load(tabu[0:1, T_LAST:T_LAST + 1], min_val=2, max_val=BLOCKS * DEPTH + 1)
                before = pe.value_load(tabu[0:1, T_BLOCKS + PAIRS - 1:T_BLOCKS + PAIRS], min_val=0, max_val=T // HALF)
                with pe.If(before > 0):
                    for h in range(2):
                        pe.wait_ge(down_in[2 + h], (L + 1) * (E // BUFS) * 16)
                    for n in range(2):
                        down(end, buffers(1), n)
                pe.drain().then_inc(pair_done, 1)

        @block.scalar
        def _(act):
            restart, link = chain(act, act_done)
            copy = ACT.Copy

            def pre_normalise(layer, t):
                act.wait_ge(pre_rstd, 3 * layer + t + 1)
                act.activation(xn[:, t, :], x[:, t, :], ACT.Identity, scale=lnv[:, 3 + t, 1:2],
                               bias=lnv[:, 3 + t, 2:3]).then_inc(pre_xn, 1)

            def normalise(L, n, src, dst):
                act.wait_ge(rstd_ready, 9 * L + n - 2)
                act.activation(dst, src, ACT.Identity, scale=lnv[:, n % 3, 1:2],
                               bias=lnv[:, n % 3, 2:3]).then_inc(xn_ready, 1)

            act.dma_start(condv[:, :, :], cond_in).then_inc(cond_in_s, 16)
            for t in range(TILES):
                act.dma_start(x[:, t, :], x_in[t]).then_inc(x_in_s, 16)
            act.dma_start(bmod1[:, :, :, :], bmod1_in).then_inc(const_in_s, 16)
            act.dma_start(const[:, :], const_in[:, 0:N_KEPT]).then_inc(const_in_s, 16)
            act.dma_start(wide[:, 0:2 * P], const_in[:, N_KEPT:N_CONST]).then_inc(const_in_s, 16)
            act.dma_start(routw[:, :, :], router_in).then_inc(const_in_s, 16)
            act.dma_start(broute[:, :], brouter_in.partition_broadcast(P)).then_inc(const_in_s, 16)
            act.wait_ge(cond_in_s, 16)
            act.activation(conds[:, 0, :, :], condv[:, :, :], ACT.Exp, scale=-1.0).then_inc(cond_exp, 1)
            for s in (xT_ready, up_exp, hidT_ready):
                act.sem_inc(s, 1)
            act.sem_inc(yo_ready, 2)
            act.sem_inc(yo_stored, 32)
            act.sem_inc(state_out, 16)
            for t in range(TILES):
                pre_normalise(0, t)
            with act.Fori(0, DEPTH) as L:
                restart()
                act.wait_ge(mod1_ready, L + 1)
                for t in range(TILES):
                    name = ("hT", t)
                    await_product(act, L, name)
                    c = min(t, 1)
                    for k in range(KC // 2, KC):
                        ins = act.activation(hT[:, k, t * P:(t + 1) * P],
                                             bank(name, 2).rearrange("p a b -> p (a b)")[:, k * P:(k + 1) * P],
                                             ACT.Identity, scale=modT[:, c, 1, k:k + 1], bias=modT[:, c, 0, k:k + 1])
                    ins.then_inc(hT_second, 1)
                proj = 0
                for piece, half_n in PIECES:
                    for j in range(TILES if piece in V_COL else 2):
                        name = ("proj", proj)
                        await_product(act, L, name)
                        if piece in V_COL:
                            col = V_COL[piece] + 256 * half_n
                            ins = act.activation(v_sb[:, j, col:col + 256], bank(name)[:, 0:256], copy)
                        elif piece in KCH:
                            ins = act.activation(kT[:, KCH[piece] + 2 * half_n + j, 0:T], bank(name)[:, 0:T], copy)
                        else:
                            ins = act.activation(qT[:, QCH[piece] + 2 * half_n + j, :], bank(name)[:, 0:T], copy,
                                                 scale=SCALE if piece in ("daq", "naq") else 1.0)
                        read_out(ins, name)
                        proj += 1
                act.wait_ge(lam_dot, 2 * L + 2)
                act.activation(lams[:, 2:4], lams[:, 0:2], ACT.Exp).then_inc(lam_exp, 1)
                await_product(act, L, "cacheT")
                read_out(act.activation(kT[:, :, 384:512], bank("cacheT", 2).rearrange("p a b -> p (a b)")[:, 0:768]
                                        .rearrange("p (c t) -> p c t", c=6), copy), "cacheT")
                await_product(act, L, "kout")
                read_out(act.activation(kout[:, :], bank("kout", 2).rearrange("p a b -> p (a b)")[:, 0:768], copy), "kout")
                await_read(act, L, "kout")
                act.dma_start(new_da_k[L], kout[:, 0:512]).then_inc(state_out, 16)
                act.dma_start(new_na_k[L], kout[:, 512:768]).then_inc(state_out, 16)
                act.dma_start(new_da_v[L], v_sb[:, 0, 0:512]).then_inc(state_out, 16)
                act.dma_start(new_na_v[L], v_sb[:, 0, 512:768]).then_inc(state_out, 16)

                def exps(i):
                    kind, h, t = STEPS[i]
                    nk = P if t == 0 else 384
                    act.wait_ge(max_ready, N_STEPS * L + i + 1)
                    if i >= 3:
                        await_product(act, L, ("probT", i - 3))
                    n = 2 if kind == "da" else 1
                    for m in range(n):
                        src = bank(("score", i), 2)[:, m, 0:nk]
                        ins = act.activation(probs[:, i % 3, m, 0:nk], src, ACT.Exp, bias=mxs[:, i % 3, m:m + 1],
                                             accum_out=rsum[:, i % 3, m:m + 1])
                    read_out(ins, ("score", i))

                def probT_out(i):
                    kind, h, t = STEPS[i]
                    n = 1 if t == 0 else 3
                    name = ("probT", i)
                    await_product(act, L, name)
                    if i >= 2:
                        act.wait_ge(av_done, N_STEPS * L + i - 1)
                    read_out(act.activation(probT[:, i % 2, 0:n, :],
                                            bank(name)[:, 0:n * P].rearrange("p (k t) -> p k t", k=n), copy), name)

                def head_out(i):
                    kind, h, t = STEPS[i]
                    name = ("out", kind, h)
                    await_product(act, L, name)
                    if kind == "da":
                        if h:
                            act.wait_ge(on_ready, 4 * L + h)
                        read_out(act.activation(osb[:, :, :], bank(name)[:, 0:T].rearrange("p (t d) -> p t d", t=TILES),
                                                copy), name)
                        await_read(act, L, name)
                        for u in range(TILES):
                            ins = act.activation(sq[:, u, :], osb[:, u, :], ACT.Square, accum_out=msr[:, 0, u:u + 1])
                        ins.then_inc(ms_ready, 1)
                    else:
                        r = slice(DH * (h % 2), DH * (h % 2) + DH)
                        read_out(act.activation(mix[r, h // 2, :], bank(name)[r, 0:T], copy), name)

                def mod_store(h):
                    act.wait_ge(mrow_ready, 4 * L + h + 1)
                    for c in range(2):
                        act.dma_start(mod_d[c, h, :].rearrange("(g n) -> g n", g=4),
                                      mrow[c:c + 97:32, h, :]).then_inc(mod_stored, 16)

                exps(0)
                mixes = 0
                for i in range(N_STEPS):
                    if i + 1 < N_STEPS:
                        exps(i + 1)
                    probT_out(i)
                    if i % 3 == 0 and i > 0:
                        head_out(i - 1)
                    if i % 3 == 1 and i // 3 in range(1, DA_HEADS + 1):
                        mod_store(i // 3 - 1)
                    if mixes < DA_HEADS and i == 3 * mixes + 2 + MIX_DELAY:
                        name = ("mixT", mixes)
                        await_product(act, L, name)
                        read_out(act.activation(mix[:, 4 + mixes, :], bank(name)[:, 0:T], copy), name)
                        mixes += 1
                head_out(N_STEPS - 1)

                def h2T_out(t):
                    name = ("h2T", t)
                    await_product(act, L, name)
                    read_out(act.activation(hT[:, :, t * P:(t + 1) * P],
                                            bank(name, 2).rearrange("p a (b q) -> p (a b) q", q=P), copy), name)
                    act.wait_ge(h2_ready, 3 * L + t + 1)
                    act.dma_start(h2_d[t * P:(t + 1) * P, :], h2[:, t, :]).then_inc(h2_stored, 16)

                def logit_exps(t):
                    name = ("logit", t)
                    await_product(act, L, name)
                    read_out(act.activation(rt[:, 0, t * E:(t + 1) * E], bank(name)[:, 0:E], ACT.Exp, scale=-1.0), name)

                def post_norm(t):
                    normalise(L, 3 + 2 * t, x[:, t, :], x[:, t, :])

                def pre_norm(t):
                    normalise(L, 4 + 2 * t, x[:, t, :], h2[:, t, :])

                post_norm(0)
                pre_norm(0)
                post_norm(1)
                pre_norm(1)
                post_norm(2)
                h2T_out(0)
                h2T_out(1)
                pre_norm(2)
                logit_exps(0)
                h2T_out(2)
                logit_exps(1)
                logit_exps(2)

                act.wait_ge(table_ready, L + 1)
                stop_here(act, "act")
                first = act.value_load(tabu[0:1, T_FIRST:T_FIRST + 1], min_val=1, max_val=BLOCKS * DEPTH + 1)
                count = act.value_load(tabu[0:1, T_COUNT:T_COUNT + 1], min_val=1, max_val=BLOCKS)

                def tokens_out(i):
                    act.wait_ge(xT_full, i + L + 1)
                    act.wait_ge(up_full, i)
                    act.activation(xT, psA, copy).then_inc(xT_ready, 1)

                def up_exps(i):
                    act.wait_ge(up_full, i + 1)
                    act.wait_ge(hid_ready, i)
                    act.activation(silu, psD[:, 0:DE], ACT.Exp, scale=-1.0).then_inc(up_exp, 1)

                def hidden_out(i):
                    act.wait_ge(hidT_full, i + 1)
                    act.wait_ge(down_full, i)
                    act.activation(hidT, psB[:, 0:DE], copy).then_inc(hidT_ready, 1)

                def block_out(after, j):
                    act.wait_ge(down_full, after)
                    act.wait_ge(yo_stored, after * 16)
                    act.activation(yo, psC, copy).then_inc(yo_ready, 1)
                    act.wait_ge(yo_ready, after + 1)
                    act.dma_start(moe_d[bass.ds(j * P, P), :], yo).then_inc(yo_stored, 16)

                tokens_out(first)
                up_exps(first)
                tokens_out(first + 1)
                hidden_out(first)
                with act.If(count > 1):
                    with act.Fori(1, count) as j:
                        up_exps(first + j)
                        tokens_out(first + j + 1)
                        block_out(first + j, j - 1)
                        hidden_out(first + j)
                block_out(first + count, count - 1)
                act.wait_ge(gates_ready, L + 1)
                for t in range(TILES):
                    act.wait_ge(pick_in[2 * t], 16 * (L + 1))
                    act.activation(fetched[2 * t], fetched[2 * t], copy, scale=gates[:, 0, t:t + 1]).then_inc(first_gated, 1)
                normalise(L, 9, x[:, 0, :], x[:, 0, :])
                normalise(L, 10, x[:, 1, :], x[:, 1, :])
                normalise(L, 11, x[:, 2, :], x[:, 2, :])
                with act.If(L < DEPTH - 1):
                    for t in range(TILES):
                        pre_normalise(L + 1, t)
            for t in range(TILES):
                act.wait_ge(gained, 6 * (DEPTH - 1) + 3 + t + 2)
                act.dma_start(y_prompt if t == 0 else y_sample[(t - 1) * P:t * P, :], x[:, t, :]).then_inc(x_out, 16)
            act.wait_ge(x_out, 48)
            act.wait_ge(state_out, 64 * DEPTH + 16)

        @block.vector
        def _(dve):
            restart, link = chain(dve, dve_done)
            tt, ts, stt = dve.tensor_tensor, dve.tensor_scalar, dve.scalar_tensor_tensor

            def norm_stats(L, n, src):
                for half_n in range(2):
                    ins = dve.bn_stats(stats[:, n % 3, half_n, :], src[:, 512 * half_n:512 * half_n + 512])
                    link(ins)
                dve.bn_aggr(mv[:, n % 3, :], stats[:, n % 3, :, :].rearrange("p a b -> p (a b)")).then_inc(stats_ready, 1)

            def pre_stats(t):
                for half_n in range(2):
                    ins = dve.bn_stats(stats[:, 3 + t, half_n, :], x[:, t, 512 * half_n:512 * half_n + 512])
                    link(ins)
                dve.bn_aggr(mv[:, 3 + t, :], stats[:, 3 + t, :, :].rearrange("p a b -> p (a b)")).then_inc(pre_mv, 1)

            def mod_out(L, v):
                name = ("mod", v)
                if v == 2:
                    dve.wait_ge(bmod_in_s, 64 * (L + 1))
                await_product(dve, L, name)
                link(tt(mrow[:, v - 2, :], bank(name)[:, 0:256], mrow[:, v - 2, :], ALU.add))
                dve.sem_inc(free[plan[name][0]], 1)
                dve.sem_inc(mrow_ready, 1)

            link(dve.memset(tab[:, :], 1.0))
            link(dve.memset(tab[:, T_NONE:T_NONE + 1], 0.0))
            dve.sem_inc(hid_ready, 1)
            dve.sem_inc(gained, 1)
            dve.sem_inc(silu_step, 3)
            link(dve.memset(condT[:, :, :], 0.0))
            link(dve.memset(half[:, 0:3], -0.5))
            dve.memset(half[:, 3:4], EPS).then_inc(cond_ready, 1)
            dve.wait_ge(cond_in_s, 16)
            dve.wait_ge(cond_exp, 1)
            link(ts(conds[:, 1, :, :], conds[:, 0, :, :], 1.0, None, ALU.add))
            link(dve.reciprocal(conds[:, 0, :, :], conds[:, 1, :, :]))
            tt(condT[:, :, 0:2], condv[:, :, :].rearrange("p c k -> p k c"),
               conds[:, 0, :, :].rearrange("p c k -> p k c"), ALU.mult).then_inc(cond_ready, 1)
            dve.wait_ge(x_in_s, 48)
            for t in range(TILES):
                pre_stats(t)
            dve.wait_ge(const_in_s, 80)
            dve.tensor_copy(constb[:, 0:P], wide[:, 0:P]).then_inc(constb_ready, 1)
            dve.memset(constb[:, P:2 * P], 1.0).then_inc(constb_ready, 1)
            dve.tensor_copy(constb[:, 2 * P:3 * P], wide[:, P:2 * P]).then_inc(constb_ready, 1)
            dve.tensor_copy(constb[:, 3 * P:3 * P + 6], const[:, C_TOK:C_TOK + 6]).then_inc(constb_ready, 1)
            dve.wait_ge(constb_ready, 4)

            def first_mods_rows(layer):
                dve.wait_ge(mod1_full, layer + 1)
                dve.tensor_copy(mrow1[:, :, :], ps_mod1).then_inc(mod1_rows, 1)

            def first_mods_out(layer, b):
                dve.wait_ge(mod1T_full, layer + 1)
                for c in range(2):
                    for v in range(2):
                        ins = tt(modT[:, c, v, :].rearrange("p (g h) -> p g h", h=2),
                                 ps_mod1T[:, v, :, c::32].rearrange("p h g -> p g h"),
                                 b[:, v, :].rearrange("p (g h) -> p g h", h=2), ALU.add)
                ins.then_inc(mod1_biased, 1)
                dve.wait_ge(mod1_biased, layer + 1)
                ts(modT[:, :, 1, :], modT[:, :, 1, :], 1.0, None, ALU.add).then_inc(mod1_ready, 1)

            first_mods_rows(0)
            first_mods_out(0, bmod1[:, 0, :, :])

            with dve.Fori(0, DEPTH) as L:
                restart()
                dve.wait_ge(mod1_ready, L + 1)
                for t in range(TILES):
                    name = ("hT", t)
                    await_product(dve, L, name)
                    c = min(t, 1)
                    for k in range(KC // 2):
                        ins = ts(hT[:, k, t * P:(t + 1) * P], bank(name, 2).rearrange("p a b -> p (a b)")[:, k * P:(k + 1) * P],
                                 modT[:, c, 1, k:k + 1], modT[:, c, 0, k:k + 1], ALU.mult, ALU.add)
                    link(ins)
                    dve.wait_ge(hT_second, 3 * L + t + 1)
                    dve.sem_inc(free[plan[name][0]], 1)
                dve.wait_ge(layer_in_s, (L + 1) * 16 * 5)
                link(tt(wide[:, 0:128].rearrange("p (a b) -> p a b", a=2), lamv[:, 0:3:2, :], lamv[:, 1:4:2, :], ALU.mult))
                for a in range(2):
                    dve.tensor_reduce(lams[:, a:a + 1], wide[:, 64 * a:64 * a + 64], AX.X, ALU.add).then_inc(lam_dot, 1)
                dve.wait_ge(lam_dot, 2 * L + 2)
                for c in range(8):
                    name = ("rope", c)
                    await_product(dve, L, name)
                    src = (kT[:, c, :] if c < 4 else qT[:, c - 4, :])[:, P:P + LAT]
                    ins = tt(wide[:, 0:LAT], bank(name)[:, 0:LAT], sin_t, ALU.mult)
                    read_out(ins, name)
                    link(tt(src, src, cos_t, ALU.mult))
                    tt(src, src, wide[:, 0:LAT], ALU.add).then_inc(roped, 1)
                    dve.wait_ge(roped, 8 * L + c + 1)
                dve.wait_ge(lam_exp, L + 1)
                link(tt(lams[:, 4:5], lams[:, 2:3], lams[:, 3:4], ALU.subtract))
                link(tt(lams[:, 5:6], lams[:, 4:5], lamc[:, 0:1], ALU.add))
                link(ts(gain[:, :], gain[:, :], lamc[:, 1:2], None, ALU.mult))

                def row_max(i):
                    kind, h, t = STEPS[i]
                    nk = P if t == 0 else 384
                    name = ("score", i)
                    await_product(dve, L, name)
                    if kind == "da":
                        ins = dve.tensor_reduce(mxs[:, i % 3, :], bank(name, 2)[:, :, 0:nk], AX.X, ALU.max, negate=True)
                    else:
                        if t > 0:
                            if h == 0 and t == 1:
                                dve.wait_ge(bias_ready, L + 1)
                            s0 = 2 - 2 * (t - 1)
                            link(tt(bank(name)[:, 0:LAT], bank(name)[:, 0:LAT],
                                    bias[:, h, s0:s0 + 4, :].rearrange("p a b -> p (a b)"), ALU.add))
                        ins = dve.tensor_reduce(mxs[:, i % 3, 0:1], bank(name)[:, 0:nk], AX.X, ALU.max, negate=True)
                    ins.then_inc(max_ready, 1)

                def probabilities(i):
                    kind, h, t = STEPS[i]
                    nk = P if t == 0 else 384
                    await_read(dve, L, ("score", i))
                    p = probs[:, i % 3, :, 0:nk]
                    r = rinv[:, i % 3, :]
                    if kind == "da":
                        link(dve.reciprocal(r[:, 0:2], rsum[:, i % 3, :]))
                        link(tt(r[:, 2:3], r[:, 1:2], lams[:, 5:6], ALU.mult))
                        link(ts(p[:, 1, :], p[:, 1, :], r[:, 2:3], None, ALU.mult))
                        stt(p[:, 0, :], p[:, 0, :], r[:, 0:1], p[:, 1, :], ALU.mult, ALU.subtract).then_inc(prob_ready, 1)
                    else:
                        link(dve.reciprocal(r[:, 0:1], rsum[:, i % 3, 0:1]))
                        ts(p[:, 0, :], p[:, 0, :], r[:, 0:1], None, ALU.mult).then_inc(prob_ready, 1)

                def head_scale(h):
                    dve.wait_ge(rms_ready, 4 * L + h + 1)
                    if h:
                        await_product(dve, L, ("mixT", h - 1))
                    for t in range(TILES):
                        ins = stt(on[:, t, :], osb[:, t, :], msr[:, 2, t:t + 1], gain[:, :], ALU.mult, ALU.mult)
                    link(ins)
                    dve.sem_inc(on_ready, 1)

                def conv(c):
                    z, o = wide[:, 0:T], wide[:, T:2 * T]
                    link(tt(z, qT[:, QCH["scc"] + c, :], qT[:, QCH["scx"] + c, :], ALU.mult))
                    link(ts(o, z, convp[:, c, 1:2], convp[:, c, 3:4], ALU.mult, ALU.add))
                    for a, b in ((0, P), (P, T)):
                        link(stt(o[:, a + 1:b], z[:, a:b - 1], convp[:, c, 0:1], o[:, a + 1:b], ALU.mult, ALU.add))
                        link(stt(o[:, a:b - 1], z[:, a + 1:b], convp[:, c, 2:3], o[:, a:b - 1], ALU.mult, ALU.add))
                    link(tt(mix[:, 2 + c, :], o, qT[:, QCH["scb"] + c, :], ALU.mult))
                    dve.sem_inc(mix_sc, 1)

                row_max(0)
                row_max(1)
                for i in range(N_STEPS):
                    probabilities(i)
                    if i % 3 == 1 and i // 3 in range(1, DA_HEADS + 1):
                        mod_out(L, 2 + i // 3 - 1)
                    if i + 2 < N_STEPS:
                        row_max(i + 2)
                    if i in (3, 6):
                        conv(i // 3 - 1)
                    if i % 3 == 2 and i // 3 in range(1, DA_HEADS + 1):
                        head_scale(i // 3 - 1)

                def residual(t, tmp):
                    ins = stt(x[:, t, :], x[:, t, :], ALPHA, tmp, ALU.mult, ALU.add)
                    link(ins)

                dve.wait_ge(gate1_in, 16 * (L + 1))

                def gain_bias(t):
                    link(tt(x[:, t, :], x[:, t, :], ln_b[:, 0, :], ALU.mult))
                    link(tt(x[:, t, :], x[:, t, :], ln_b[:, 1, :], ALU.add))
                    dve.sem_inc(gained, 1)

                def first_residual(t):
                    name = ("y", t)
                    await_product(dve, L, name)
                    ins = tt(wide[:, 0:D], bank(name, 2).rearrange("p a b -> p (a b)"), gate_b[:, min(t, 1), :], ALU.mult)
                    read_out(ins, name)
                    await_read(dve, L, name)
                    residual(t, wide[:, 0:D])
                    norm_stats(L, 3 + 2 * t, x[:, t, :])

                def first_gain(t):
                    dve.wait_ge(xn_ready, 9 * L + 1 + 2 * t)
                    gain_bias(t)
                    norm_stats(L, 4 + 2 * t, x[:, t, :])

                def modulate(t):
                    dve.wait_ge(xn_ready, 9 * L + 2 + 2 * t)
                    link(stt(h2[:, t, :], mod2_b[:, min(t, 1), 1, :], 1.0, h2[:, t, :], ALU.add, ALU.mult))
                    tt(h2[:, t, :], h2[:, t, :], mod2_b[:, min(t, 1), 0, :], ALU.add).then_inc(h2_ready, 1)

                dve.wait_ge(ln_in_s, (2 * L + 1) * 16)
                first_residual(0)
                first_gain(0)
                dve.wait_ge(mod2_in, 16 * (L + 1))
                modulate(0)
                first_residual(1)
                first_gain(1)
                first_residual(2)
                modulate(1)
                first_gain(2)
                with dve.If(L < DEPTH - 1):
                    first_mods_rows(L + 1)
                    first_mods_out(L + 1, bmod1[:, bass.ds(before_last(L) + 1, 1), :, :].rearrange("p u v k -> p (u v) k"))
                modulate(2)

                def v16(n):
                    return rt[:, n, :]

                def v44(n):
                    return rt[:, n, :].rearrange("p (g j) -> p g j", j=4)

                def ranks(val, n_out, a, b):
                    n = val.shape[1]
                    vi = val.rearrange("p (g u i) -> p g u i", u=1, i=4).broadcast_to([P, n // 4, 4, 4])
                    vj = val.rearrange("p (g j u) -> p g j u", j=4, u=1).broadcast_to([P, n // 4, 4, 4])
                    pa = pair[:, 0, 0:4 * n].rearrange("p (g j i) -> p g j i", j=4, i=4)
                    pb = pair[:, 1, 0:4 * n].rearrange("p (g j i) -> p g j i", j=4, i=4)
                    lt = const[:, C_LT4:C_LT4 + 16].rearrange("p (g j i) -> p g j i", g=1, i=4).broadcast_to([P, n // 4, 4, 4])
                    link(tt(pa, vi, vj, ALU.is_gt))
                    link(tt(pb, vi, vj, ALU.is_equal))
                    link(tt(pb, pb, lt, ALU.mult))
                    link(tt(pa, pa, pb, ALU.add))
                    link(dve.tensor_reduce(n_out, pa, AX.X, ALU.add))

                for t in range(TILES):
                    await_read(dve, L, ("logit", t))
                link(ts(v16(1), v16(0), 1.0, None, ALU.add))
                link(dve.reciprocal(v16(2), v16(1)))
                link(tt(v16(3).rearrange("p (t e) -> p t e", t=TILES), v16(2).rearrange("p (t e) -> p t e", t=TILES),
                        broute[:, :].rearrange("p (u e) -> p u e", u=1).broadcast_to([P, TILES, E]), ALU.add))
                ranks(v16(3), v44(4), 0, 1)
                link(ts(v16(4), v16(4), 2.0, None, ALU.is_lt))
                link(tt(v16(5), v16(4), v16(3), ALU.mult))
                link(dve.tensor_reduce(rt[:, 6, 0:TILES * GROUPS], v44(5), AX.X, ALU.add))
                ranks(rt[:, 6, 0:TILES * GROUPS], rt[:, 7, 0:TILES * GROUPS].rearrange("p (t g) -> p t g", g=4), 0, 1)
                link(ts(rt[:, 7, 0:TILES * GROUPS], rt[:, 7, 0:TILES * GROUPS], 1.0, None, ALU.is_lt))
                link(tt(v44(8), v44(4), rt[:, 7, 0:TILES * GROUPS].rearrange("p (g u) -> p g u", u=1)
                        .broadcast_to([P, TILES * GROUPS, 4]), ALU.mult))
                dve.tensor_copy(maskb[:, :], v16(8)).then_inc(mask_ready, 1)
                link(tt(v16(9), v16(8), v16(2), ALU.mult))
                link(dve.tensor_reduce(st[:, 0:3], v16(9).rearrange("p (t e) -> p t e", t=TILES), AX.X, ALU.add))
                link(dve.reciprocal(st[:, 3:6], st[:, 0:3]))
                link(tt(v16(9).rearrange("p (t e) -> p t e", t=TILES), v16(9).rearrange("p (t e) -> p t e", t=TILES),
                        st[:, 3:6].rearrange("p (t u) -> p t u", u=1).broadcast_to([P, TILES, E]), ALU.mult))
                await_product(dve, L, "place")
                link(dve.tensor_copy(v16(10), bank("place")[:, 0:TILES * E]))
                tokens = rt[:, 15, 0:E]
                read_out(dve.tensor_copy(tokens, bank("place")[:, TILES * E:TILES * E + E]), "place")
                await_read(dve, L, "place")

                def rows(ap, n):
                    return ap.rearrange("p (u e) -> p u e", u=1).broadcast_to([P, n, E])

                def cols(ap, n):
                    return ap.rearrange("p (e u) -> p e u", u=1).broadcast_to([P, ap.shape[1], n])

                def grid(b, n, m):
                    return pair[:, b, 0:n * m].rearrange("p (a b) -> p a b", a=n)

                lt16 = const[:, C_LT16:C_LT16 + E * E].rearrange("p (a b) -> p a b", a=E)
                prev = const[:, C_PREV:C_PREV + E * E].rearrange("p (a b) -> p a b", a=E)
                num = const[:, C_NUM:C_NUM + 32]
                halves, rank, by_rank, base, bases = (rt[:, 11, 0:16], rt[:, 11, 16:32], rt[:, 11, 32:48],
                                                      rt[:, 12, 0:16], rt[:, 12, 16:32])
                link(tt(grid(0, E, 6), cols(tokens, 6),
                        const[:, C_HALF:C_HALF + 6].rearrange("p (u j) -> p u j", u=1).broadcast_to([P, E, 6]), ALU.is_gt))
                link(dve.tensor_reduce(halves, grid(0, E, 6), AX.X, ALU.add))
                link(tt(grid(0, E, E), rows(halves, E), cols(halves, E), ALU.is_gt))
                link(tt(grid(1, E, E), rows(halves, E), cols(halves, E), ALU.is_equal))
                link(tt(grid(1, E, E), grid(1, E, E), lt16, ALU.mult))
                link(tt(grid(0, E, E), grid(0, E, E), grid(1, E, E), ALU.add))
                link(dve.tensor_reduce(rank, grid(0, E, E), AX.X, ALU.add))
                link(tt(grid(1, E, E), rows(rank, E), cols(num[:, 0:E], E), ALU.is_equal))
                link(tt(grid(0, E, E), grid(1, E, E), rows(halves, E), ALU.mult))
                link(dve.tensor_reduce(by_rank, grid(0, E, E), AX.X, ALU.add))
                link(tt(grid(0, E, E), prev, rows(by_rank, E), ALU.mult))
                link(dve.tensor_reduce(base, grid(0, E, E), AX.X, ALU.add))
                link(ts(grid(0, 1, E), halves.rearrange("p (u e) -> p u e", u=1), 0.0, None, ALU.is_gt))
                link(dve.tensor_reduce(tab[:, T_ACTIVE:T_ACTIVE + 1], pair[:, 0, 0:E], AX.X, ALU.add))
                link(tt(grid(0, E, E), grid(1, E, E), rows(num[:, 0:E], E), ALU.mult))
                link(dve.tensor_reduce(tab[:, T_WHO:T_WHO + E], grid(0, E, E), AX.X, ALU.add))
                link(dve.tensor_copy(tab[:, T_BLOCKS:T_BLOCKS + PAIRS], by_rank[:, 0::2]))
                link(dve.tensor_reduce(tab[:, T_COUNT:T_COUNT + 1], by_rank[:, 0::2], AX.X, ALU.add))
                link(dve.tensor_copy(tab[:, T_FIRST:T_FIRST + 1], tab[:, T_LAST:T_LAST + 1]))
                link(ts(tab[:, T_START:T_START + PAIRS], base[:, 0::2], tab[:, T_FIRST:T_FIRST + 1], None, ALU.add))
                link(tt(tab[:, T_LAST:T_LAST + 1], tab[:, T_FIRST:T_FIRST + 1], tab[:, T_COUNT:T_COUNT + 1], ALU.add))
                link(dve.tensor_copy(tabu[:, :], tab[:, :]))
                dve.sem_inc(table_ready, 1)
                link(stt(bases, base, float(P), const[:, C_HALF + 8:C_HALF + 24], ALU.mult, ALU.add))
                link(tt(grid(0, E, E), cols(rank, E), rows(num[:, 0:E], E), ALU.is_equal))
                link(tt(grid(0, E, E), grid(0, E, E), rows(bases, E), ALU.mult))
                link(dve.tensor_reduce(rt[:, 12, 32:48], grid(0, E, E), AX.X, ALU.add))
                link(tt(v16(0).rearrange("p (t e) -> p t e", t=TILES), rows(rt[:, 12, 32:48], TILES),
                        v16(10).rearrange("p (t e) -> p t e", t=TILES), ALU.add))
                t16 = lambda n: rt[:, n, :].rearrange("p (t e) -> p t e", t=TILES)
                link(tt(t16(13), t16(8), rows(const[:, C_NUM + 1:C_NUM + 1 + E], TILES), ALU.mult))
                link(dve.tensor_reduce(st[:, 0:3], t16(13), AX.X, ALU.max))
                link(tt(t16(13), t16(13), st[:, 0:3].rearrange("p (t u) -> p t u", u=1).broadcast_to([P, TILES, E]),
                        ALU.is_equal))
                link(tt(v16(14), v16(8), v16(13), ALU.subtract))
                for a, who in ((0, 14), (1, 13)):
                    link(tt(v16(3), v16(0), v16(who), ALU.mult))
                    link(dve.tensor_reduce(st[:, 8 + 3 * a:11 + 3 * a], t16(3), AX.X, ALU.add))
                    link(tt(v16(3), v16(10), v16(who), ALU.mult))
                    link(dve.tensor_reduce(st[:, 14 + 3 * a:17 + 3 * a], t16(3), AX.X, ALU.add))
                over = pair[:, 0, 0:30].rearrange("p (c j) -> p c j", c=6)
                link(tt(over, cols(st[:, 14:20], 5),
                        const[:, C_HALF + 1:C_HALF + 6].rearrange("p (u j) -> p u j", u=1).broadcast_to([P, 6, 5]), ALU.is_ge))
                link(dve.tensor_reduce(st[:, 14:20], over, AX.X, ALU.add))
                link(stt(st[:, 8:14], st[:, 14:20], float(HALF), st[:, 8:14], ALU.mult, ALU.add))
                link(dve.tensor_copy(ridx[:, :, :].rearrange("p a t -> p (a t)"), st[:, 8:14]))
                link(tt(pair[:, 0, 0:6 * (BLOCKS - 1)].rearrange("p (c b) -> p c b", c=6), cols(st[:, 8:14], BLOCKS - 1),
                        const[:, C_ROWS:C_ROWS + BLOCKS - 1].rearrange("p (u b) -> p u b", u=1)
                        .broadcast_to([P, 6, BLOCKS - 1]), ALU.is_ge))
                link(dve.tensor_reduce(st[:, 14:20], pair[:, 0, 0:6 * (BLOCKS - 1)].rearrange("p (c b) -> p c b", c=6),
                                       AX.X, ALU.add))
                link(stt(st[:, 8:14], st[:, 14:20], -float(P), st[:, 8:14], ALU.mult, ALU.add))
                dve.wait_ge(state_out, 64 * (L + 1) + 16)
                link(tt(sel, cols(st[:, 8:14], P), iota.rearrange("p (u s) -> p u s", u=1).broadcast_to([P, 6, P]),
                        ALU.is_equal))
                blk = pair[:, 0, 0:6 * COLS].rearrange("p (c b) -> p c b", c=6)
                link(tt(blk, cols(st[:, 14:20], COLS),
                        num[:, 0:COLS].rearrange("p (u b) -> p u b", u=1).broadcast_to([P, 6, COLS]), ALU.is_equal))
                for part in range(2):
                    for t in range(TILES):
                        ins = ts(where[:, t::TILES, part, :], blk[:, t::TILES, :],
                                 const[:, C_TOK + 2 * t + part:C_TOK + 2 * t + part + 1], None, ALU.mult)
                link(ins)
                dve.sem_inc(sel_ready, 1)
                for a, who in ((0, 14), (1, 13)):
                    link(tt(v16(3), v16(9), v16(who), ALU.mult))
                    link(dve.tensor_reduce(gates[:, a, :], t16(3), AX.X, ALU.add))
                dve.sem_inc(gates_ready, 1)
                await_product(dve, L, "index")
                src = bank("index")[:, 0:2 * COLS]
                link(dve.tensor_copy(pair[:, 0, 0:COLS], src[:, COLS:2 * COLS]))
                read_out(tt(gidx[:, :], src[:, 0:COLS], pair[:, 0, 0:COLS], ALU.add), "index")

                first = dve.value_load(tabu[0:1, T_FIRST:T_FIRST + 1], min_val=1, max_val=BLOCKS * DEPTH + 1)
                count = dve.value_load(tabu[0:1, T_COUNT:T_COUNT + 1], min_val=1, max_val=BLOCKS)
                with dve.Fori(0, count) as j:
                    i = j + first
                    dve.wait_ge(up_exp, i + 1)
                    ts(silu, silu, 1.0, None, ALU.add).then_inc(silu_step, 1)
                    dve.wait_ge(silu_step, i * 3 + 1)
                    dve.reciprocal(silu, silu).then_inc(silu_step, 1)
                    dve.wait_ge(silu_step, i * 3 + 2)
                    tt(silu, silu, psD[:, 0:DE], ALU.mult).then_inc(silu_step, 1)
                    dve.wait_ge(silu_step, i * 3 + 3)
                    dve.wait_ge(hidT_full, i)
                    tt(hid, silu, psD[:, DE:2 * DE], ALU.mult).then_inc(hid_ready, 1)

                def combine(t):
                    a, b = fetched[2 * t], fetched[2 * t + 1]
                    dve.wait_ge(first_gated, 3 * L + t + 1)
                    dve.wait_ge(pick_in[2 * t + 1], 16 * (L + 1))
                    link(stt(a, b, gates[:, 1, t:t + 1], a, ALU.mult, ALU.add))
                    link(tt(a, a, gate_b[:, min(t, 1), :], ALU.mult))
                    residual(t, a)
                    norm_stats(L, 9 + t, x[:, t, :])

                dve.wait_ge(gate2_in, 16 * (L + 1))
                dve.wait_ge(ln_in_s, (2 * L + 2) * 16)
                combine(0)
                combine(1)
                combine(2)
                dve.wait_ge(gained, 6 * L + 5)
                pre_stats(0)
                for t in (1, 2):
                    dve.wait_ge(xn_ready, 9 * L + 7 + t)
                    gain_bias(t)
                    pre_stats(t)

        @block.gpsimd
        def _(pool):
            restart, link = chain(pool, pool_done)

            def rstd(L, n):
                pool.wait_ge(stats_ready, 9 * L + n - 2)
                reciprocal_root(n % 3, rstd_ready)

            def pre_rstd_of(layer, t):
                pool.wait_ge(pre_mv, 3 * layer + t + 1)
                reciprocal_root(3 + t, pre_rstd)

            def reciprocal_root(b, done):
                link(pool.tensor_tensor(lnv[:, b, 0:1], mv[:, b, 1:2], half[:, 3:4], ALU.add))
                link(pool.tensor_tensor(lnv[:, b, 1:2], lnv[:, b, 0:1], half[:, 0:1], ALU.pow))
                pool.tensor_scalar(lnv[:, b, 2:3], mv[:, b, 0:1], lnv[:, b, 1:2], -1.0, ALU.mult, ALU.mult)\
                    .then_inc(done, 1)

            def layer_loads(l):
                pool.dma_start(cache[:, :], cache_in[l]).then_inc(layer_in_s, 16)
                pool.dma_start(convp[:, :, :], conv_in[l]).then_inc(layer_in_s, 16)
                pool.dma_start(lamv[:, :, :], lam_in[l].partition_broadcast(P)).then_inc(layer_in_s, 16)
                pool.dma_start(lamc[:, :], lamc_in[l].partition_broadcast(P)).then_inc(layer_in_s, 16)
                pool.dma_start(gain[:, :], gain_in[l].partition_broadcast(P)).then_inc(layer_in_s, 16)
                for g in range(4):
                    pool.dma_start(mrow[32 * g:32 * g + 32, :, :], bmod_in[l, g].partition_broadcast(32)).then_inc(bmod_in_s, 16)

            pool.wait_ge(cond_ready, 1)
            for t in range(TILES):
                pre_rstd_of(0, t)
            layer_loads(0)
            pool.wait_ge(const_in_s, 80)
            pool.dma_start(bias[:, :, :, :], bias_in[0]).then_inc(layer_bias_in, 16)
            pool.sem_inc(gcol_ready, 1)
            with pool.Fori(0, DEPTH) as L:
                restart()
                pool.wait_ge(gained, 6 * L + 1)
                stop_here(pool, "pool")
                pool.dma_start(ln_b[:, :, :], ln_in[L, 0:2].partition_broadcast(P)).then_inc(ln_in_s, 16)
                pool.wait_ge(layer_bias_in, (L + 1) * 16)
                flat = bias[:, :, :, :].rearrange("p h s c -> p (h s) c")
                pool.tensor_tensor(flat, flat, const[:, C_MASK:C_MASK + GRID_W].rearrange("p (u c) -> p u c", u=1)
                                   .broadcast_to([P, 6 * NA_HEADS, GRID_W]), ALU.add).then_inc(bias_ready, 1)
                with pool.If(L < 1):
                    pool.wait_ge(ln_in_s, 16)
                    pool.wait_ge(roped, 8)
                    for q in range(4):
                        pool.dma_start(moe_d.rearrange("(b p) d -> p b d", p=P)[:, BLOCKS // 4 * q:BLOCKS // 4 * (q + 1), :],
                                       ln_b[:, 0:1, :].broadcast_to([P, BLOCKS // 4, D])).then_inc(filled, 16)
                    pool.wait_ge(filled, 64)
                for h in range(DA_HEADS):
                    pool.wait_ge(ms_ready, 4 * L + h + 1)
                    stop_here(pool, "pool")
                    link(pool.tensor_scalar(msr[:, 1, :], msr[:, 0, :], 1.0 / P, EPS, ALU.mult, ALU.add))
                    pool.tensor_tensor(msr[:, 2, :], msr[:, 1, :], half[:, 0:3], ALU.pow).then_inc(rms_ready, 1)
                pool.wait_ge(mod_stored, (L + 1) * 8 * 16)
                stop_here(pool, "pool")
                pool.dma_start(gate_b[:, :, :], mod_d[:, 0, :].partition_broadcast(P)).then_inc(gate1_in, 16)
                pool.wait_ge(av_done, N_STEPS * (L + 1))
                stop_here(pool, "pool")
                pool.dma_start(mod2_b[:, :, :, :], mod_d[:, 1:3, :].partition_broadcast(P)).then_inc(mod2_in, 16)
                for n in range(3, 9):
                    rstd(L, n)
                pool.wait_ge(h2_ready, 3 * L + 3)
                stop_here(pool, "pool")
                pool.dma_start(ln_b[:, :, :], ln_in[L, 2:4].partition_broadcast(P)).then_inc(ln_in_s, 16)
                pool.dma_start(gate_b[:, :, :], mod_d[:, 3, :].partition_broadcast(P)).then_inc(gate2_in, 16)
                pool.wait_ge(h2_stored, 16 * 3 * (L + 1))
                await_read(pool, L, "index")
                pool.wait_ge(table_ready, L + 1)
                stop_here(pool, "pool")
                first = pool.value_load(tabu[0:1, T_FIRST:T_FIRST + 1], min_val=1, max_val=BLOCKS * DEPTH + 1)
                count = pool.value_load(tabu[0:1, T_COUNT:T_COUNT + 1], min_val=1, max_val=BLOCKS)
                with pool.Fori(0, count + 1) as j:
                    i = j + first + L
                    pool.wait_ge(xT_full, i)
                    pool.tensor_copy(gcol[:, :], gidx[:, bass.ds(j, 1)]).then_inc(gcol_ready, 1)
                    pool.wait_ge(gcol_ready, i + 1)
                    stop_here(pool, "pool")
                    pool.indirect_dma_start(xg, None, h2_d[:, :],
                                            bass.IndirectOffsetOnAxis(gcol[:, 0:1], 0)).then_inc(xg_in, 16)
                with pool.If(L < DEPTH - 1):
                    pool.wait_ge(state_out, 64 * (L + 1) + 16)
                    stop_here(pool, "pool")
                    layer_loads(before_last(L) + 1)
                pool.wait_ge(xT_ready, first + count + L + 1)
                pool.wait_ge(yo_stored, (first + count) * 16 + 16)
                stop_here(pool, "pool")
                for t in range(TILES):
                    for a in range(2):
                        pool.indirect_dma_start(fetched[2 * t + a], None, moe_d[:, :],
                                                bass.IndirectOffsetOnAxis(ridx[:, a, t:t + 1], 0))\
                            .then_inc(pick_in[2 * t + a], 16)
                pool.wait_ge(ln_in_s, (2 * L + 2) * 16)
                rstd(L, 9)
                pool.wait_ge(xn_ready, 9 * L + 7)
                link(pool.tensor_tensor(x[:, 0, :], x[:, 0, :], ln_b[:, 0, :], ALU.mult))
                pool.tensor_tensor(x[:, 0, :], x[:, 0, :], ln_b[:, 1, :], ALU.add).then_inc(gained, 1)
                rstd(L, 10)
                rstd(L, 11)
                for t in range(TILES):
                    pre_rstd_of(L + 1, t)
                with pool.If(L < DEPTH - 1):
                    pool.wait_ge(pair_done, (L + 1) * STAGES + 1)
                    stop_here(pool, "pool")
                    pool.dma_start(bias[:, :, :, :], bias_in[before_last(L) + 1]).then_inc(layer_bias_in, 16)


def _constants():
    c = np.zeros((P, N_CONST), np.float32)
    p = np.arange(P)
    c[:, C_ID:C_ID + P] = np.eye(P)
    c[p, C_SWAP + (p ^ 16)] = 1.0
    j = p % 64
    inv = (np.float32(10000.0) ** (-np.arange(16, dtype=np.float32) / 16)).astype(np.float32)
    t = np.arange(LAT)
    pos = np.where((j // 32 == 0)[:, None], t[None, :] // GRID_W, t[None, :] % GRID_W).astype(np.float32)
    ang = pos * inv[j % 16][:, None]
    c[:, C_COS:C_COS + LAT] = np.cos(ang)
    c[:, C_SIN:C_SIN + LAT] = np.where((j % 32 < 16)[:, None], -np.sin(ang), np.sin(ang))
    qc, kc = p % GRID_W, np.arange(GRID_W)
    w0 = np.clip(qc - 8, 0, GRID_W - 16)[:, None]
    c[:, C_MASK:C_MASK + GRID_W] = np.where((kc >= w0) & (kc < w0 + 16), 0.0, MASKED)
    c[:, C_UTRI:C_UTRI + P] = p[:, None] < p[None, :]
    c[:, C_IOTA:C_IOTA + P] = p[None, :]
    jj, ii = np.meshgrid(np.arange(4), np.arange(4), indexing="ij")
    c[:, C_LT4:C_LT4 + 16] = (ii < jj).reshape(1, 16)
    c[:, C_NUM:C_NUM + 32] = np.arange(32)
    r = np.arange(E)
    c[:, C_LT16:C_LT16 + E * E] = (r[None, :] < r[:, None]).reshape(1, E * E)
    c[:, C_PREV:C_PREV + E * E] = ((r[None, :] % 2 == 0) & (r[None, :] < r[:, None] // 2 * 2)).reshape(1, E * E)
    c[:, C_ROWS:C_ROWS + BLOCKS - 1] = P * np.arange(1, BLOCKS)
    c[:, C_HALF:C_HALF + 6] = HALF * np.arange(6)
    c[:, C_HALF + 8:C_HALF + 24] = HALF * (r % 2)
    for t in range(TILES):
        c[:, C_TOK + 2 * t] = p
        c[:, C_TOK + 2 * t + 1] = P * t
    return c


def _experts(w1, w3, w2):
    up = np.concatenate([w1.reshape(DEPTH, E, P, KC, DE), w3.reshape(DEPTH, E, P, KC, DE)], axis=4)
    down = w2.reshape(DEPTH, E, 2, P, D).transpose(0, 1, 3, 2, 4)
    return np.concatenate([up.reshape(DEPTH, E, P, -1), down.reshape(DEPTH, E, P, -1)], axis=3).reshape(DEPTH * E, P, EXPERT)


def _weights(w_mod, w_in, w_out):
    walls = np.empty((DEPTH * ITEMS, P, ITEM), np.float32)
    for l in range(DEPTH):
        at = RING + l * ITEMS
        m = w_mod[l].reshape(P, KC, N_MOD, D)
        for v in range(2):
            cols = m[:, :, v].reshape(P, KC, P, 4, 2).transpose(3, 0, 1, 4, 2).reshape(4, P, ITEM)
            walls[at - RING + 4 * v:at - RING + 4 * v + 4] = cols
        for v in range(2, N_MOD):
            for g in range(4):
                walls[at + MODS0 + 4 * (v - 2) + g] = m[:, :, v, 256 * g:256 * g + 256].reshape(P, ITEM)
        wi = w_in[l].reshape(P, KC, -1)
        for n, (piece, half) in enumerate(PIECES):
            col = PIECE_COL[piece] + 256 * half
            walls[at + W_IN0 + n] = wi[:, :, col:col + 256].reshape(P, ITEM)
        wo = w_out[l].reshape(KC, P, D)
        for n in range(4):
            walls[at + W_OUT0 + n] = wo[:, :, 256 * n:256 * n + 256].transpose(1, 0, 2).reshape(P, ITEM)
    return walls


def _local_bias(rel):
    p = np.arange(P)[:, None, None]
    row = np.arange(6)[None, :, None] + np.where(p < 64, 5, 4)
    col = np.clip(np.arange(GRID_W)[None, None, :] - p % GRID_W + 15, 0, 30)
    return np.ascontiguousarray(rel[:, :, row, col].transpose(0, 2, 1, 3, 4))


def kernel(x_prompt, x_sample, cache_na_k, cache_na_v, cache_da_k, cache_da_v, c, c_ctx,
           w_mod, b_mod, w_in, na_rel_bias, sc_conv_w, sc_conv_b, da_lambda, da_norm_g, w_out,
           ln1_g, ln1_b, w_router, b_router, moe_w1, moe_w3, moe_w2, ln2_g, ln2_b):
    import math

    import concourse.bacc as bacc
    from concourse.bass_utils import run_bass_kernel_spmd

    a = np.asarray
    cache = np.concatenate([a(cache_da_k)[0].reshape(DEPTH, P, 512), a(cache_na_k)[0].reshape(DEPTH, P, 256),
                            a(cache_da_v)[0].reshape(DEPTH, P, 512), a(cache_na_v)[0].reshape(DEPTH, P, 256)], axis=2)
    conv = np.concatenate([a(sc_conv_w), a(sc_conv_b)[:, None]], axis=1).reshape(DEPTH, 4, 2, P).transpose(0, 3, 2, 1)
    lam_init = [0.8 - 0.6 * math.exp(-0.3 * l) for l in range(DEPTH)]
    ins = {
        "weights": _weights(a(w_mod), a(w_in), a(w_out)),
        "experts": _experts(a(moe_w1), a(moe_w3), a(moe_w2)),
        "x": np.concatenate([a(x_prompt)[0], a(x_sample)[0]]).reshape(TILES, P, D),
        "cond": np.stack([a(c_ctx), a(c)[0]]).reshape(2, P, KC).transpose(1, 0, 2),
        "cache": cache,
        "local_bias": _local_bias(a(na_rel_bias)),
        "conv": conv,
        "da_lambda": a(da_lambda),
        "lambda_init": np.array([[v, 1.0 - v] for v in lam_init], np.float32),
        "da_gain": a(da_norm_g),
        "ln": np.stack([a(ln1_g), a(ln1_b), a(ln2_g), a(ln2_b)], axis=1),
        "w_router": a(w_router).reshape(P, KC, E),
        "b_router": a(b_router),
        "b_mod": a(b_mod).reshape(DEPTH, N_MOD, 4, 256)[:, 2:].transpose(0, 2, 1, 3),
        "b_mod_first": a(b_mod).reshape(DEPTH, N_MOD, P, KC)[:, :2].transpose(2, 0, 1, 3),
        "constants": _constants(),
    }
    ins = {k: np.ascontiguousarray(v) for k, v in ins.items()}
    outs = {"y_prompt": (P, D), "y_sample": (LAT, D), "new_na_k": (DEPTH, P, 256), "new_na_v": (DEPTH, P, 256),
            "new_da_k": (DEPTH, P, 512), "new_da_v": (DEPTH, P, 512)}
    nc = bacc.Bacc("TRN2", target_bir_lowering=False, num_devices=1)
    args = [nc.dram_tensor(f"in_{k}", v.shape, F32, kind="ExternalInput").ap() for k, v in ins.items()]
    args += [nc.dram_tensor(f"out_{k}", s, F32, kind="ExternalOutput").ap() for k, s in outs.items()]
    hybrid_step_kernel(nc, *args)
    r = run_bass_kernel_spmd(nc, [{f"in_{k}": v for k, v in ins.items()}], core_ids=[0]).results[0]
    return (r["out_y_prompt"].reshape(1, P, D), r["out_y_sample"].reshape(1, LAT, D),
            r["out_new_na_k"].reshape(1, DEPTH, P, 4, 64), r["out_new_na_v"].reshape(1, DEPTH, P, 4, 64),
            r["out_new_da_k"].reshape(1, DEPTH, P, 8, 64), r["out_new_da_v"].reshape(1, DEPTH, P, 4, 128))
```

```python
from contextlib import ExitStack

import numpy as np

import concourse.bass as bass
from concourse import mybir

ALU = mybir.AluOpType
ACT = mybir.ActivationFunctionType
AX = mybir.AxisListType
F32 = mybir.dt.float32
BF16 = mybir.dt.bfloat16
U32 = mybir.dt.uint32

P = 128
D = 1024
KC = D // P
DEPTH = 2
TILES = 3
T = TILES * P
LAT = 2 * P
GRID_W = 64
DA_HEADS = 4
NA_HEADS = 4
DH = 64
E = 16
GROUPS = 4
DE = 256
HALF = 64
PAIRS = E // 2
BLOCKS = (2 * T // HALF + E - 1 + T // HALF) // 2
EXPERT = 6144
UP = 4096
BUFS = 4
SCALE = DH ** -0.5
ALPHA = (2 * DEPTH) ** 0.25
EPS = 1e-5
MASKED = -1.0e30

RING = 8
ITEM = 2048
N_MOD = 6
W_IN0, MODS0, W_OUT0, NEXT0, ITEMS = 0, 12, 28, 32, 40

T_FIRST, T_ACTIVE, T_COUNT, T_START, T_LAST, T_NONE, T_BLOCKS, T_WHO = 0, 1, 2, 3, 11, 12, 13, 21
STAGES = PAIRS + 1
COLS = BLOCKS + 1

KCH = {"dak": 0, "nak": 4}
QCH = {"daq": 0, "naq": 4, "scc": 6, "scx": 8, "scb": 10}
PIECES = [("dav", 0), ("dav", 1), ("nav", 0), ("dak", 0), ("dak", 1), ("daq", 0), ("daq", 1),
          ("nak", 0), ("naq", 0), ("scc", 0), ("scx", 0), ("scb", 0)]
VALUES = 3
KEY0 = VALUES * TILES
ROPES = 8
PIECE_COL = {"naq": 0, "nak": 256, "nav": 512, "scb": 768, "scc": 1024, "scx": 1280,
             "daq": 1536, "dak": 2048, "dav": 2560}
V_COL = {"dav": 0, "nav": 512}

(C_ID, C_SWAP, C_COS, C_SIN, C_MASK, C_LT4, C_NUM, C_TOK, C_PREV, C_ROWS, C_HALF, C_UTRI, C_IOTA) = (
    0, 128, 256, 512, 768, 832, 848, 880, 892, 1148, 1164, 1188, 1316)
N_KEPT = 1188
N_CONST = 1444
SLOT_BANK = {"A": 0, "B": 2, "C": 4, "D": 6, "E": 7}

STEPS = [("da", h, t) for h in range(DA_HEADS) for t in range(TILES)] + \
        [("na", h, t) for h in range(NA_HEADS) for t in range(TILES)]
N_STEPS = len(STEPS)
MIX_DELAY = 4


def projection_order():
    order = []
    for n in range(KEY0):
        if n < TILES:
            order.append(("hT", n))
        order.append(("proj", n))
    for n in range(2 * (len(PIECES) - VALUES)):
        order.append(("proj", KEY0 + n))
        if 0 < n <= ROPES:
            order.append(("rope", n - 1))
    return order


def projected(n):
    return (n % VALUES, n // VALUES) if n < KEY0 else (VALUES + (n - KEY0) // 2, (n - KEY0) % 2)


def psum_plan():
    jobs, at = [], 0
    for name in projection_order():
        jobs.append((name, "DE"[name[1] % 2] if name[0] == "rope" else "BCA"[at % 3]))
        at += name[0] != "rope"
    jobs += [("cacheT", "C"), ("kout", "B")]
    jobs += [(("score", 0), "A"), (("score", 1), "B")]
    mixes = 0
    for i, (kind, h, t) in enumerate(STEPS):
        if i + 2 < N_STEPS:
            jobs.append((("score", i + 2), "ABC"[(i + 2) % 3]))
        jobs.append((("probT", i), "D"))
        if i > 0:
            last, g, u = STEPS[i - 1]
            if u == 0:
                jobs.append((("out", last, g), "E"))
            if last == "da" and u == 2:
                jobs.append((("mod", 2 + g), "D"))
        if mixes < DA_HEADS and i == 3 * mixes + 2 + MIX_DELAY:
            jobs.append((("mixT", mixes), "D"))
            mixes += 1
    jobs += [(("y", t), "ABC"[t]) for t in range(TILES)]
    for t in range(TILES):
        jobs += [(("h2T", t), "ABC"[t]), (("logit", t), "DED"[t])]
    jobs.append(("place", "E"))
    jobs.append(("index", "D"))
    turn, plan = {s: 0 for s in SLOT_BANK}, {}
    for name, slot in jobs:
        assert name not in plan, name
        plan[name] = (slot, turn[slot])
        turn[slot] += 1
    return plan, turn


def hybrid_step_kernel(nc, walls, experts_in, x_in, cond_in, cache_in, bias_in, conv_in, lam_in, lamc_in, gain_in,
                       ln_in, router_in, brouter_in, bmod_in, bmod1_in, const_in,
                       y_prompt, y_sample, new_na_k, new_na_v, new_da_k, new_da_v):
    plan, turns = psum_plan()
    mod_d = nc.dram_tensor("mod_rows", [2, 4, D], F32, kind="Internal").ap()
    h2_d = nc.dram_tensor("h2_rows", [T, D], F32, kind="Internal").ap()
    moe_d = nc.dram_tensor("moe_rows", [BLOCKS * P, D], F32, kind="Internal").ap()

    with ExitStack() as ctx:
        def sb(name, shape, dt=F32):
            return ctx.enter_context(nc.sbuf_tensor(name, shape, dt))

        def sem(name):
            return ctx.enter_context(nc.semaphore(name))

        big = sb("big", [P, RING * ITEM + 2 * TILES * D + 4608])
        ring = big[:, 0:RING * ITEM].rearrange("p (s n) -> p s n", s=RING)
        expert_w = big[:, 0:BUFS * EXPERT]
        tail = big[:, RING * ITEM:]
        x = sb("x", [P, TILES, D])
        act_a = tail[:, 0:TILES * D].rearrange("p (t d) -> p t d", t=TILES)
        act_b = tail[:, TILES * D:2 * TILES * D]
        attn = tail[:, 2 * TILES * D:]
        shared = sb("shared", [P, 7680])
        v_sb = sb("v_sb", [P, TILES, 768])
        cache = sb("cache", [P, 1536])
        bias = attn[:, 0:1536].rearrange("p (h s c) -> p h s c", h=NA_HEADS, s=6)
        probs = attn[:, 1536:3840].rearrange("p (b m k) -> p b m k", b=3, m=2)
        probT = attn[:, 3840:4608].rearrange("p (b k t) -> p b k t", b=2, k=3)
        mod2_b = attn[:, 0:4096].rearrange("p (c v d) -> p c v d", c=2, v=2)
        gate_b = sb("gate_b", [P, 2, D])
        ln_b = sb("ln_b", [P, 2, D])
        wide = sb("wide", [P, 1280])
        mrow = sb("mrow", [P, 4, 256])
        bmod1 = sb("bmod1", [P, DEPTH, 2, KC])
        modT = sb("modT", [P, 2, 2, KC])
        const = sb("const", [P, N_KEPT])
        constb = sb("constb", [P, 3 * P], BF16)
        convp = sb("convp", [P, 2, 4])
        lamv = sb("lamv", [P, 4, 64])
        lamc = sb("lamc", [P, 2])
        lams = sb("lams", [P, 8])
        gain = sb("gain", [P, P])
        routw = sb("routw", [P, KC, E])
        broute = sb("broute", [P, E])
        condv = sb("condv", [P, 2, KC])
        conds = sb("conds", [P, 2, 2, KC])
        condT = sb("condT", [P, KC, 32])
        kout = cache[:, 0:768]
        head = sb("head", [P, 2 * T])
        osb = head[:, 0:T].rearrange("p (t d) -> p t d", t=TILES)
        on = head[:, T:2 * T].rearrange("p (t d) -> p t d", t=TILES)
        mrow1 = head[:, 0:512].rearrange("p (v n) -> p v n", v=2)
        sq = wide[:, 768:1152].rearrange("p (t d) -> p t d", t=TILES)
        st = sb("st", [P, 24])
        mxs = sb("mxs", [P, 3, 2])
        rsum = sb("rsum", [P, 3, 2])
        rinv = sb("rinv", [P, 3, 4])
        msr = sb("msr", [P, 4, TILES])
        stats = sb("stats", [P, 6, 2, 6])
        mv = sb("mv", [P, 6, 2])
        lnv = sb("lnv", [P, 6, 3])
        half = sb("half", [P, 4])
        rt = sb("rt", [P, 16, TILES * E])
        pair = wide[:, 0:1024].rearrange("p (b n) -> p b n", b=2)
        sel = v_sb[:, :, :].rearrange("p a b -> p (a b)").bitcast(BF16)[:, 0:2 * TILES * P]\
            .rearrange("p (c s) -> p c s", c=2 * TILES)
        where = sb("where", [P, 2 * TILES, 2, COLS], BF16)
        maskb = sb("maskb", [P, TILES * E], BF16)
        gidx = sb("gidx", [P, COLS], U32)
        gcol = sb("gcol", [P, 1], U32)
        ridx = sb("ridx", [P, 2, TILES], U32)
        tab = sb("tab", [P, 37])
        tabu = sb("tabu", [P, 37], U32)
        gates = sb("gates", [P, 2, TILES])
        psum = ctx.enter_context(nc.psum_tensor("psum", [P, 8, 512], F32))

        ident = const[:, C_ID:C_ID + P]
        swap = const[:, C_SWAP:C_SWAP + P]
        cos_t = const[:, C_COS:C_COS + LAT]
        sin_t = const[:, C_SIN:C_SIN + LAT]
        utri, ones, iota = constb[:, 0:P], constb[:, P:2 * P], constb[:, 2 * P:3 * P]
        xn = act_a
        h2 = shared[:, 0:3072].rearrange("p (t d) -> p t d", t=TILES)
        mix = tail[:, 0:TILES * D].rearrange("p (c t) -> p c t", c=8)
        hT = act_b.rearrange("p (k t) -> p k t", k=KC)
        kT = shared[:, 0:3072].rearrange("p (c t) -> p c t", c=6)
        qT = shared[:, 3072:7680].rearrange("p (c t) -> p c t", c=12)
        xg = shared[:, 0:1024]
        xT = shared[:, 1024:2048]
        yo = shared[:, 2048:3072]
        hid = shared[:, 3072:3328]
        hidT = shared[:, 3328:3584]
        silu = shared[:, 3584:3840]
        fetched = [shared[:, 1024 * i:1024 * i + 1024] for i in range(6)]

        arrived = [sem(f"arrived{s}") for s in range(RING)]
        ring_free = sem("ring_free")
        full = {s: sem(f"full_{s}") for s in SLOT_BANK}
        free = {s: sem(f"free_{s}") for s in SLOT_BANK}
        dve_done, act_done, pool_done = sem("dve_done"), sem("act_done"), sem("pool_done")
        cond_in_s, const_in_s, router_in_s, layer_in_s = sem("cond_in"), sem("const_in"), sem("router_in"), sem("layer_in")
        x_in_s = [sem(f"x_in{t}") for t in range(TILES)]
        bmod_in_s, layer_bias_in = sem("bmod_in"), sem("layer_bias_in")
        ln_in_s = sem("ln_in")
        cond_exp, cond_ready = sem("cond_exp"), sem("cond_ready")
        constb_ready = sem("constb_ready")
        lam_dot, lam_exp = sem("lam_dot"), sem("lam_exp")
        stats_ready, rstd_ready, xn_ready = sem("stats_ready"), sem("rstd_ready"), sem("xn_ready")
        pre_mv, pre_rstd, pre_xn = sem("pre_mv"), sem("pre_rstd"), sem("pre_xn")
        gained = sem("gained")
        mrow_ready, mod_stored = sem("mrow_ready"), sem("mod_stored")
        mod1_full, mod1_rows, mod1T_full, mod1_biased, mod1_ready = (
            sem(n) for n in ("mod1_full", "mod1_rows", "mod1T_full", "mod1_biased", "mod1_ready"))
        gate1_in, mod2_in, gate2_in = sem("gate1_in"), sem("mod2_in"), sem("gate2_in")
        hT_second = sem("hT_second")
        roped = sem("roped")
        kout_ready, state_out = sem("kout_ready"), sem("state_out")
        bias_ready = sem("bias_ready")
        max_ready, prob_ready, av_done = sem("max_ready"), sem("prob_ready"), sem("av_done")
        ms_ready, rms_ready, on_ready, mix_sc = sem("ms_ready"), sem("rms_ready"), sem("on_ready"), sem("mix_sc")
        y_half = sem("y_half")
        h2_ready, h2_stored = sem("h2_ready"), sem("h2_stored")
        mask_ready, sel_ready, sidx_ready = sem("mask_ready"), sem("sel_ready"), sem("sidx_ready")
        who_ready, table_ready = sem("who_ready"), sem("table_ready")
        gates_ready, first_gated = sem("gates_ready"), sem("first_gated")
        pair_done = sem("pair_done")
        up_used = sem("up_used")
        up_in = [sem(f"up_in{q}") for q in range(BUFS)]
        down_in = [sem(f"down_in{q}") for q in range(BUFS)]
        xg_in, gcol_ready = sem("xg_in"), sem("gcol_ready")
        xT_full, xT_ready, up_full, up_exp, hid_ready, hidT_full, hidT_ready, down_full, yo_ready, yo_stored = (
            sem(n) for n in ("xT_full", "xT_ready", "up_full", "up_exp", "hid_ready", "hidT_full", "hidT_ready",
                             "down_full", "yo_ready", "yo_stored"))
        filled = sem("filled")
        silu_step = sem("silu_step")
        pick_in = [sem(f"pick_in{i}") for i in range(6)]
        x_out = sem("x_out")

        def bank(name, n=1):
            b = SLOT_BANK[plan[name][0]]
            return psum[:, b:b + n, :] if n > 1 else psum[:, b, :]

        def claim(eng, L, name):
            slot, turn = plan[name]
            eng.wait_ge(free[slot], L * turns[slot] + turn + 1)

        def produced(ins, name):
            ins.then_inc(full[plan[name][0]], 1)

        def await_product(eng, L, name):
            slot, turn = plan[name]
            eng.wait_ge(full[slot], L * turns[slot] + turn + 1)

        def read_out(ins, name):
            ins.then_inc(free[plan[name][0]], 1)

        def await_read(eng, L, name):
            slot, turn = plan[name]
            eng.wait_ge(free[slot], L * turns[slot] + turn + 2)

        def before_last(L):
            return L.with_bounds(min_val=0, max_val=DEPTH - 2)

        def chain(eng, done):
            at = [0]

            def restart():
                at[0] = 0
                eng.sem_clear(done)

            def link(ins):
                at[0] += 1
                ins.then_inc(done, 1)
                eng.wait_ge(done, at[0])
            return restart, link

        ps_mod1 = psum[:, 6, :].rearrange("p (v n) -> p v n", v=2)
        ps_mod1T = psum[:, 7, :].rearrange("p (v c r) -> p v c r", v=2, c=2)
        psA, psB, psC, psD = (psum[:, 0:2, :].rearrange("p a b -> p (a b)"), psum[:, 2, :],
                              psum[:, 4:6, :].rearrange("p a b -> p (a b)"), psum[:, 6, :])

        passed = {e: sem(f"passed_{e}") for e in ("sp", "pe", "act", "pool")}

        def stop_here(eng, name):
            eng.sem_inc(passed[name], 1)

        block = ctx.enter_context(nc.Block())

        @block.sync
        def _(sp):
            for s in range(RING):
                if s == RING - 1:
                    sp.dma_start(x[:, 0, :], x_in[0]).then_inc(x_in_s[0], 16)
                sp.dma_start(ring[:, s, :], walls[s]).then_inc(arrived[s], 16)
            sp.dma_start(bmod1[:, :, :, :], bmod1_in).then_inc(const_in_s, 16)
            sp.dma_start(const[:, :], const_in[:, 0:N_KEPT]).then_inc(const_in_s, 16)
            for t in (1, 2):
                sp.dma_start(x[:, t, :], x_in[t]).then_inc(x_in_s[t], 16)
            sp.dma_start(wide[:, 0:2 * P], const_in[:, N_KEPT:N_CONST]).then_inc(router_in_s, 16)
            sp.dma_start(routw[:, :, :], router_in).then_inc(router_in_s, 16)
            sp.dma_start(broute[:, :], brouter_in.partition_broadcast(P)).then_inc(router_in_s, 16)
            with sp.Fori(0, DEPTH) as L:
                sp.wait_ge(pair_done, L * STAGES + 1)
                stop_here(sp, "sp")
                with sp.If(L > 0):
                    for s in pick_in:
                        sp.wait_ge(s, L * 16)
                    stop_here(sp, "sp")

                def fill(L, turn):
                    for s in range(RING):
                        sp.wait_ge(ring_free, L * ITEMS + turn * RING + (s + 1))
                        sp.dma_start(ring[:, s, :], walls[(L * ITEMS + RING) + turn * RING + s]).then_inc(arrived[s], 16)

                with sp.Fori(0, NEXT0 // RING) as turn:
                    fill(L, turn)
                with sp.If(L < DEPTH - 1):
                    fill(before_last(L), NEXT0 // RING)
                def experts(L, m):
                    return [sp.value_load(tabu[0:1, T_WHO + 2 * m + h:T_WHO + 2 * m + h + 1], min_val=0, max_val=E - 1)
                            + L * E for h in range(2)]

                def load_up(who, buffers):
                    for e, q in zip(who, buffers):
                        sp.dma_start(expert_w[:, q * EXPERT:q * EXPERT + UP], experts_in[e, :, 0:UP]).then_inc(up_in[q], 16)

                def load_down(who, buffers):
                    for e, q in zip(who, buffers):
                        sp.dma_start(expert_w[:, q * EXPERT + UP:(q + 1) * EXPERT], experts_in[e, :, UP:EXPERT])\
                            .then_inc(down_in[q], 16)

                sp.wait_ge(who_ready, L + 1)
                stop_here(sp, "sp")
                who = experts(L, 0)
                load_up(who, (0, 1))
                load_down(who[:1], (0,))
                sp.wait_ge(table_ready, L + 1)
                stop_here(sp, "sp")
                active = sp.value_load(tabu[0:1, T_ACTIVE:T_ACTIVE + 1], min_val=1, max_val=E)
                first = sp.value_load(tabu[0:1, T_FIRST:T_FIRST + 1], min_val=1, max_val=BLOCKS * DEPTH + 1)
                sp.wait_ge(xg_in, (first + L) * 16)
                stop_here(sp, "sp")
                load_down(who[1:], (1,))
                for m in range(1, PAIRS):
                    buffers = [(2 * m + h) % BUFS for h in range(2)]
                    if m > 1:
                        sp.wait_ge(up_used, L * PAIRS + (m - 1))
                        stop_here(sp, "sp")
                    with sp.If(active > 2 * m):
                        who = experts(L, m)
                        if m == 1:
                            sp.wait_ge(xg_in, (first + L + 1) * 16)
                            stop_here(sp, "sp")
                        load_up(who, buffers)
                        if m > 1:
                            sp.wait_ge(pair_done, L * STAGES + (m + 1))
                            stop_here(sp, "sp")
                        load_down(who, buffers)
                    with sp.Else():
                        if m > 1:
                            sp.wait_ge(pair_done, L * STAGES + (m + 1))
                        for q in buffers:
                            sp.sem_inc(up_in[q], 16)
                            sp.sem_inc(down_in[q], 16)

        @block.tensor
        def _(pe):
            def item(L, j):
                pe.wait_ge(arrived[j % RING], (L * (ITEMS // RING) + (j // RING + 2)) * 16)
                return ring[:, j % RING, :]

            def transposes(name, n, src):
                out = bank(name, 2).rearrange("p a b -> p (a b)") if n > 4 else bank(name)
                for k in range(n):
                    ins = pe.transpose(out[:, k * P:(k + 1) * P], src(k), ident)
                produced(ins, name)

            def mod_vector(L, v):
                claim(pe, L, ("mod", v))
                column_groups(bank(("mod", v))[:, 0:256], range(4), lambda g: item(L, MODS0 + 4 * (v - 2) + g))
                pe.drain().then_inc(full[plan[("mod", v)][0]], 1)

            def column_groups(out, groups, items):
                w = [items(g).rearrange("p (k n) -> p k n", k=KC) for g in groups]
                for k in range(KC):
                    for n, g in enumerate(groups):
                        ins = pe.matmul(out[32 * g:32 * g + 32, :], condT[:, k, :], w[n][:, k, :],
                                        start=(k == 0), stop=(k == KC - 1), skip_group_check=True)
                        if k == KC - 1:
                            ins.then_inc(ring_free, 1)

            def first_mods(items, waves):
                column_groups(ps_mod1[:, 0, :], range(4), items)
                for groups in waves:
                    column_groups(ps_mod1[:, 1, :], groups, lambda g: items(4 + g))
                pe.drain().then_inc(mod1_full, 1)

            def first_mods_T(layer):
                pe.wait_ge(mod1_rows, layer + 1)
                for v in range(2):
                    for c in range(2):
                        ins = pe.transpose(ps_mod1T[:, v, c, :], mrow1[:, v, c * P:(c + 1) * P], ident)
                ins.then_inc(mod1T_full, 1)

            def first_item(j):
                pe.wait_ge(arrived[j], 16)
                return ring[:, j, :]

            def project(L, n, w):
                name = ("proj", n)
                piece, part = projected(n)
                if piece not in w:
                    w[piece] = item(L, W_IN0 + piece).rearrange("p (k n) -> p k n", k=KC)
                if n < KEY0 and n % VALUES == 0:
                    await_read(pe, L, ("hT", part))
                claim(pe, L, name)
                for k in range(KC):
                    if n < KEY0:
                        ins = pe.matmul(bank(name)[:, 0:256], hT[:, k, part * P:(part + 1) * P], w[piece][:, k, :],
                                        start=(k == 0), stop=(k == KC - 1))
                    else:
                        ins = pe.matmul(bank(name)[:, 0:T], w[piece][:, k, part * P:(part + 1) * P], hT[:, k, :],
                                        start=(k == 0), stop=(k == KC - 1))
                if part == (TILES if n < KEY0 else 2) - 1:
                    ins.then_inc(ring_free, 1)
                    pe.drain().then_inc(full[plan[name][0]], 1)
                else:
                    produced(ins, name)

            def rope(L, c):
                await_read(pe, L, ("proj", KEY0 + c))
                claim(pe, L, ("rope", c))
                src = kT[:, c, :] if c < 4 else qT[:, c - 4, :]
                ins = pe.matmul(bank(("rope", c))[:, 0:LAT], swap, src[:, P:P + LAT], start=True, stop=True)
                produced(ins, ("rope", c))

            def score(L, i):
                kind, h, t = STEPS[i]
                claim(pe, L, ("score", i))
                if i == 0:
                    pe.wait_ge(roped, L * 8 + 8)
                    await_read(pe, L, "cacheT")
                keys = slice(0, P) if t == 0 else slice(P, P + 384)
                nk = P if t == 0 else 384
                if kind == "da":
                    for m in range(2):
                        r = slice(DH * m, DH * m + DH)
                        ins = pe.matmul(bank(("score", i), 2)[:, m, 0:nk], qT[r, QCH["daq"] + h, t * P:(t + 1) * P],
                                        kT[r, KCH["dak"] + h, keys], start=True, stop=True)
                else:
                    r = slice(DH * (h % 2), DH * (h % 2) + DH)
                    ins = pe.matmul(bank(("score", i))[:, 0:nk], qT[r, QCH["naq"] + h // 2, t * P:(t + 1) * P],
                                    kT[r, KCH["nak"] + h // 2, keys], start=True, stop=True)
                produced(ins, ("score", i))

            def values(kind, h, t, kc):
                w, col = (P, P * h) if kind == "da" else (DH, 512 + DH * h)
                if t == 0:
                    return v_sb[:, 0, col:col + w]
                if kc < 2:
                    return v_sb[:, 1 + kc, col:col + w]
                return cache[:, 768 + col:768 + col + w]

            def prob_transposes(L, i):
                kind, h, t = STEPS[i]
                pe.wait_ge(prob_ready, L * N_STEPS + i + 1)
                claim(pe, L, ("probT", i))
                transposes(("probT", i), 1 if t == 0 else 3, lambda k: probs[:, i % 3, 0, k * P:(k + 1) * P])

            def attend(L, i):
                kind, h, t = STEPS[i]
                name = ("out", kind, h)
                if i == 0:
                    for n in range(KEY0 - 3, KEY0):
                        await_read(pe, L, ("proj", n))
                if t == 0:
                    claim(pe, L, name)
                await_read(pe, L, ("probT", i))
                n = 1 if t == 0 else 3
                for kc in range(n):
                    v = values(kind, h, t, kc)
                    p = probT[:, i % 2, kc, :]
                    if kind == "da":
                        ins = pe.matmul(bank(name)[:, t * P:(t + 1) * P], p, v, start=(kc == 0), stop=(kc == n - 1),
                                        skip_group_check=True)
                    else:
                        r = slice(DH * (h % 2), DH * (h % 2) + DH)
                        ins = pe.matmul(bank(name)[r, t * P:(t + 1) * P], v, p, start=(kc == 0), stop=(kc == n - 1),
                                        skip_group_check=True)
                ins.then_inc(av_done, 1)
                if t == 2:
                    pe.drain().then_inc(full[plan[name][0]], 1)

            def out_proj(L, t):
                name = ("y", t)
                if t == 0:
                    for h in range(DA_HEADS):
                        await_read(pe, L, ("mixT", h))
                        await_read(pe, L, ("out", "na", h))
                    pe.wait_ge(mix_sc, 2 * L + 2)
                claim(pe, L, name)
                y = bank(name, 2).rearrange("p a b -> p (a b)")
                for n in range(4):
                    w = item(L, W_OUT0 + n).rearrange("p (k n) -> p k n", k=KC)
                    for k in range(KC):
                        ins = pe.matmul(y[:, 256 * n:256 * n + 256], mix[:, k, t * P:(t + 1) * P], w[:, k, :],
                                        start=(k == 0), stop=(k == KC - 1), skip_group_check=True)
                    if t == 2:
                        ins.then_inc(ring_free, 1)
                    if t == 2 and n == 1:
                        pe.drain().then_inc(y_half, 1)
                if t == 2:
                    pe.drain().then_inc(full[plan[name][0]], 1)
                else:
                    produced(ins, name)

            def router_T(L, t):
                pe.wait_ge(h2_ready, 3 * L + t + 1)
                claim(pe, L, ("h2T", t))
                transposes(("h2T", t), KC, lambda k: h2[:, t, :].rearrange("p (a k) -> p a k", k=KC)[:, :, k])

            def router(L, t):
                await_read(pe, L, ("h2T", t))
                claim(pe, L, ("logit", t))
                for k in range(KC):
                    ins = pe.matmul(bank(("logit", t))[:, 0:E], hT[:, k, t * P:(t + 1) * P], routw[:, k, :],
                                    start=(k == 0), stop=(k == KC - 1))
                produced(ins, ("logit", t))

            def tokens_T(L, i):
                pe.wait_ge(xg_in, (i + L) * 16)
                pe.wait_ge(xT_ready, i + L)
                for k in range(KC):
                    ins = pe.transpose(psA[:, k * P:(k + 1) * P],
                                       xg.rearrange("p (a k) -> p a k", k=KC)[:, :, k], ident)
                ins.then_inc(xT_full, 1)

            def up(L, i, w):
                pe.wait_ge(xT_ready, i + L + 1)
                pe.wait_ge(hid_ready, i)
                for k in range(KC):
                    for h in range(2):
                        ins = pe.matmul(psD[HALF * h:HALF * h + HALF, :],
                                        xT[:, k * P + HALF * h:k * P + HALF * h + HALF],
                                        w[h][:, 2 * DE * k:2 * DE * k + 2 * DE],
                                        start=(k == 0), stop=(k == KC - 1), skip_group_check=True)
                ins.then_inc(up_full, 1)

            def hidden_T(i):
                pe.wait_ge(hid_ready, i + 1)
                for k in range(2):
                    ins = pe.transpose(psB[:, k * P:(k + 1) * P], hid[:, k * P:(k + 1) * P], ident)
                ins.then_inc(hidT_full, 1)

            def down(after, w, n):
                pe.wait_ge(hidT_ready, after)
                pe.wait_ge(yo_ready, after)
                for k in range(2):
                    for h in range(2):
                        ins = pe.matmul(psC[HALF * h:HALF * h + HALF, 512 * n:512 * n + 512],
                                        hidT[:, k * P + HALF * h:k * P + HALF * h + HALF],
                                        w[h][:, UP + D * k + 512 * n:UP + D * k + 512 * n + 512],
                                        start=(k == 0), stop=(k == 1), skip_group_check=True)
                if n == 1:
                    ins.then_inc(down_full, 1)

            def buffers(odd):
                return [expert_w[:, q * EXPERT:(q + 1) * EXPERT] for q in (2 * odd, 2 * odd + 1)]

            def stage(L, two, odd):
                w, last_w = buffers(odd), buffers(1 - odd)
                load = lambda at, low, high: pe.value_load(tabu[0:1, bass.ds(two * 2 + (at + odd), 1)], min_val=low, max_val=high)
                start = load(T_START, 1, BLOCKS * DEPTH + 1)
                blocks = load(T_BLOCKS, 0, T // HALF)
                before = load(T_BLOCKS - 1, 0, T // HALF)
                for h in range(2):
                    pe.wait_ge(up_in[2 * odd + h], (L * (E // BUFS) + two + 1) * 16)
                with pe.If(blocks > 0):
                    up(L, start, w)
                with pe.If(blocks < 2):
                    pe.drain().then_inc(up_used, 1)
                with pe.If(before > 0):
                    for h in range(2):
                        pe.wait_ge(down_in[2 * (1 - odd) + h], (L * (E // BUFS) + two + odd) * 16)
                    for n in range(2):
                        down(start, last_w, n)
                pe.drain().then_inc(pair_done, 1)
                with pe.If(blocks > 0):
                    tokens_T(L, start + 1)
                    hidden_T(start)
                    with pe.If(blocks > 1):
                        for h in range(2):
                            pe.wait_ge(down_in[2 * odd + h], (L * (E // BUFS) + two + 1) * 16)
                        stop_here(pe, "pe")
                        with pe.Fori(1, blocks) as j:
                            up(L, start + j, w)
                            down(start + j, w, 0)
                            tokens_T(L, start + j + 1)
                            down(start + j, w, 1)
                            hidden_T(start + j)
                        pe.drain().then_inc(up_used, 1)

            for s in SLOT_BANK:
                pe.sem_inc(free[s], 1)
            for s in (pair_done, xT_full, up_full, hidT_full, down_full):
                pe.sem_inc(s, 1)
            pe.wait_ge(cond_ready, 2)
            first_mods(first_item, ((0, 1, 2), (3,)))
            pe.wait_ge(const_in_s, 32)
            first_mods_T(0)
            with pe.Fori(0, DEPTH) as L:
                w = {}
                for kind, n in projection_order():
                    if kind == "hT":
                        pe.wait_ge(pre_xn, 3 * L + n + 1)
                        claim(pe, L, (kind, n))
                        transposes((kind, n), KC, lambda k: xn[:, n, :].rearrange("p (a k) -> p a k", k=KC)[:, :, k])
                    elif kind == "rope":
                        rope(L, n)
                    else:
                        project(L, n, w)
                pe.wait_ge(layer_in_s, (L + 1) * 16 * 5)
                claim(pe, L, "cacheT")
                transposes("cacheT", 6, lambda c: cache[:, c * P:(c + 1) * P])
                for n in range(KEY0 + 9, KEY0 + 12):
                    await_read(pe, L, ("proj", n))
                claim(pe, L, "kout")
                transposes("kout", 6, lambda c: kT[:, c, 0:P])
                score(L, 0)
                score(L, 1)
                mixes = 0
                for i, (kind, h, t) in enumerate(STEPS):
                    if i + 2 < N_STEPS:
                        score(L, i + 2)
                    prob_transposes(L, i)
                    if i > 0:
                        attend(L, i - 1)
                        if STEPS[i - 1][0] == "da" and STEPS[i - 1][2] == 2:
                            mod_vector(L, 2 + STEPS[i - 1][1])
                    if mixes < DA_HEADS and i == 3 * mixes + 2 + MIX_DELAY:
                        pe.wait_ge(on_ready, 4 * L + mixes + 1)
                        claim(pe, L, ("mixT", mixes))
                        transposes(("mixT", mixes), 3, lambda k: on[:, k, :])
                        mixes += 1
                attend(L, N_STEPS - 1)
                for t in range(TILES):
                    out_proj(L, t)
                with pe.If(L < DEPTH - 1):
                    claim(pe, L, ("logit", 0))
                    first_mods(lambda j: item(L, NEXT0 + j), (range(4),))
                router_T(L, 0)
                router_T(L, 1)
                with pe.If(L < DEPTH - 1):
                    claim(pe, L, ("logit", 1))
                    first_mods_T(L + 1)
                pe.wait_ge(router_in_s, 48)
                router(L, 0)
                with pe.If(L < DEPTH - 1):
                    pe.wait_ge(mod1_ready, L + 2)
                    stop_here(pe, "pe")
                router(L, 1)
                router_T(L, 2)
                router(L, 2)
                pe.wait_ge(constb_ready, 3)
                pe.wait_ge(mask_ready, L + 1)
                claim(pe, L, "place")
                place = bank("place")
                for t in range(TILES):
                    for s in range(t + 1):
                        pe.matmul(place[:, t * E:(t + 1) * E], ones if s < t else utri, maskb[:, s * E:(s + 1) * E],
                                  start=(s == 0), stop=(s == t), skip_group_check=True)
                for t in range(TILES):
                    ins = pe.matmul(place[:, TILES * E:TILES * E + E], ones, maskb[:, t * E:(t + 1) * E],
                                    start=(t == 0), stop=(t == TILES - 1), skip_group_check=True)
                produced(ins, "place")
                pe.wait_ge(sel_ready, L + 1)
                claim(pe, L, "index")
                for n in range(2 * TILES):
                    ins = pe.matmul(bank("index")[:, 0:2 * COLS], sel[:, n, :],
                                    where[:, n, :, :].rearrange("p a b -> p (a b)"),
                                    start=(n == 0), stop=(n == 2 * TILES - 1))
                produced(ins, "index")
                pe.wait_ge(table_ready, L + 1)
                stop_here(pe, "pe")
                first = pe.value_load(tabu[0:1, T_FIRST:T_FIRST + 1], min_val=1, max_val=BLOCKS * DEPTH + 1)
                tokens_T(L, first)
                with pe.Fori(0, PAIRS // 2) as two:
                    for odd in range(2):
                        stage(L, two, odd)
                end = pe.value_load(tabu[0:1, T_LAST:T_LAST + 1], min_val=2, max_val=BLOCKS * DEPTH + 1)
                before = pe.value_load(tabu[0:1, T_BLOCKS + PAIRS - 1:T_BLOCKS + PAIRS], min_val=0, max_val=T // HALF)
                with pe.If(before > 0):
                    for h in range(2):
                        pe.wait_ge(down_in[2 + h], (L + 1) * (E // BUFS) * 16)
                    for n in range(2):
                        down(end, buffers(1), n)
                pe.drain().then_inc(pair_done, 1)

        @block.scalar
        def _(act):
            restart, link = chain(act, act_done)
            copy = ACT.Copy

            def pre_normalise(layer, t):
                act.wait_ge(pre_rstd, 3 * layer + t + 1)
                act.activation(xn[:, t, :], x[:, t, :], ACT.Identity, scale=lnv[:, 3 + t, 1:2],
                               bias=lnv[:, 3 + t, 2:3]).then_inc(pre_xn, 1)

            def normalise(L, n, src, dst):
                act.wait_ge(rstd_ready, 9 * L + n - 2)
                act.activation(dst, src, ACT.Identity, scale=lnv[:, n % 3, 1:2],
                               bias=lnv[:, n % 3, 2:3]).then_inc(xn_ready, 1)

            def modulated(t, first_k):
                src, c = bank(("hT", t), 2).rearrange("p a b -> p (a b)"), min(t, 1)
                for k in range(first_k, KC):
                    ins = act.activation(hT[:, k, t * P:(t + 1) * P], src[:, k * P:(k + 1) * P],
                                         ACT.Identity, scale=modT[:, c, 1, k:k + 1], bias=modT[:, c, 0, k:k + 1])
                return ins

            def modulate_first(layer):
                act.wait_ge(mod1_ready, layer + 1)
                await_product(act, layer, ("hT", 0))
                read_out(modulated(0, 0), ("hT", 0))

            def project_out(L, n):
                name = ("proj", n)
                item, part = projected(n)
                piece, piece_half = PIECES[item]
                await_product(act, L, name)
                if piece in V_COL:
                    col = V_COL[piece] + 256 * piece_half
                    ins = act.activation(v_sb[:, part, col:col + 256], bank(name)[:, 0:256], copy)
                elif piece in KCH:
                    ins = act.activation(kT[:, KCH[piece] + 2 * piece_half + part, 0:T], bank(name)[:, 0:T], copy)
                else:
                    ins = act.activation(qT[:, QCH[piece] + 2 * piece_half + part, :], bank(name)[:, 0:T], copy,
                                         scale=SCALE if piece in ("daq", "naq") else 1.0)
                read_out(ins, name)

            act.dma_start(condv[:, :, :], cond_in).then_inc(cond_in_s, 16)
            act.wait_ge(cond_in_s, 16)
            act.activation(conds[:, 0, :, :], condv[:, :, :], ACT.Exp, scale=-1.0).then_inc(cond_exp, 1)
            for s in (xT_ready, up_exp, hidT_ready):
                act.sem_inc(s, 1)
            act.sem_inc(yo_ready, 2)
            act.sem_inc(yo_stored, 32)
            act.sem_inc(state_out, 16)
            pre_normalise(0, 0)
            modulate_first(0)
            pre_normalise(0, 1)
            pre_normalise(0, 2)
            with act.Fori(0, DEPTH) as L:
                restart()
                for kind, n in projection_order():
                    if kind == "hT" and n > 0:
                        await_product(act, L, (kind, n))
                        modulated(n, KC // 2).then_inc(hT_second, 1)
                    elif kind == "proj":
                        project_out(L, n)
                act.wait_ge(lam_dot, 2 * L + 2)
                act.activation(lams[:, 2:4], lams[:, 0:2], ACT.Exp).then_inc(lam_exp, 1)
                await_product(act, L, "cacheT")
                read_out(act.activation(kT[:, :, 384:512], bank("cacheT", 2).rearrange("p a b -> p (a b)")[:, 0:768]
                                        .rearrange("p (c t) -> p c t", c=6), copy), "cacheT")
                await_product(act, L, "kout")
                read_out(act.activation(kout[:, :], bank("kout", 2).rearrange("p a b -> p (a b)")[:, 0:768], copy), "kout")
                await_read(act, L, "kout")
                act.dma_start(new_da_k[L], kout[:, 0:512]).then_inc(state_out, 16)
                act.dma_start(new_na_k[L], kout[:, 512:768]).then_inc(state_out, 16)
                act.dma_start(new_da_v[L], v_sb[:, 0, 0:512]).then_inc(state_out, 16)
                act.dma_start(new_na_v[L], v_sb[:, 0, 512:768]).then_inc(state_out, 16)

                def exps(i):
                    kind, h, t = STEPS[i]
                    nk = P if t == 0 else 384
                    act.wait_ge(max_ready, N_STEPS * L + i + 1)
                    if i >= 3:
                        await_product(act, L, ("probT", i - 3))
                    n = 2 if kind == "da" else 1
                    for m in range(n):
                        src = bank(("score", i), 2)[:, m, 0:nk]
                        ins = act.activation(probs[:, i % 3, m, 0:nk], src, ACT.Exp, bias=mxs[:, i % 3, m:m + 1],
                                             accum_out=rsum[:, i % 3, m:m + 1])
                    read_out(ins, ("score", i))

                def probT_out(i):
                    kind, h, t = STEPS[i]
                    n = 1 if t == 0 else 3
                    name = ("probT", i)
                    await_product(act, L, name)
                    if i >= 2:
                        act.wait_ge(av_done, N_STEPS * L + i - 1)
                    read_out(act.activation(probT[:, i % 2, 0:n, :],
                                            bank(name)[:, 0:n * P].rearrange("p (k t) -> p k t", k=n), copy), name)

                def head_out(i):
                    kind, h, t = STEPS[i]
                    name = ("out", kind, h)
                    await_product(act, L, name)
                    if kind == "da":
                        if h:
                            act.wait_ge(on_ready, 4 * L + h)
                        read_out(act.activation(osb[:, :, :], bank(name)[:, 0:T].rearrange("p (t d) -> p t d", t=TILES),
                                                copy), name)
                        await_read(act, L, name)
                        for u in range(TILES):
                            ins = act.activation(sq[:, u, :], osb[:, u, :], ACT.Square, accum_out=msr[:, 0, u:u + 1])
                        ins.then_inc(ms_ready, 1)
                    else:
                        r = slice(DH * (h % 2), DH * (h % 2) + DH)
                        read_out(act.activation(mix[r, h // 2, :], bank(name)[r, 0:T], copy), name)

                def mod_store(h):
                    act.wait_ge(mrow_ready, 4 * L + h + 1)
                    for c in range(2):
                        act.dma_start(mod_d[c, h, :].rearrange("(g n) -> g n", g=4),
                                      mrow[c:c + 97:32, h, :]).then_inc(mod_stored, 16)

                exps(0)
                mixes = 0
                for i in range(N_STEPS):
                    if i + 1 < N_STEPS:
                        exps(i + 1)
                    probT_out(i)
                    if i % 3 == 0 and i > 0:
                        head_out(i - 1)
                    if i % 3 == 1 and i // 3 in range(1, DA_HEADS + 1):
                        mod_store(i // 3 - 1)
                    if mixes < DA_HEADS and i == 3 * mixes + 2 + MIX_DELAY:
                        name = ("mixT", mixes)
                        await_product(act, L, name)
                        read_out(act.activation(mix[:, 4 + mixes, :], bank(name)[:, 0:T], copy), name)
                        mixes += 1
                head_out(N_STEPS - 1)

                def h2T_out(t):
                    name = ("h2T", t)
                    await_product(act, L, name)
                    read_out(act.activation(hT[:, :, t * P:(t + 1) * P],
                                            bank(name, 2).rearrange("p a (b q) -> p (a b) q", q=P), copy), name)
                    act.wait_ge(h2_ready, 3 * L + t + 1)
                    act.dma_start(h2_d[t * P:(t + 1) * P, :], h2[:, t, :]).then_inc(h2_stored, 16)

                def logit_exps(t):
                    name = ("logit", t)
                    await_product(act, L, name)
                    read_out(act.activation(rt[:, 0, t * E:(t + 1) * E], bank(name)[:, 0:E], ACT.Exp, scale=-1.0), name)

                def post_norm(t):
                    normalise(L, 3 + 2 * t, x[:, t, :], x[:, t, :])

                def pre_norm(t):
                    normalise(L, 4 + 2 * t, x[:, t, :], h2[:, t, :])

                post_norm(0)
                pre_norm(0)
                post_norm(1)
                pre_norm(1)
                post_norm(2)
                h2T_out(0)
                pre_norm(2)
                h2T_out(1)
                logit_exps(0)
                logit_exps(1)
                h2T_out(2)
                logit_exps(2)

                act.wait_ge(table_ready, L + 1)
                stop_here(act, "act")
                first = act.value_load(tabu[0:1, T_FIRST:T_FIRST + 1], min_val=1, max_val=BLOCKS * DEPTH + 1)
                count = act.value_load(tabu[0:1, T_COUNT:T_COUNT + 1], min_val=1, max_val=BLOCKS)

                def tokens_out(i):
                    act.wait_ge(xT_full, i + L + 1)
                    act.wait_ge(up_full, i)
                    act.activation(xT, psA, copy).then_inc(xT_ready, 1)

                def up_exps(i):
                    act.wait_ge(up_full, i + 1)
                    act.wait_ge(hid_ready, i)
                    act.activation(silu, psD[:, 0:DE], ACT.Exp, scale=-1.0).then_inc(up_exp, 1)

                def hidden_out(i):
                    act.wait_ge(hidT_full, i + 1)
                    act.wait_ge(down_full, i)
                    act.activation(hidT, psB[:, 0:DE], copy).then_inc(hidT_ready, 1)

                def block_out(after, j):
                    act.wait_ge(down_full, after)
                    act.wait_ge(yo_stored, after * 16)
                    act.activation(yo, psC, copy).then_inc(yo_ready, 1)
                    act.wait_ge(yo_ready, after + 1)
                    act.dma_start(moe_d[bass.ds(j * P, P), :], yo).then_inc(yo_stored, 16)

                tokens_out(first)
                up_exps(first)
                tokens_out(first + 1)
                hidden_out(first)
                with act.If(count > 1):
                    with act.Fori(1, count) as j:
                        up_exps(first + j)
                        tokens_out(first + j + 1)
                        block_out(first + j, j - 1)
                        hidden_out(first + j)
                block_out(first + count, count - 1)
                act.wait_ge(gates_ready, L + 1)
                for t in range(TILES):
                    act.wait_ge(pick_in[2 * t], 16 * (L + 1))
                    act.activation(fetched[2 * t], fetched[2 * t], copy, scale=gates[:, 0, t:t + 1]).then_inc(first_gated, 1)
                normalise(L, 9, x[:, 0, :], x[:, 0, :])
                normalise(L, 10, x[:, 1, :], x[:, 1, :])
                with act.If(L < DEPTH - 1):
                    pre_normalise(L + 1, 0)
                    modulate_first(L + 1)
                normalise(L, 11, x[:, 2, :], x[:, 2, :])
                with act.If(L < DEPTH - 1):
                    for t in (1, 2):
                        pre_normalise(L + 1, t)
            for t in range(TILES):
                act.wait_ge(gained, 6 * (DEPTH - 1) + 3 + t + 2)
                act.dma_start(y_prompt if t == 0 else y_sample[(t - 1) * P:t * P, :], x[:, t, :]).then_inc(x_out, 16)
            act.wait_ge(x_out, 48)
            act.wait_ge(state_out, 64 * DEPTH + 16)

        @block.vector
        def _(dve):
            restart, link = chain(dve, dve_done)
            tt, ts, stt = dve.tensor_tensor, dve.tensor_scalar, dve.scalar_tensor_tensor

            def norm_stats(L, n, src):
                for half_n in range(2):
                    ins = dve.bn_stats(stats[:, n % 3, half_n, :], src[:, 512 * half_n:512 * half_n + 512])
                    link(ins)
                dve.bn_aggr(mv[:, n % 3, :], stats[:, n % 3, :, :].rearrange("p a b -> p (a b)")).then_inc(stats_ready, 1)

            def pre_stats(t):
                for half_n in range(2):
                    ins = dve.bn_stats(stats[:, 3 + t, half_n, :], x[:, t, 512 * half_n:512 * half_n + 512])
                    link(ins)
                dve.bn_aggr(mv[:, 3 + t, :], stats[:, 3 + t, :, :].rearrange("p a b -> p (a b)")).then_inc(pre_mv, 1)

            def mod_out(L, v):
                name = ("mod", v)
                if v == 2:
                    dve.wait_ge(bmod_in_s, 64 * (L + 1))
                await_product(dve, L, name)
                link(tt(mrow[:, v - 2, :], bank(name)[:, 0:256], mrow[:, v - 2, :], ALU.add))
                dve.sem_inc(free[plan[name][0]], 1)
                dve.sem_inc(mrow_ready, 1)

            link(dve.memset(tab[:, :], 1.0))
            link(dve.memset(tab[:, T_NONE:T_NONE + 1], 0.0))
            dve.sem_inc(hid_ready, 1)
            dve.sem_inc(gained, 1)
            dve.sem_inc(silu_step, 3)
            link(dve.memset(condT[:, :, :], 0.0))
            link(dve.memset(half[:, 0:3], -0.5))
            dve.memset(half[:, 3:4], EPS).then_inc(cond_ready, 1)
            dve.wait_ge(cond_in_s, 16)
            dve.wait_ge(cond_exp, 1)
            link(ts(conds[:, 1, :, :], conds[:, 0, :, :], 1.0, None, ALU.add))
            link(dve.reciprocal(conds[:, 0, :, :], conds[:, 1, :, :]))
            tt(condT[:, :, 0:2], condv[:, :, :].rearrange("p c k -> p k c"),
               conds[:, 0, :, :].rearrange("p c k -> p k c"), ALU.mult).then_inc(cond_ready, 1)
            dve.wait_ge(x_in_s[0], 16)
            pre_stats(0)

            def first_mods_rows(layer):
                dve.wait_ge(mod1_full, layer + 1)
                dve.tensor_copy(mrow1[:, :, :], ps_mod1).then_inc(mod1_rows, 1)

            def first_mods_out(layer, b):
                dve.wait_ge(mod1T_full, layer + 1)
                for c in range(2):
                    for v in range(2):
                        ins = tt(modT[:, c, v, :].rearrange("p (g h) -> p g h", h=2),
                                 ps_mod1T[:, v, :, c::32].rearrange("p h g -> p g h"),
                                 b[:, v, :].rearrange("p (g h) -> p g h", h=2), ALU.add)
                ins.then_inc(mod1_biased, 1)
                dve.wait_ge(mod1_biased, layer + 1)
                ts(modT[:, :, 1, :], modT[:, :, 1, :], 1.0, None, ALU.add).then_inc(mod1_ready, 1)

            first_mods_rows(0)
            dve.wait_ge(const_in_s, 32)
            first_mods_out(0, bmod1[:, 0, :, :])
            for t in (1, 2):
                dve.wait_ge(x_in_s[t], 16)
                pre_stats(t)
            dve.wait_ge(router_in_s, 48)
            dve.tensor_copy(constb[:, 0:P], wide[:, 0:P]).then_inc(constb_ready, 1)
            dve.memset(constb[:, P:2 * P], 1.0).then_inc(constb_ready, 1)
            dve.tensor_copy(constb[:, 2 * P:3 * P], wide[:, P:2 * P]).then_inc(constb_ready, 1)
            dve.wait_ge(constb_ready, 3)

            with dve.Fori(0, DEPTH) as L:
                restart()
                dve.wait_ge(mod1_ready, L + 1)
                for t in (1, 2):
                    name = ("hT", t)
                    await_product(dve, L, name)
                    c = min(t, 1)
                    for k in range(KC // 2):
                        ins = ts(hT[:, k, t * P:(t + 1) * P], bank(name, 2).rearrange("p a b -> p (a b)")[:, k * P:(k + 1) * P],
                                 modT[:, c, 1, k:k + 1], modT[:, c, 0, k:k + 1], ALU.mult, ALU.add)
                    link(ins)
                    dve.wait_ge(hT_second, 2 * L + t)
                    dve.sem_inc(free[plan[name][0]], 1)
                dve.wait_ge(layer_in_s, (L + 1) * 16 * 5)
                link(tt(wide[:, 0:128].rearrange("p (a b) -> p a b", a=2), lamv[:, 0:3:2, :], lamv[:, 1:4:2, :], ALU.mult))
                for a in range(2):
                    dve.tensor_reduce(lams[:, a:a + 1], wide[:, 64 * a:64 * a + 64], AX.X, ALU.add).then_inc(lam_dot, 1)
                dve.wait_ge(lam_dot, 2 * L + 2)
                for c in range(8):
                    name = ("rope", c)
                    await_product(dve, L, name)
                    src = (kT[:, c, :] if c < 4 else qT[:, c - 4, :])[:, P:P + LAT]
                    ins = tt(wide[:, 0:LAT], bank(name)[:, 0:LAT], sin_t, ALU.mult)
                    read_out(ins, name)
                    link(tt(src, src, cos_t, ALU.mult))
                    tt(src, src, wide[:, 0:LAT], ALU.add).then_inc(roped, 1)
                    dve.wait_ge(roped, 8 * L + c + 1)
                dve.wait_ge(lam_exp, L + 1)
                link(tt(lams[:, 4:5], lams[:, 2:3], lams[:, 3:4], ALU.subtract))
                link(tt(lams[:, 5:6], lams[:, 4:5], lamc[:, 0:1], ALU.add))
                link(ts(gain[:, :], gain[:, :], lamc[:, 1:2], None, ALU.mult))

                def row_max(i):
                    kind, h, t = STEPS[i]
                    nk = P if t == 0 else 384
                    name = ("score", i)
                    await_product(dve, L, name)
                    if kind == "da":
                        ins = dve.tensor_reduce(mxs[:, i % 3, :], bank(name, 2)[:, :, 0:nk], AX.X, ALU.max, negate=True)
                    else:
                        if t > 0:
                            if h == 0 and t == 1:
                                dve.wait_ge(bias_ready, L + 1)
                            s0 = 2 - 2 * (t - 1)
                            link(tt(bank(name)[:, 0:LAT], bank(name)[:, 0:LAT],
                                    bias[:, h, s0:s0 + 4, :].rearrange("p a b -> p (a b)"), ALU.add))
                        ins = dve.tensor_reduce(mxs[:, i % 3, 0:1], bank(name)[:, 0:nk], AX.X, ALU.max, negate=True)
                    ins.then_inc(max_ready, 1)

                def probabilities(i):
                    kind, h, t = STEPS[i]
                    nk = P if t == 0 else 384
                    await_read(dve, L, ("score", i))
                    p = probs[:, i % 3, :, 0:nk]
                    r = rinv[:, i % 3, :]
                    if kind == "da":
                        link(dve.reciprocal(r[:, 0:2], rsum[:, i % 3, :]))
                        link(tt(r[:, 2:3], r[:, 1:2], lams[:, 5:6], ALU.mult))
                        link(ts(p[:, 1, :], p[:, 1, :], r[:, 2:3], None, ALU.mult))
                        stt(p[:, 0, :], p[:, 0, :], r[:, 0:1], p[:, 1, :], ALU.mult, ALU.subtract).then_inc(prob_ready, 1)
                    else:
                        link(dve.reciprocal(r[:, 0:1], rsum[:, i % 3, 0:1]))
                        ts(p[:, 0, :], p[:, 0, :], r[:, 0:1], None, ALU.mult).then_inc(prob_ready, 1)

                def head_scale(h):
                    dve.wait_ge(rms_ready, 4 * L + h + 1)
                    if h:
                        await_product(dve, L, ("mixT", h - 1))
                    for t in range(TILES):
                        ins = stt(on[:, t, :], osb[:, t, :], msr[:, 2, t:t + 1], gain[:, :], ALU.mult, ALU.mult)
                    link(ins)
                    dve.sem_inc(on_ready, 1)

                def conv(c):
                    z, o = wide[:, 0:T], wide[:, T:2 * T]
                    link(tt(z, qT[:, QCH["scc"] + c, :], qT[:, QCH["scx"] + c, :], ALU.mult))
                    link(ts(o, z, convp[:, c, 1:2], convp[:, c, 3:4], ALU.mult, ALU.add))
                    for a, b in ((0, P), (P, T)):
                        link(stt(o[:, a + 1:b], z[:, a:b - 1], convp[:, c, 0:1], o[:, a + 1:b], ALU.mult, ALU.add))
                        link(stt(o[:, a:b - 1], z[:, a + 1:b], convp[:, c, 2:3], o[:, a:b - 1], ALU.mult, ALU.add))
                    link(tt(mix[:, 2 + c, :], o, qT[:, QCH["scb"] + c, :], ALU.mult))
                    dve.sem_inc(mix_sc, 1)

                row_max(0)
                row_max(1)
                for i in range(N_STEPS):
                    probabilities(i)
                    if i % 3 == 1 and i // 3 in range(1, DA_HEADS + 1):
                        mod_out(L, 2 + i // 3 - 1)
                    if i + 2 < N_STEPS:
                        row_max(i + 2)
                    if i in (3, 6):
                        conv(i // 3 - 1)
                    if i % 3 == 2 and i // 3 in range(1, DA_HEADS + 1):
                        head_scale(i // 3 - 1)

                def residual(t, tmp):
                    ins = stt(x[:, t, :], x[:, t, :], ALPHA, tmp, ALU.mult, ALU.add)
                    link(ins)

                dve.wait_ge(gate1_in, 16 * (L + 1))

                def gain_bias(t):
                    link(tt(x[:, t, :], x[:, t, :], ln_b[:, 0, :], ALU.mult))
                    link(tt(x[:, t, :], x[:, t, :], ln_b[:, 1, :], ALU.add))
                    dve.sem_inc(gained, 1)

                def first_residual(t):
                    name = ("y", t)
                    await_product(dve, L, name)
                    ins = tt(wide[:, 0:D], bank(name, 2).rearrange("p a b -> p (a b)"), gate_b[:, min(t, 1), :], ALU.mult)
                    read_out(ins, name)
                    await_read(dve, L, name)
                    residual(t, wide[:, 0:D])
                    norm_stats(L, 3 + 2 * t, x[:, t, :])

                def last_residual(half_n):
                    name, t = ("y", 2), 2
                    if half_n == 0:
                        dve.wait_ge(y_half, L + 1)
                    else:
                        await_product(dve, L, name)
                    c = slice(512 * half_n, 512 * half_n + 512)
                    ins = tt(wide[:, c], bank(name, 2)[:, half_n, :], gate_b[:, 1, c], ALU.mult)
                    if half_n == 0:
                        link(ins)
                    else:
                        read_out(ins, name)
                        await_read(dve, L, name)
                    link(stt(x[:, t, c], x[:, t, c], ALPHA, wide[:, c], ALU.mult, ALU.add))
                    link(dve.bn_stats(stats[:, (3 + 2 * t) % 3, half_n, :], x[:, t, c]))
                    if half_n == 1:
                        dve.bn_aggr(mv[:, (3 + 2 * t) % 3, :], stats[:, (3 + 2 * t) % 3, :, :].rearrange("p a b -> p (a b)"))\
                            .then_inc(stats_ready, 1)

                def first_gain(t):
                    dve.wait_ge(xn_ready, 9 * L + 1 + 2 * t)
                    gain_bias(t)
                    norm_stats(L, 4 + 2 * t, x[:, t, :])

                def modulate(t):
                    dve.wait_ge(xn_ready, 9 * L + 2 + 2 * t)
                    link(stt(h2[:, t, :], mod2_b[:, min(t, 1), 1, :], 1.0, h2[:, t, :], ALU.add, ALU.mult))
                    tt(h2[:, t, :], h2[:, t, :], mod2_b[:, min(t, 1), 0, :], ALU.add).then_inc(h2_ready, 1)

                dve.wait_ge(ln_in_s, (2 * L + 1) * 16)
                first_residual(0)
                first_gain(0)
                dve.wait_ge(mod2_in, 16 * (L + 1))
                modulate(0)
                first_residual(1)
                last_residual(0)
                first_gain(1)
                last_residual(1)
                modulate(1)
                first_gain(2)
                with dve.If(L < DEPTH - 1):
                    first_mods_rows(L + 1)
                    first_mods_out(L + 1, bmod1[:, bass.ds(before_last(L) + 1, 1), :, :].rearrange("p u v k -> p (u v) k"))
                modulate(2)

                def v16(n):
                    return rt[:, n, :]

                def v44(n):
                    return rt[:, n, :].rearrange("p (g j) -> p g j", j=4)

                def ranks(val, n_out):
                    n = val.shape[1]
                    vi = val.rearrange("p (g u i) -> p g u i", u=1, i=4).broadcast_to([P, n // 4, 4, 4])
                    vj = val.rearrange("p (g j u) -> p g j u", j=4, u=1).broadcast_to([P, n // 4, 4, 4])
                    pa = pair[:, 0, 0:4 * n].rearrange("p (g j i) -> p g j i", j=4, i=4)
                    pb = pair[:, 1, 0:4 * n].rearrange("p (g j i) -> p g j i", j=4, i=4)
                    lt = const[:, C_LT4:C_LT4 + 16].rearrange("p (g j i) -> p g j i", g=1, i=4).broadcast_to([P, n // 4, 4, 4])
                    link(tt(pa, vi, vj, ALU.is_gt))
                    link(tt(pb, vi, vj, ALU.is_equal))
                    link(tt(pb, pb, lt, ALU.mult))
                    link(tt(pa, pa, pb, ALU.add))
                    link(dve.tensor_reduce(n_out, pa, AX.X, ALU.add))

                for t in range(TILES):
                    await_read(dve, L, ("logit", t))
                link(ts(v16(1), v16(0), 1.0, None, ALU.add))
                link(dve.reciprocal(v16(2), v16(1)))
                link(tt(v16(3).rearrange("p (t e) -> p t e", t=TILES), v16(2).rearrange("p (t e) -> p t e", t=TILES),
                        broute[:, :].rearrange("p (u e) -> p u e", u=1).broadcast_to([P, TILES, E]), ALU.add))
                ranks(v16(3), v44(4))
                link(ts(v16(4), v16(4), 2.0, None, ALU.is_lt))
                link(tt(v16(5), v16(4), v16(3), ALU.mult))
                link(dve.tensor_reduce(rt[:, 6, 0:TILES * GROUPS], v44(5), AX.X, ALU.add))
                ranks(rt[:, 6, 0:TILES * GROUPS], rt[:, 7, 0:TILES * GROUPS].rearrange("p (t g) -> p t g", g=4))
                link(ts(rt[:, 7, 0:TILES * GROUPS], rt[:, 7, 0:TILES * GROUPS], 1.0, None, ALU.is_lt))
                link(tt(v44(8), v44(4), rt[:, 7, 0:TILES * GROUPS].rearrange("p (g u) -> p g u", u=1)
                        .broadcast_to([P, TILES * GROUPS, 4]), ALU.mult))
                dve.tensor_copy(maskb[:, :], v16(8)).then_inc(mask_ready, 1)
                link(tt(v16(9), v16(8), v16(2), ALU.mult))
                link(dve.tensor_reduce(st[:, 0:3], v16(9).rearrange("p (t e) -> p t e", t=TILES), AX.X, ALU.add))
                link(dve.reciprocal(st[:, 3:6], st[:, 0:3]))
                link(tt(v16(9).rearrange("p (t e) -> p t e", t=TILES), v16(9).rearrange("p (t e) -> p t e", t=TILES),
                        st[:, 3:6].rearrange("p (t u) -> p t u", u=1).broadcast_to([P, TILES, E]), ALU.mult))
                await_product(dve, L, "place")
                tokens = rt[:, 2, 0:E]
                read_out(dve.tensor_copy(rt[:, :, :].rearrange("p n e -> p (n e)")[:, TILES * E:(2 * TILES + 1) * E],
                                         bank("place")[:, 0:(TILES + 1) * E]), "place")
                await_read(dve, L, "place")

                def rows(ap, n):
                    return ap.rearrange("p (u e) -> p u e", u=1).broadcast_to([P, n, E])

                def cols(ap, n):
                    return ap.rearrange("p (e u) -> p e u", u=1).broadcast_to([P, ap.shape[1], n])

                def grid(b, n, m):
                    return pair[:, b, 0:n * m].rearrange("p (a b) -> p a b", a=n)

                prev = const[:, C_PREV:C_PREV + E * E].rearrange("p (a b) -> p a b", a=E)
                num = const[:, C_NUM:C_NUM + 32]
                halves, rank, by_rank = (rt[:, 11, E * n:E * n + E] for n in range(3))
                base, bases, first_row = (rt[:, 12, E * n:E * n + E] for n in range(3))
                key = rt[:, 15, 0:E]
                link(tt(grid(0, E, 6), cols(tokens, 6),
                        const[:, C_HALF:C_HALF + 6].rearrange("p (u j) -> p u j", u=1).broadcast_to([P, E, 6]), ALU.is_gt))
                link(dve.tensor_reduce(halves, grid(0, E, 6), AX.X, ALU.add))
                link(stt(key, num[:, 0:E], -1.0 / (2 * E), halves, ALU.mult, ALU.add))
                link(tt(grid(0, E, E), rows(key, E), cols(key, E), ALU.is_gt))
                link(dve.tensor_reduce(rank, grid(0, E, E), AX.X, ALU.add))
                link(tt(grid(1, E, E), rows(rank, E), cols(num[:, 0:E], E), ALU.is_equal))
                link(tt(grid(0, E, E), grid(1, E, E), rows(num[:, 0:E], E), ALU.mult))
                link(dve.tensor_reduce(tab[:, T_WHO:T_WHO + E], grid(0, E, E), AX.X, ALU.add))
                link(dve.tensor_copy(tabu[:, T_WHO:T_WHO + E], tab[:, T_WHO:T_WHO + E]))
                dve.sem_inc(who_ready, 1)
                link(tt(grid(0, E, E), grid(1, E, E), rows(halves, E), ALU.mult))
                link(dve.tensor_reduce(by_rank, grid(0, E, E), AX.X, ALU.add))
                link(tt(grid(0, E, E), prev, rows(by_rank, E), ALU.mult))
                link(dve.tensor_reduce(base, grid(0, E, E), AX.X, ALU.add))
                link(stt(bases, base, float(P), const[:, C_HALF + 8:C_HALF + 24], ALU.mult, ALU.add))
                link(tt(grid(0, E, E), grid(1, E, E).rearrange("p r e -> p e r"), rows(bases, E), ALU.mult))
                link(dve.tensor_reduce(first_row, grid(0, E, E), AX.X, ALU.add))
                link(tt(v16(0).rearrange("p (t e) -> p t e", t=TILES), rows(first_row, TILES),
                        v16(1).rearrange("p (t e) -> p t e", t=TILES), ALU.add))
                t16 = lambda n: rt[:, n, :].rearrange("p (t e) -> p t e", t=TILES)
                link(tt(t16(14), t16(8), rows(const[:, C_NUM + 1:C_NUM + 1 + E], TILES), ALU.mult))
                link(dve.tensor_reduce(st[:, 0:3], t16(14), AX.X, ALU.max))
                link(tt(t16(14), t16(14), st[:, 0:3].rearrange("p (t u) -> p t u", u=1).broadcast_to([P, TILES, E]),
                        ALU.is_equal))
                link(tt(v16(13), v16(8), v16(14), ALU.subtract))
                both = pair[:, 0, 0:4 * TILES * E].rearrange("p (v a n) -> p v a n", v=2, a=2)
                link(tt(both, rt[:, 0:2, :].rearrange("p (v u) n -> p v u n", u=1).broadcast_to([P, 2, 2, TILES * E]),
                        rt[:, 13:15, :].rearrange("p (u a) n -> p u a n", u=1).broadcast_to([P, 2, 2, TILES * E]), ALU.mult))
                link(dve.tensor_reduce(st[:, 8:20], pair[:, 0, 0:4 * TILES * E].rearrange("p (c e) -> p c e", e=E),
                                       AX.X, ALU.add))
                over = pair[:, 0, 0:30].rearrange("p (c j) -> p c j", c=6)
                link(tt(over, cols(st[:, 14:20], 5),
                        const[:, C_HALF + 1:C_HALF + 6].rearrange("p (u j) -> p u j", u=1).broadcast_to([P, 6, 5]), ALU.is_ge))
                link(dve.tensor_reduce(st[:, 14:20], over, AX.X, ALU.add))
                link(stt(st[:, 8:14], st[:, 14:20], float(HALF), st[:, 8:14], ALU.mult, ALU.add))
                link(dve.tensor_copy(ridx[:, :, :].rearrange("p a t -> p (a t)"), st[:, 8:14]))
                link(tt(pair[:, 0, 0:6 * (BLOCKS - 1)].rearrange("p (c b) -> p c b", c=6), cols(st[:, 8:14], BLOCKS - 1),
                        const[:, C_ROWS:C_ROWS + BLOCKS - 1].rearrange("p (u b) -> p u b", u=1)
                        .broadcast_to([P, 6, BLOCKS - 1]), ALU.is_ge))
                link(dve.tensor_reduce(st[:, 14:20], pair[:, 0, 0:6 * (BLOCKS - 1)].rearrange("p (c b) -> p c b", c=6),
                                       AX.X, ALU.add))
                link(stt(st[:, 8:14], st[:, 14:20], -float(P), st[:, 8:14], ALU.mult, ALU.add))
                dve.wait_ge(state_out, 64 * (L + 1) + 16)
                link(tt(sel, cols(st[:, 8:14], P), iota.rearrange("p (u s) -> p u s", u=1).broadcast_to([P, 6, P]),
                        ALU.is_equal))
                blk = pair[:, 0, 0:6 * COLS].rearrange("p (c b) -> p c b", c=6)
                link(tt(blk, cols(st[:, 14:20], COLS),
                        num[:, 0:COLS].rearrange("p (u b) -> p u b", u=1).broadcast_to([P, 6, COLS]), ALU.is_equal))
                for part in range(2):
                    ins = tt(where[:, :, part, :], blk, cols(const[:, C_TOK + 6 * part:C_TOK + 6 * part + 6], COLS), ALU.mult)
                link(ins)
                dve.sem_inc(sel_ready, 1)
                link(ts(grid(0, 1, E), halves.rearrange("p (u e) -> p u e", u=1), 0.0, None, ALU.is_gt))
                link(dve.tensor_reduce(tab[:, T_ACTIVE:T_ACTIVE + 1], pair[:, 0, 0:E], AX.X, ALU.add))
                link(dve.tensor_copy(tab[:, T_BLOCKS:T_BLOCKS + PAIRS], by_rank[:, 0::2]))
                link(dve.tensor_reduce(tab[:, T_COUNT:T_COUNT + 1], by_rank[:, 0::2], AX.X, ALU.add))
                link(dve.tensor_copy(tab[:, T_FIRST:T_FIRST + 1], tab[:, T_LAST:T_LAST + 1]))
                link(ts(tab[:, T_START:T_START + PAIRS], base[:, 0::2], tab[:, T_FIRST:T_FIRST + 1], None, ALU.add))
                link(tt(tab[:, T_LAST:T_LAST + 1], tab[:, T_FIRST:T_FIRST + 1], tab[:, T_COUNT:T_COUNT + 1], ALU.add))
                link(dve.tensor_copy(tabu[:, 0:T_WHO], tab[:, 0:T_WHO]))
                dve.sem_inc(table_ready, 1)
                await_product(dve, L, "index")
                src = bank("index")[:, 0:2 * COLS]
                link(dve.tensor_copy(pair[:, 0, 0:COLS], src[:, COLS:2 * COLS]))
                read_out(tt(gidx[:, :], src[:, 0:COLS], pair[:, 0, 0:COLS], ALU.add), "index")
                both = pair[:, 1, 0:2 * TILES * E].rearrange("p (a n) -> p a n", a=2)
                link(tt(both, rt[:, 13:15, :], rt[:, 9:10, :].broadcast_to([P, 2, TILES * E]), ALU.mult))
                link(dve.tensor_reduce(gates[:, :, :].rearrange("p a t -> p (a t)"),
                                       pair[:, 1, 0:2 * TILES * E].rearrange("p (c e) -> p c e", e=E), AX.X, ALU.add))
                dve.sem_inc(gates_ready, 1)

                first = dve.value_load(tabu[0:1, T_FIRST:T_FIRST + 1], min_val=1, max_val=BLOCKS * DEPTH + 1)
                count = dve.value_load(tabu[0:1, T_COUNT:T_COUNT + 1], min_val=1, max_val=BLOCKS)
                with dve.Fori(0, count) as j:
                    i = j + first
                    dve.wait_ge(up_exp, i + 1)
                    ts(silu, silu, 1.0, None, ALU.add).then_inc(silu_step, 1)
                    dve.wait_ge(silu_step, i * 3 + 1)
                    dve.reciprocal(silu, silu).then_inc(silu_step, 1)
                    dve.wait_ge(silu_step, i * 3 + 2)
                    tt(silu, silu, psD[:, 0:DE], ALU.mult).then_inc(silu_step, 1)
                    dve.wait_ge(silu_step, i * 3 + 3)
                    dve.wait_ge(hidT_full, i)
                    tt(hid, silu, psD[:, DE:2 * DE], ALU.mult).then_inc(hid_ready, 1)

                def combine(t):
                    a, b = fetched[2 * t], fetched[2 * t + 1]
                    dve.wait_ge(first_gated, 3 * L + t + 1)
                    dve.wait_ge(pick_in[2 * t + 1], 16 * (L + 1))
                    link(stt(a, b, gates[:, 1, t:t + 1], a, ALU.mult, ALU.add))
                    link(tt(a, a, gate_b[:, min(t, 1), :], ALU.mult))
                    residual(t, a)
                    norm_stats(L, 9 + t, x[:, t, :])

                dve.wait_ge(gate2_in, 16 * (L + 1))
                dve.wait_ge(ln_in_s, (2 * L + 2) * 16)
                combine(0)
                combine(1)
                dve.wait_ge(gained, 6 * L + 5)
                pre_stats(0)
                combine(2)
                for t in (1, 2):
                    dve.wait_ge(xn_ready, 9 * L + 7 + t)
                    gain_bias(t)
                    pre_stats(t)

        @block.gpsimd
        def _(pool):
            restart, link = chain(pool, pool_done)

            def rstd(L, n):
                pool.wait_ge(stats_ready, 9 * L + n - 2)
                reciprocal_root(n % 3, rstd_ready)

            def pre_rstd_of(layer, t):
                pool.wait_ge(pre_mv, 3 * layer + t + 1)
                reciprocal_root(3 + t, pre_rstd)

            def reciprocal_root(b, done):
                link(pool.tensor_tensor(lnv[:, b, 0:1], mv[:, b, 1:2], half[:, 3:4], ALU.add))
                link(pool.tensor_tensor(lnv[:, b, 1:2], lnv[:, b, 0:1], half[:, 0:1], ALU.pow))
                pool.tensor_scalar(lnv[:, b, 2:3], mv[:, b, 0:1], lnv[:, b, 1:2], -1.0, ALU.mult, ALU.mult)\
                    .then_inc(done, 1)

            def layer_loads(l):
                pool.dma_start(cache[:, :], cache_in[l]).then_inc(layer_in_s, 16)
                pool.dma_start(convp[:, :, :], conv_in[l]).then_inc(layer_in_s, 16)
                pool.dma_start(lamv[:, :, :], lam_in[l].partition_broadcast(P)).then_inc(layer_in_s, 16)
                pool.dma_start(lamc[:, :], lamc_in[l].partition_broadcast(P)).then_inc(layer_in_s, 16)
                pool.dma_start(gain[:, :], gain_in[l].partition_broadcast(P)).then_inc(layer_in_s, 16)
                for g in range(4):
                    pool.dma_start(mrow[32 * g:32 * g + 32, :, :], bmod_in[l, g].partition_broadcast(32)).then_inc(bmod_in_s, 16)

            pool.wait_ge(cond_ready, 1)
            for t in range(TILES):
                pre_rstd_of(0, t)
            layer_loads(0)
            pool.wait_ge(const_in_s, 32)
            pool.dma_start(bias[:, :, :, :], bias_in[0]).then_inc(layer_bias_in, 16)
            pool.sem_inc(gcol_ready, 1)
            with pool.Fori(0, DEPTH) as L:
                restart()
                pool.wait_ge(gained, 6 * L + 1)
                stop_here(pool, "pool")
                pool.dma_start(ln_b[:, :, :], ln_in[L, 0:2].partition_broadcast(P)).then_inc(ln_in_s, 16)
                pool.wait_ge(layer_bias_in, (L + 1) * 16)
                flat = bias[:, :, :, :].rearrange("p h s c -> p (h s) c")
                pool.tensor_tensor(flat, flat, const[:, C_MASK:C_MASK + GRID_W].rearrange("p (u c) -> p u c", u=1)
                                   .broadcast_to([P, 6 * NA_HEADS, GRID_W]), ALU.add).then_inc(bias_ready, 1)
                with pool.If(L < 1):
                    pool.wait_ge(ln_in_s, 16)
                    pool.wait_ge(roped, 8)
                    for q in range(4):
                        pool.dma_start(moe_d.rearrange("(b p) d -> p b d", p=P)[:, BLOCKS // 4 * q:BLOCKS // 4 * (q + 1), :],
                                       ln_b[:, 0:1, :].broadcast_to([P, BLOCKS // 4, D])).then_inc(filled, 16)
                    pool.wait_ge(filled, 64)
                for h in range(DA_HEADS):
                    pool.wait_ge(ms_ready, 4 * L + h + 1)
                    stop_here(pool, "pool")
                    link(pool.tensor_scalar(msr[:, 1, :], msr[:, 0, :], 1.0 / P, EPS, ALU.mult, ALU.add))
                    pool.tensor_tensor(msr[:, 2, :], msr[:, 1, :], half[:, 0:3], ALU.pow).then_inc(rms_ready, 1)
                pool.wait_ge(mod_stored, (L + 1) * 8 * 16)
                stop_here(pool, "pool")
                pool.dma_start(gate_b[:, :, :], mod_d[:, 0, :].partition_broadcast(P)).then_inc(gate1_in, 16)
                pool.wait_ge(av_done, N_STEPS * (L + 1))
                stop_here(pool, "pool")
                pool.dma_start(mod2_b[:, :, :, :], mod_d[:, 1:3, :].partition_broadcast(P)).then_inc(mod2_in, 16)
                for n in range(3, 9):
                    rstd(L, n)
                pool.wait_ge(h2_ready, 3 * L + 3)
                stop_here(pool, "pool")
                pool.dma_start(ln_b[:, :, :], ln_in[L, 2:4].partition_broadcast(P)).then_inc(ln_in_s, 16)
                pool.dma_start(gate_b[:, :, :], mod_d[:, 3, :].partition_broadcast(P)).then_inc(gate2_in, 16)
                pool.wait_ge(h2_stored, 16 * 3 * (L + 1))
                await_read(pool, L, "index")
                pool.wait_ge(table_ready, L + 1)
                stop_here(pool, "pool")
                first = pool.value_load(tabu[0:1, T_FIRST:T_FIRST + 1], min_val=1, max_val=BLOCKS * DEPTH + 1)
                count = pool.value_load(tabu[0:1, T_COUNT:T_COUNT + 1], min_val=1, max_val=BLOCKS)
                with pool.Fori(0, count + 1) as j:
                    i = j + first + L
                    pool.wait_ge(xT_full, i)
                    pool.tensor_copy(gcol[:, :], gidx[:, bass.ds(j, 1)]).then_inc(gcol_ready, 1)
                    pool.wait_ge(gcol_ready, i + 1)
                    stop_here(pool, "pool")
                    pool.indirect_dma_start(xg, None, h2_d[:, :],
                                            bass.IndirectOffsetOnAxis(gcol[:, 0:1], 0)).then_inc(xg_in, 16)
                with pool.If(L < DEPTH - 1):
                    pool.wait_ge(state_out, 64 * (L + 1) + 16)
                    stop_here(pool, "pool")
                    layer_loads(before_last(L) + 1)
                pool.wait_ge(xT_ready, first + count + L + 1)
                pool.wait_ge(yo_stored, (first + count) * 16 + 16)
                stop_here(pool, "pool")
                for t in range(TILES):
                    for a in range(2):
                        pool.indirect_dma_start(fetched[2 * t + a], None, moe_d[:, :],
                                                bass.IndirectOffsetOnAxis(ridx[:, a, t:t + 1], 0))\
                            .then_inc(pick_in[2 * t + a], 16)
                pool.wait_ge(ln_in_s, (2 * L + 2) * 16)
                rstd(L, 9)
                pool.wait_ge(xn_ready, 9 * L + 7)
                link(pool.tensor_tensor(x[:, 0, :], x[:, 0, :], ln_b[:, 0, :], ALU.mult))
                pool.tensor_tensor(x[:, 0, :], x[:, 0, :], ln_b[:, 1, :], ALU.add).then_inc(gained, 1)
                rstd(L, 10)
                pre_rstd_of(L + 1, 0)
                rstd(L, 11)
                for t in (1, 2):
                    pre_rstd_of(L + 1, t)
                with pool.If(L < DEPTH - 1):
                    pool.wait_ge(pair_done, (L + 1) * STAGES + 1)
                    stop_here(pool, "pool")
                    pool.dma_start(bias[:, :, :, :], bias_in[before_last(L) + 1]).then_inc(layer_bias_in, 16)


def _constants():
    c = np.zeros((P, N_CONST), np.float32)
    p = np.arange(P)
    c[:, C_ID:C_ID + P] = np.eye(P)
    c[p, C_SWAP + (p ^ 16)] = 1.0
    j = p % 64
    inv = (np.float32(10000.0) ** (-np.arange(16, dtype=np.float32) / 16)).astype(np.float32)
    t = np.arange(LAT)
    pos = np.where((j // 32 == 0)[:, None], t[None, :] // GRID_W, t[None, :] % GRID_W).astype(np.float32)
    ang = pos * inv[j % 16][:, None]
    c[:, C_COS:C_COS + LAT] = np.cos(ang)
    c[:, C_SIN:C_SIN + LAT] = np.where((j % 32 < 16)[:, None], -np.sin(ang), np.sin(ang))
    qc, kc = p % GRID_W, np.arange(GRID_W)
    w0 = np.clip(qc - 8, 0, GRID_W - 16)[:, None]
    c[:, C_MASK:C_MASK + GRID_W] = np.where((kc >= w0) & (kc < w0 + 16), 0.0, MASKED)
    c[:, C_UTRI:C_UTRI + P] = p[:, None] < p[None, :]
    c[:, C_IOTA:C_IOTA + P] = p[None, :]
    jj, ii = np.meshgrid(np.arange(4), np.arange(4), indexing="ij")
    c[:, C_LT4:C_LT4 + 16] = (ii < jj).reshape(1, 16)
    c[:, C_NUM:C_NUM + 32] = np.arange(32)
    r = np.arange(E)
    c[:, C_PREV:C_PREV + E * E] = ((r[None, :] % 2 == 0) & (r[None, :] < r[:, None] // 2 * 2)).reshape(1, E * E)
    c[:, C_ROWS:C_ROWS + BLOCKS - 1] = P * np.arange(1, BLOCKS)
    c[:, C_HALF:C_HALF + 6] = HALF * np.arange(6)
    c[:, C_HALF + 8:C_HALF + 24] = HALF * (r % 2)
    for t in range(TILES):
        c[:, C_TOK + t:C_TOK + 6:TILES] = p[:, None]
        c[:, C_TOK + 6 + t:C_TOK + 12:TILES] = P * t
    return c


def _experts(w1, w3, w2):
    up = np.concatenate([w1.reshape(DEPTH, E, P, KC, DE), w3.reshape(DEPTH, E, P, KC, DE)], axis=4)
    down = w2.reshape(DEPTH, E, 2, P, D).transpose(0, 1, 3, 2, 4)
    return np.concatenate([up.reshape(DEPTH, E, P, -1), down.reshape(DEPTH, E, P, -1)], axis=3).reshape(DEPTH * E, P, EXPERT)


def _weights(w_mod, w_in, w_out):
    walls = np.empty((DEPTH * ITEMS, P, ITEM), np.float32)
    for l in range(DEPTH):
        at = RING + l * ITEMS
        m = w_mod[l].reshape(P, KC, N_MOD, D)
        for v in range(2):
            cols = m[:, :, v].reshape(P, KC, P, 4, 2).transpose(3, 0, 1, 4, 2).reshape(4, P, ITEM)
            walls[at - RING + 4 * v:at - RING + 4 * v + 4] = cols
        for v in range(2, N_MOD):
            for g in range(4):
                walls[at + MODS0 + 4 * (v - 2) + g] = m[:, :, v, 256 * g:256 * g + 256].reshape(P, ITEM)
        wi = w_in[l].reshape(P, KC, -1)
        for n, (piece, half) in enumerate(PIECES):
            col = PIECE_COL[piece] + 256 * half
            walls[at + W_IN0 + n] = wi[:, :, col:col + 256].reshape(P, ITEM)
        wo = w_out[l].reshape(KC, P, D)
        for n in range(4):
            walls[at + W_OUT0 + n] = wo[:, :, 256 * n:256 * n + 256].transpose(1, 0, 2).reshape(P, ITEM)
    return walls


def _local_bias(rel):
    p = np.arange(P)[:, None, None]
    row = np.arange(6)[None, :, None] + np.where(p < 64, 5, 4)
    col = np.clip(np.arange(GRID_W)[None, None, :] - p % GRID_W + 15, 0, 30)
    return np.ascontiguousarray(rel[:, :, row, col].transpose(0, 2, 1, 3, 4))


def kernel(x_prompt, x_sample, cache_na_k, cache_na_v, cache_da_k, cache_da_v, c, c_ctx,
           w_mod, b_mod, w_in, na_rel_bias, sc_conv_w, sc_conv_b, da_lambda, da_norm_g, w_out,
           ln1_g, ln1_b, w_router, b_router, moe_w1, moe_w3, moe_w2, ln2_g, ln2_b):
    import math

    import concourse.bacc as bacc
    from concourse.bass_utils import run_bass_kernel_spmd

    a = np.asarray
    cache = np.concatenate([a(cache_da_k)[0].reshape(DEPTH, P, 512), a(cache_na_k)[0].reshape(DEPTH, P, 256),
                            a(cache_da_v)[0].reshape(DEPTH, P, 512), a(cache_na_v)[0].reshape(DEPTH, P, 256)], axis=2)
    conv = np.concatenate([a(sc_conv_w), a(sc_conv_b)[:, None]], axis=1).reshape(DEPTH, 4, 2, P).transpose(0, 3, 2, 1)
    lam_init = [0.8 - 0.6 * math.exp(-0.3 * l) for l in range(DEPTH)]
    ins = {
        "weights": _weights(a(w_mod), a(w_in), a(w_out)),
        "experts": _experts(a(moe_w1), a(moe_w3), a(moe_w2)),
        "x": np.concatenate([a(x_prompt)[0], a(x_sample)[0]]).reshape(TILES, P, D),
        "cond": np.stack([a(c_ctx), a(c)[0]]).reshape(2, P, KC).transpose(1, 0, 2),
        "cache": cache,
        "local_bias": _local_bias(a(na_rel_bias)),
        "conv": conv,
        "da_lambda": a(da_lambda),
        "lambda_init": np.array([[v, 1.0 - v] for v in lam_init], np.float32),
        "da_gain": a(da_norm_g),
        "ln": np.stack([a(ln1_g), a(ln1_b), a(ln2_g), a(ln2_b)], axis=1),
        "w_router": a(w_router).reshape(P, KC, E),
        "b_router": a(b_router),
        "b_mod": a(b_mod).reshape(DEPTH, N_MOD, 4, 256)[:, 2:].transpose(0, 2, 1, 3),
        "b_mod_first": a(b_mod).reshape(DEPTH, N_MOD, P, KC)[:, :2].transpose(2, 0, 1, 3),
        "constants": _constants(),
    }
    ins = {k: np.ascontiguousarray(v) for k, v in ins.items()}
    outs = {"y_prompt": (P, D), "y_sample": (LAT, D), "new_na_k": (DEPTH, P, 256), "new_na_v": (DEPTH, P, 256),
            "new_da_k": (DEPTH, P, 512), "new_da_v": (DEPTH, P, 512)}
    nc = bacc.Bacc("TRN2", target_bir_lowering=False, num_devices=1)
    args = [nc.dram_tensor(f"in_{k}", v.shape, F32, kind="ExternalInput").ap() for k, v in ins.items()]
    args += [nc.dram_tensor(f"out_{k}", s, F32, kind="ExternalOutput").ap() for k, s in outs.items()]
    hybrid_step_kernel(nc, *args)
    r = run_bass_kernel_spmd(nc, [{f"in_{k}": v for k, v in ins.items()}], core_ids=[0]).results[0]
    return (r["out_y_prompt"].reshape(1, P, D), r["out_y_sample"].reshape(1, LAT, D),
            r["out_new_na_k"].reshape(1, DEPTH, P, 4, 64), r["out_new_na_v"].reshape(1, DEPTH, P, 4, 64),
            r["out_new_da_k"].reshape(1, DEPTH, P, 8, 64), r["out_new_da_v"].reshape(1, DEPTH, P, 4, 128))
```
